# Optimizing a Trainium2 kernel written in Bass

```python
import jax, jax.numpy as jnp
from jax import lax
import numpy as np

D_MODEL = 1024
BATCH = 1
SEQ = 1024
DEPTH = 2
DEC_BATCH = 8
DEC_SEQ = 1
PAST_LEN = 8192
PAGE_SIZE = 128

CONV_W = 4
D_RG = D_MODEL
RG_HEADS = 8
RG_BW = D_RG // RG_HEADS
RG_C = 8.0
D_ML = D_MODEL
ML_HEADS = 4
ML_DH = D_ML // ML_HEADS
D_RET = D_MODEL
RET_HEADS = 4
RET_DH = D_RET // RET_HEADS
N_BRANCH = 3
CHUNK = 128
ROPE_BASE = 10000.0
EPS = 1e-6
IN_SPLITS = (D_RG, D_RG, D_ML, D_ML, D_RET, D_RET, D_RET, D_RET, N_BRANCH * D_MODEL)
D_IN = 2 * D_RG + 2 * D_ML + 4 * D_RET + N_BRANCH * D_MODEL

kernel_name = 'hybrid_rglru_mlstm_retention_step'

def rmsnorm(x, g):
    xf = x.astype(jnp.float32)
    y = xf * lax.rsqrt(jnp.mean(xf * xf, axis=-1, keepdims=True) + EPS)
    return y * g.astype(jnp.float32)

def headnorm(h, g, n_heads):
    B, L, D = h.shape
    hf = h.astype(jnp.float32).reshape(B, L, n_heads, D // n_heads)
    mu = jnp.mean(hf, axis=-1, keepdims=True)
    var = jnp.mean(jnp.square(hf - mu), axis=-1, keepdims=True)
    y = ((hf - mu) * lax.rsqrt(var + EPS)).reshape(B, L, D)
    return y * g.astype(jnp.float32)

def rope(x, pos):
    half = x.shape[-1] // 2
    inv = ROPE_BASE ** (-jnp.linspace(0.0, 1.0, half, dtype=jnp.float32))
    ang = pos.astype(jnp.float32)[:, None] * inv[None, :]
    cos = jnp.cos(ang)[None, :, None, :]
    sin = jnp.sin(ang)[None, :, None, :]
    x1, x2 = x[..., :half], x[..., half:]
    return jnp.concatenate([x1 * cos - x2 * sin, x1 * sin + x2 * cos], axis=-1)

def causal_conv(x, buf, w, b):
    L = x.shape[1]
    xx = jnp.concatenate([buf.astype(x.dtype), x], axis=1)
    y = b + sum(xx[:, j:j + L] * w[j] for j in range(CONV_W))
    return y, xx[:, L:]

def _lin_comb(left, right):
    a_l, b_l = left
    a_r, b_r = right
    return a_l * a_r, a_r * b_l + b_r

def rg_lru(xc, h0, w_a, b_a, w_x, b_x, lam):
    B, L, _ = xc.shape
    xb = xc.reshape(B, L, RG_HEADS, RG_BW)
    r = jax.nn.sigmoid(jnp.einsum('blhi,hij->blhj', xb, w_a).reshape(B, L, D_RG) + b_a)
    i = jax.nn.sigmoid(jnp.einsum('blhi,hij->blhj', xb, w_x).reshape(B, L, D_RG) + b_x)
    log_a = -RG_C * r * jax.nn.softplus(-lam)
    a = jnp.exp(log_a)
    bterm = jnp.sqrt(-jnp.expm1(2.0 * log_a)) * (i * xc)
    bterm = bterm.at[:, 0].add(a[:, 0] * h0)
    _, h = lax.associative_scan(_lin_comb, (a, bterm), axis=1)
    return h, h[:, -1]

def mlstm_chunk(carry, inp):
    C0, n0, m0 = carry
    q, k, v, ig, lf = inp
    L = q.shape[2]
    F = jnp.cumsum(lf, axis=-1)
    u = ig - F
    m = F + jnp.maximum(m0[..., None], lax.cummax(u, axis=2))
    causal = jnp.tril(jnp.ones((L, L), dtype=bool))
    logD = (F - m)[..., :, None] + u[..., None, :]
    D = jnp.exp(jnp.where(causal, logD, -jnp.inf))
    inter = jnp.exp(F + m0[..., None] - m)
    s = jnp.einsum('bhtd,bhsd->bhts', q, k) * D
    num = inter[..., None] * jnp.einsum('bhtd,bhde->bhte', q, C0) + jnp.einsum('bhts,bhse->bhte', s, v)
    den = inter * jnp.einsum('bhtd,bhd->bht', q, n0) + jnp.sum(s, axis=-1)
    h = num / jnp.maximum(jnp.abs(den), jnp.exp(-m))[..., None]
    mL = m[..., -1]
    wL = jnp.exp(F[..., -1:] - mL[..., None] + u)
    decayL = jnp.exp(F[..., -1] + m0 - mL)
    C = decayL[..., None, None] * C0 + jnp.einsum('bhs,bhsd,bhse->bhde', wL, k, v)
    n = decayL[..., None] * n0 + jnp.einsum('bhs,bhsd->bhd', wL, k)
    return (C, n, mL), h

def retention_chunk(S0, inp):
    q, k, v = inp
    L = q.shape[2]
    lg = jnp.log1p(-jnp.exp2(-5.0 - jnp.arange(RET_HEADS, dtype=jnp.float32)))
    idx = jnp.arange(L, dtype=jnp.float32)
    causal = jnp.tril(jnp.ones((L, L), dtype=bool))
    rel = idx[:, None] - idx[None, :]
    D = jnp.exp(jnp.where(causal[None], rel[None] * lg[:, None, None], -jnp.inf))
    cross = jnp.exp((idx + 1.0)[None, :] * lg[:, None])
    wk = jnp.exp((L - 1.0 - idx)[None, :] * lg[:, None])
    decayL = jnp.exp(L * lg)
    s = jnp.einsum('bhtd,bhsd->bhts', q, k) * D[None]
    h = jnp.einsum('bhts,bhse->bhte', s, v) + jnp.einsum('bhtd,bhde->bhte', q, S0) * cross[None, :, :, None]
    S = decayL[None, :, None, None] * S0 + jnp.einsum('bhsd,bhse->bhde', k * wk[None, :, :, None], v)
    return S, h

def chunked_scan(step, carry, xs):
    L = xs[0].shape[2]
    c = CHUNK if L % CHUNK == 0 else L
    n = L // c
    xs = tuple(jnp.moveaxis(a.reshape(a.shape[:2] + (n, c) + a.shape[3:]), 2, 0) for a in xs)
    carry, ys = lax.scan(step, carry, xs)
    ys = jnp.moveaxis(ys, 0, 2)
    return carry, ys.reshape(ys.shape[:2] + (L,) + ys.shape[4:])

def _to_bhld(a):
    return jnp.transpose(a, (0, 2, 1, 3))

def zero_state(B):
    f = jnp.float32
    return (jnp.zeros((B, D_RG), f), jnp.zeros((B, CONV_W - 1, D_RG), f),
            jnp.zeros((B, ML_HEADS, ML_DH, ML_DH), f), jnp.zeros((B, ML_HEADS, ML_DH), f),
            jnp.zeros((B, ML_HEADS), f), jnp.zeros((B, CONV_W - 1, D_ML), f),
            jnp.zeros((B, RET_HEADS, RET_DH, RET_DH), f))

def mixer_layer(x, c, state, pos0, params):
    rg_h, rg_conv, ml_C, ml_n, ml_m, ml_conv, ret_S = tuple(s.astype(jnp.float32) for s in state)
    (w_ada, b_ada, norm_pre, norm_post, w_in, rg_conv_w, rg_conv_b, rg_w_a, rg_b_a, rg_w_x, rg_b_x,
     rg_lambda, ml_conv_w, ml_conv_b, ml_w_q, ml_w_k, ml_w_v, ml_w_if, ml_b_if, ml_skip, ml_gn,
     ret_gn, w_out) = params
    B, L, _ = x.shape
    shift, scale, gate = jnp.split(c.astype(jnp.float32) @ w_ada + b_ada, 3, axis=-1)
    u = rmsnorm(x, norm_pre) * (1.0 + scale[:, None]) + shift[:, None]
    proj = u @ w_in
    offs = []
    o = 0
    for s in IN_SPLITS[:-1]:
        o += s
        offs.append(o)
    x_rg, z_rg, x_ml, z_ml, q_r, k_r, v_r, g_r, g_br = jnp.split(proj, offs, axis=-1)

    xc_rg, rg_conv_new = causal_conv(x_rg, rg_conv, rg_conv_w, rg_conv_b)
    h_rg, rg_h_new = rg_lru(xc_rg, rg_h, rg_w_a, rg_b_a, rg_w_x, rg_b_x, rg_lambda)
    y_a = h_rg * jax.nn.silu(z_rg)

    xc_ml, ml_conv_new = causal_conv(x_ml, ml_conv, ml_conv_w, ml_conv_b)
    xc_ml = jax.nn.silu(xc_ml)
    xh = xc_ml.reshape(B, L, ML_HEADS, ML_DH)
    q = jnp.einsum('blhi,hij->blhj', xh, ml_w_q)
    k = jnp.einsum('blhi,hij->blhj', xh, ml_w_k) * (ML_DH ** -0.5)
    v = jnp.einsum('blhi,hij->blhj', x_ml.reshape(B, L, ML_HEADS, ML_DH), ml_w_v)
    gpre = jnp.concatenate([q.reshape(B, L, D_ML), k.reshape(B, L, D_ML), v.reshape(B, L, D_ML)], axis=-1) @ ml_w_if + ml_b_if
    ig = jnp.transpose(gpre[..., :ML_HEADS], (0, 2, 1))
    lf = jnp.transpose(jax.nn.log_sigmoid(gpre[..., ML_HEADS:]), (0, 2, 1))
    (ml_C_new, ml_n_new, ml_m_new), h_ml = chunked_scan(
        mlstm_chunk, (ml_C, ml_n, ml_m), (_to_bhld(q), _to_bhld(k), _to_bhld(v), ig, lf))
    h_ml = _to_bhld(h_ml).reshape(B, L, D_ML)
    y_b = (headnorm(h_ml, ml_gn, ML_HEADS) + ml_skip * xc_ml) * jax.nn.silu(z_ml)

    pos = pos0 + jnp.arange(L)
    qr = rope(q_r.reshape(B, L, RET_HEADS, RET_DH), pos)
    kr = rope(k_r.reshape(B, L, RET_HEADS, RET_DH), pos) * (RET_DH ** -0.5)
    vr = v_r.reshape(B, L, RET_HEADS, RET_DH)
    ret_S_new, h_ret = chunked_scan(retention_chunk, ret_S, (_to_bhld(qr), _to_bhld(kr), _to_bhld(vr)))
    h_ret = _to_bhld(h_ret).reshape(B, L, D_RET)
    y_c = headnorm(h_ret, ret_gn, RET_HEADS) * jax.nn.silu(g_r)

    g_a, g_b, g_c = jnp.split(jax.nn.sigmoid(g_br), 3, axis=-1)
    mix = g_a * y_a + g_b * y_b + g_c * y_c
    out = mix @ w_out
    x_new = x.astype(jnp.float32) + gate[:, None] * rmsnorm(out, norm_post)
    return x_new.astype(x.dtype), (rg_h_new, rg_conv_new, ml_C_new, ml_n_new, ml_m_new, ml_conv_new, ret_S_new)

def setup_inputs(seed: int = 0) -> dict:
    key = jax.random.key(seed)
    k = jax.random.split(key, 35)
    f = jnp.float32

    def nrm(kk, shape, s):
        return s * jax.random.normal(kk, shape, f)

    u = jax.random.uniform(k[22], (DEPTH, D_RG), f, minval=0.9, maxval=0.999)
    a = u ** (1.0 / RG_C)
    rg_lambda = jnp.log(a) - jnp.log1p(-a)
    b_ml_if = jnp.concatenate([nrm(k[29], (DEPTH, ML_HEADS), 0.02),
                               jnp.linspace(3.0, 6.0, ML_HEADS, dtype=f)[None, :] + nrm(k[30], (DEPTH, ML_HEADS), 0.02)], axis=-1)
    return {
        'x_prompt': nrm(k[0], (BATCH, SEQ, D_MODEL), 1.0),
        'x_sample': nrm(k[1], (DEC_BATCH, DEC_SEQ, D_MODEL), 1.0),
        'c_prompt': nrm(k[2], (BATCH, D_MODEL), 1.0),
        'c_sample': nrm(k[3], (DEC_BATCH, D_MODEL), 1.0),
        'state_rg_h': nrm(k[4], (DEPTH, DEC_BATCH, D_RG), 0.5),
        'state_rg_conv': nrm(k[5], (DEPTH, DEC_BATCH, CONV_W - 1, D_RG), 1.0),
        'state_ml_C': nrm(k[6], (DEPTH, DEC_BATCH, ML_HEADS, ML_DH, ML_DH), 0.5),
        'state_ml_n': nrm(k[7], (DEPTH, DEC_BATCH, ML_HEADS, ML_DH), 0.5),
        'state_ml_m': nrm(k[8], (DEPTH, DEC_BATCH, ML_HEADS), 1.0),
        'state_ml_conv': nrm(k[9], (DEPTH, DEC_BATCH, CONV_W - 1, D_ML), 1.0),
        'state_ret_S': nrm(k[10], (DEPTH, DEC_BATCH, RET_HEADS, RET_DH, RET_DH), 0.5),
        'w_ada': nrm(k[11], (DEPTH, D_MODEL, 3 * D_MODEL), 0.2 * D_MODEL ** -0.5),
        'b_ada': nrm(k[12], (DEPTH, 3 * D_MODEL), 0.02),
        'norm_pre': 1.0 + nrm(k[13], (DEPTH, D_MODEL), 0.02),
        'norm_post': 1.0 + nrm(k[14], (DEPTH, D_MODEL), 0.02),
        'w_in': nrm(k[15], (DEPTH, D_MODEL, D_IN), D_MODEL ** -0.5),
        'rg_conv_w': nrm(k[16], (DEPTH, CONV_W, D_RG), 0.5),
        'rg_conv_b': nrm(k[17], (DEPTH, D_RG), 0.02),
        'rg_w_a': nrm(k[18], (DEPTH, RG_HEADS, RG_BW, RG_BW), RG_BW ** -0.5),
        'rg_b_a': nrm(k[19], (DEPTH, D_RG), 0.02),
        'rg_w_x': nrm(k[20], (DEPTH, RG_HEADS, RG_BW, RG_BW), RG_BW ** -0.5),
        'rg_b_x': nrm(k[21], (DEPTH, D_RG), 0.02),
        'rg_lambda': rg_lambda,
        'ml_conv_w': nrm(k[23], (DEPTH, CONV_W, D_ML), 0.5),
        'ml_conv_b': nrm(k[24], (DEPTH, D_ML), 0.02),
        'ml_w_q': nrm(k[25], (DEPTH, ML_HEADS, ML_DH, ML_DH), ML_DH ** -0.5),
        'ml_w_k': nrm(k[26], (DEPTH, ML_HEADS, ML_DH, ML_DH), ML_DH ** -0.5),
        'ml_w_v': nrm(k[27], (DEPTH, ML_HEADS, ML_DH, ML_DH), ML_DH ** -0.5),
        'ml_w_if': nrm(k[28], (DEPTH, 3 * D_ML, 2 * ML_HEADS), (3 * D_ML) ** -0.5),
        'ml_b_if': b_ml_if,
        'ml_skip': 1.0 + nrm(k[31], (DEPTH, D_ML), 0.02),
        'ml_gn': 1.0 + nrm(k[32], (DEPTH, D_ML), 0.02),
        'ret_gn': 1.0 + nrm(k[33], (DEPTH, D_RET), 0.02),
        'w_out': nrm(k[34], (DEPTH, D_MODEL, D_MODEL), D_MODEL ** -0.5),
    }

def reference(x_prompt, x_sample, c_prompt, c_sample, state_rg_h, state_rg_conv, state_ml_C, state_ml_n,
              state_ml_m, state_ml_conv, state_ret_S, w_ada, b_ada, norm_pre, norm_post, w_in,
              rg_conv_w, rg_conv_b, rg_w_a, rg_b_a, rg_w_x, rg_b_x, rg_lambda, ml_conv_w, ml_conv_b,
              ml_w_q, ml_w_k, ml_w_v, ml_w_if, ml_b_if, ml_skip, ml_gn, ret_gn, w_out):
    params_all = (w_ada, b_ada, norm_pre, norm_post, w_in, rg_conv_w, rg_conv_b, rg_w_a, rg_b_a, rg_w_x,
                  rg_b_x, rg_lambda, ml_conv_w, ml_conv_b, ml_w_q, ml_w_k, ml_w_v, ml_w_if, ml_b_if,
                  ml_skip, ml_gn, ret_gn, w_out)
    xp, xs = x_prompt, x_sample
    st_p_list, st_s_list = [], []
    for l in range(DEPTH):
        p_l = tuple(w[l] for w in params_all)
        xp, st_p = mixer_layer(xp, c_prompt, zero_state(xp.shape[0]), 0, p_l)
        st_s0 = (state_rg_h[l], state_rg_conv[l], state_ml_C[l], state_ml_n[l], state_ml_m[l],
                 state_ml_conv[l], state_ret_S[l])
        xs, st_s = mixer_layer(xs, c_sample, st_s0, PAST_LEN, p_l)
        st_p_list.append(st_p)
        st_s_list.append(st_s)
    p_rg_h, p_rg_conv, p_ml_C, p_ml_n, p_ml_m, p_ml_conv, p_ret_S = [jnp.stack(a) for a in zip(*st_p_list)]
    s_rg_h, s_rg_conv, s_ml_C, s_ml_n, s_ml_m, s_ml_conv, s_ret_S = [jnp.stack(a) for a in zip(*st_s_list)]
    return (xp, xs, p_rg_h, p_rg_conv, p_ml_C, p_ml_n, p_ml_m, p_ml_conv, p_ret_S,
            s_rg_h, s_rg_conv, s_ml_C, s_ml_n, s_ml_m, s_ml_conv, s_ret_S)


_drawn_inputs = setup_inputs


def setup_inputs(seed=0):
    import zlib

    import numpy as np

    out = dict(_drawn_inputs(seed))
    spreads = {}
    factors = {'norm_post': 8.0,
     'rg_b_a': 8.0,
     'rg_b_x': 6.943,
     'ml_skip': 8.0,
     'ml_gn': 8.0,
     'ret_gn': 8.0}
    for name, (base, spread) in spreads.items():
        noise = np.random.default_rng([zlib.crc32(name.encode()), seed]).standard_normal(out[name].shape)
        drawn = base * np.exp(spread * noise) if base else spread * noise
        out[name] = __import__('jax').numpy.asarray(drawn.astype(out[name].dtype))
    for name, factor in factors.items():
        out[name] = (out[name] * factor).astype(out[name].dtype)
    return out
```

```python
from contextlib import ExitStack

import numpy as np

import concourse.bass as bass
from concourse import mybir

F32 = mybir.dt.float32
F32R = mybir.dt.float32r
ACT = mybir.ActivationFunctionType
ALU = mybir.AluOpType

P = 128
DEPTH, D, SEQ, NB = 2, 1024, 1024, 8
T = SEQ + NB
KT = D // P
NG, GW = 3, T // 3
HEADS, DH, CONV = 4, 256, 4
CH, NC = 128, SEQ // 128
EPS = 1e-6
RG_C = 8.0
PAST = 8192
NADA, NIN, NOUT = 3 * KT, 11 * KT, KT
NT = NADA + NIN + NOUT
XML0, RG0, RET0, ML0, OUT0 = 24, 32, 56, 96, 112
HCOL = 36
LOG1P_TERMS = [1.0 / n for n in (15, 13, 11, 9, 7, 5, 3)]

PAR = {}
_o = 0
for _n, _w in (("b_ada", 24), ("norm_pre", 8), ("norm_post", 8), ("rg_conv_w", 32), ("rg_conv_b", 8),
               ("rg_b_a", 8), ("rg_b_x", 8), ("rg_lambda", 8), ("ml_conv_w", 32), ("ml_conv_b", 8),
               ("ml_skip", 8), ("ml_gn", 8), ("ret_gn", 8)):
    PAR[_n] = (_o, _w)
    _o += _w
NPAR = _o

CR, CD = 8, 64
DMA_CREDIT = ("xsp0", "xsp1", "cs_st0", "cs_st1", "st_out")
N_PROJ = 3 * (NIN + NOUT)


def weight_order():
    xrg, zrg, xml, zml, q, k, v, g, ga, gb, gc = (range(8 * i, 8 * i + 8) for i in range(11))
    order = list(xml)
    for j in range(8):
        order += [xrg[j], zrg[j], ga[j]]
    for h in range(4):
        a, b = 2 * h, 2 * h + 1
        order += [q[a], q[b], k[a], k[b], v[a], v[b], g[a], gc[a], g[b], gc[b]]
    for h in range(4):
        a, b = 2 * h, 2 * h + 1
        order += [zml[a], gb[a], zml[b], gb[b]]
    return order


def build(nc, io):
    with ExitStack() as ctx:
        def sb(name, shape, dt=F32):
            return ctx.enter_context(nc.sbuf_tensor(name, shape, dt))

        def sem(name):
            return ctx.enter_context(nc.semaphore(name))

        ident = sb("ident", [P, P])
        ones = sb("ones", [P, P])
        mask = sb("mask", [P, P])
        sel = sb("sel", [4, 4 * P])
        dret = sb("dret", [P, 4, P])
        rcol = sb("rcol", [P, 16])
        uH = sb("uH", [P, KT, T], F32R)
        uL = sb("uL", [P, KT, T], F32R)
        xm = sb("xm", [P, KT, T])
        wraw = [sb(f"wraw{s}", [P, KT * P]) for s in range(2)]
        wH = [sb(f"wH{s}", [P, KT, P], F32R) for s in range(2)]
        wL = [sb(f"wL{s}", [P, KT, P], F32R) for s in range(2)]
        par = sb("par", [P, NPAR])
        wif = sb("wif", [P, 24, 8])
        cT = sb("cT", [P, KT, 10])
        cH = sb("cH", [P, KT, 10], F32R)
        cL = sb("cL", [P, KT, 10], F32R)
        ada = sb("ada", [P, NADA, 10])
        s1 = sb("s1", [P, KT, 10])
        gpo = sb("gpo", [P, KT, 10])
        nsp = sb("nsp", [P, 2, KT])
        rcs = sb("rcs", [P, KT, 3, NB])
        mcs = sb("mcs", [P, KT, 3, NB])
        rcsn = sb("rcsn", [P, KT, 3, NB])
        mcsn = sb("mcsn", [P, KT, 3, NB])
        pcn = sb("pcn", [P, 2, KT, 3])
        rh0 = sb("rh0", [P, KT, NB])
        rhn = sb("rhn", [P, KT, 9])
        mn0 = sb("mn0", [P, HEADS, 2, NB])
        mnn = sb("mnn", [P, 2, NB])
        mm0 = sb("mm0", [4, NB])
        pn = sb("pn", [P, 2])
        mc = sb("mc", [4, 10])
        mcols = sb("mcols", [4, 3, NC])
        exr = sb("exr", [4, 4, NB])
        smx = sb("smx", [4, 4, NB])
        fold = sb("fold", [P, 2, KT, HCOL])
        ucol = sb("ucol", [P, NC, 4, 4])
        bc = sb("bc", [P, 4, 4, NB])
        nmrow = sb("nmrow", [4, SEQ])
        selh = sb("selh", [4, P])
        fj = [sb(f"fj{s}", [P, 2, HCOL]) for s in range(2)]
        zf = sb("zf", [P, HCOL])
        bifp = sb("bifp", [HCOL, 1])
        qs = sb("qs", [P, 3, 2, NB])
        sm = sb("sm", [P, 64])
        sm2 = sb("sm2", [P, 8, 16])
        W_SIZE = 15800
        work = sb("work", [P, W_SIZE])

        def wv(off, n):
            assert off + n <= W_SIZE
            return work[:, off:off + n]

        tmp_n = [wv(T * i, T) for i in range(2)]
        sq = [wv(T * (2 + i), T) for i in range(2)]
        rs = wv(T * 4, T)
        xt = [wv(T * (5 + i), T) for i in range(2)]
        wt = [wv(12000 + 1536 * i, 1536).rearrange("p (m j i) -> p m j i", m=3, j=2) for i in range(2)]
        xj = [wv(1036 * i, 1035) for i in range(2)]
        yj = [wv(2072 + T * i, T) for i in range(2)]
        sg = [wv(2072 + T * (2 + i), T) for i in range(2)]
        row = [work[0:4, T * i:T * i + T] for i in range(12)]
        stk = wv(T * 12, SEQ)
        rgx = wv(0, 1035)
        rg = {n: wv(1036 + T * i, T) for i, n in enumerate(("xc", "r", "i", "a", "t", "z", "sz", "sg", "h"))}
        rgw = [wv(14500 + 256 * i, 256).rearrange("p (m j) -> p m j", m=2) for i in range(2)]
        qt = wv(0, 2 * T).rearrange("p (a t) -> p a t", a=2)
        kt = wv(2 * T, 2 * T).rearrange("p (a t) -> p a t", a=2)
        vt = wv(4 * T, 2 * T).rearrange("p (a t) -> p a t", a=2)
        tg = [wv((6 + i) * T, T) for i in range(3)]
        rope = wv(9 * T, 2 * T).rearrange("p (a t) -> p a t", a=2)
        xc2 = wv(9 * T, 2 * T).rearrange("p (a t) -> p a t", a=2)
        dm = wv(11 * T, SEQ)
        B0 = 12 * T
        st = wv(B0, 514).rearrange("p (a e) -> p a e", a=2)
        wvv = wv(B0 + 514, 512).rearrange("p (i e) -> p i e", i=2)
        B1 = B0 + 514 + 512
        ktok = [wv(B1 + 256 * i, 256) for i in range(2)]
        vtok = [wv(B1 + 512 + 257 * i, 257) for i in range(2)]
        vw = [wv(B1 + 1026 + 257 * i, 257) for i in range(2)]
        sd = [wv(B1 + 1540 + 128 * i, 128) for i in range(2)]
        inter = wv(B1 + 1796, 257)
        hn = wv(B1 + 2053, 257)
        wqk = wv(B1, 1024).rearrange("p (m i j) -> p m i j", m=2, i=2)
        cst = [wv(B1 + 1024 * i, 1024).rearrange("p (b d e) -> p b d e", b=2, d=2) for i in range(2)]
        dg = kt[:, 0, 0:512]

        def store(sp, b, n8, l, h, cout):
            sp.wait_ge(S["cs_new"], CR + 4 * n8 + b + 1)
            sp.dma_start(io[cout][l, h, :, 2 * b:2 * b + 2],
                         cst[b % 2]).then_inc(S[f"cs_st{b % 2}"], 16)

        psum = ctx.enter_context(nc.psum_tensor("psum", [P, 8, 512], F32))
        TK, ST, PN1, PN2, PS = 3, 4, 5, 6, 7

        own = {
            "pe": "mm sq_used ab_mm gp_done tr_mm bc_mm rg_mm kv_mm st_mm num_mm ps_mm ht_mm qk_mm dm_mm vs_mm "
                  "vb_mm hs_mm den_mm red_mm osq_used",
            "act": "evac cH_done ada_out sqr rs_sqrt uH_ready wif_ready ab_out sig_done rows_in row_exp lam_exp "
                   "tr_out exr_exp bc_out rg_sig rg_ev rg_sq2 rg_sqrt kv_out in_done sq_done g_sig qk_ev vs_out "
                   "dm_exp xc_skip cs_dec red_sqrt osq ors_sqrt",
            "dve": "cL_done ada_ready rs_var tmp_ready plane_ready zeroed xj_pad conv_done xc_ready row_abs lam_abs "
                   "stk_ready rg_xc rg_fac rg_y rope_done stt vw_done sd_done h_ready var_ready hn_ready ht_done "
                   "g_half br_done selh dm_arg dm_done dg_done cs_new red_in red_out n_out ors_var xnew ldone",
            "pool": "hi_done split",
            "sp": "xsp0 xsp1 cs_st0 cs_st1 st_out sdone",
        }
        S = {n: sem(n) for names in own.values() for n in names.split()}
        for n in "settled const_in x_in par_in wraw0 wraw1 wt_in0 wt_in1 rgw_in0 rgw_in1 rope_in ml_in cs_in0 cs_in1 xt_in0 xt_in1 spill out_st".split():
            S[n] = sem(n)

        def open_balance(eng, who):
            for n in own[who].split():
                eng.sem_inc(S[n], CD if n in DMA_CREDIT else CR)

        def settle(eng):
            eng.sem_inc(S["settled"], 1)

        def pcol(name, i, n=1):
            return par[:, bass.ds(PAR[name][0] + i, n)]

        def tok(ap, g):
            return ap[:, g * GW:(g + 1) * GW]

        def evs(l, t, g):
            return l * N_PROJ + 3 * (t - NADA) + g + 1

        def mms(l, t, g):
            return (l * NT + t) * 3 + g + 1

        block = ctx.enter_context(nc.Block())

        @block.sync
        def _(sp):
            open_balance(sp, "sp")
            for dst, name in ((ident, "ident"), (ones, "ones"), (mask, "mask"), (sel, "sel"), (rcol, "rcol"),
                              (cT, "cT")):
                sp.dma_start(dst[:], io[name]).then_inc(S["const_in"], 16)
            sp.dma_start(dret[:, :, :], io["dret"]).then_inc(S["const_in"], 16)
            for k in range(KT):
                sp.dma_start(xm[:, k, 0:SEQ], io["xp"][k]).then_inc(S["x_in"], 16)
                sp.dma_start(xm[:, k, SEQ:T], io["xs"][k]).then_inc(S["x_in"], 16)
            sp.wait_ge(S["x_in"], 32 * KT)
            with sp.Fori(0, DEPTH) as l:
                sp.wait_ge(S["ldone"], CR + l)
                for dst, name in ((par, "par"), (wif, "wif"), (rcs, "rcs"), (mcs, "mcs"), (rh0, "rh0"),
                                  (mn0, "mn0"), (mm0, "mm0"), (bifp, "bif")):
                    sp.dma_start(dst[:], io[name][l]).then_inc(S["par_in"], 16)
                sp.dma_start(io["xkeep"], xm[:, :, :]).then_inc(S["spill"], 16)
                for h in range(HEADS):
                    sp.wait_ge(S["ab_mm"], CR + 4 * l + h - 1)
                    sp.dma_start(wt[h % 2].rearrange("p m j i -> p (m j i)"), io["wqkvT"][l, h]).then_inc(S[f"wt_in{h % 2}"], 16)
                with sp.Fori(0, KT // 2) as i:
                    for s in range(2):
                        j = 2 * i + s
                        sp.wait_ge(S["evac"], CR + evs(l, XML0 + j, 2))
                        sp.dma_start(io["xml_d"][j], xj[s][:, 3:3 + T]).then_inc(S[f"xsp{s}"], 16)
                        sp.wait_ge(S["xc_ready"], CR + KT * l + j + 1)
                        sp.dma_start(io["xc_d"][j], yj[s]).then_inc(S[f"xsp{s}"], 16)
                sp.wait_ge(S["stk_ready"], CR + l + 1)
                settle(sp)
                sp.dma_start(io["p_m"][l], mc[:, NC:NC + 1]).then_inc(S["out_st"], 16)
                sp.dma_start(io["s_m"][l], smx[:, 1, :]).then_inc(S["out_st"], 16)
                sp.dma_start(io["s_mconv"][l], mcsn[:, :, :, :]).then_inc(S["out_st"], 16)
                with sp.Fori(0, KT // 2) as i:
                    for s in range(2):
                        j = 2 * i + s
                        sp.wait_ge(S["rg_mm"], CR + 3 * (KT * l + j - 1))
                        sp.dma_start(rgw[s].rearrange("p m j -> p (m j)"), io["rgw"][l, j]).then_inc(S[f"rgw_in{s}"], 16)
                sp.wait_ge(S["rg_y"], CR + KT * l + KT)
                sp.dma_start(rope[:, :, :], io["rope"]).then_inc(S["rope_in"], 16)
                sp.dma_start(io["rg_h"][l], rhn[:, :, :]).then_inc(S["out_st"], 16)
                sp.dma_start(io["s_rconv"][l], rcsn[:, :, :, :]).then_inc(S["out_st"], 16)
                sp.dma_start(io["p_conv"][l], pcn[:, :, :, :]).then_inc(S["out_st"], 16)
                for ml in (False, True):
                    cin, cout, pout = (("ml_C", "s_C", "p_C") if ml else ("ret_S", "s_S", "p_S"))
                    with sp.Fori(0, HEADS) as h:
                        n8 = 8 * l + 4 * ml + h
                        if ml:
                            sp.wait_ge(S["br_done"], CR + n8)
                            sp.wait_ge(S["xsp0"], CD + 128 * (l + 1))
                            sp.wait_ge(S["xsp1"], CD + 128 * (l + 1))
                            sp.wait_ge(S["cs_st0"], CD + 32 * n8)
                            sp.wait_ge(S["cs_st1"], CD + 32 * n8)
                            for a in range(2):
                                sp.dma_start(vt[:, a, :], io["xml_d"][2 * h + a]).then_inc(S["ml_in"], 16)
                                sp.dma_start(xc2[:, a, :], io["xc_d"][2 * h + a]).then_inc(S["ml_in"], 16)
                            sp.dma_start(wqk.rearrange("p m i j -> p (m i j)"), io["wqk"][l, h]).then_inc(S["ml_in"], 16)
                            sp.dma_start(wvv.rearrange("p i e -> p (i e)"), io["wv"][l, h]).then_inc(S["ml_in"], 16)
                        sp.wait_ge(S["ps_mm"], CR + 8 * n8 + 8)
                        sp.wait_ge(S["h_ready"], CR + 8 * n8 + 8)
                        for b in range(4):
                            if b >= 2:
                                sp.wait_ge(S[f"cs_st{b % 2}"], CD + 32 * n8 + 16)
                                sp.wait_ge(S["hs_mm"], CR + 4 * n8 + b - 1)
                            sp.dma_start(cst[b % 2], io[cin][l, h, :, 2 * b:2 * b + 2]).then_inc(S[f"cs_in{b % 2}"], 16)
                            if b == 0:
                                sp.wait_ge(S["stt"], CR + 9 * n8 + 9)
                                sp.dma_start(io[pout][l, h], st[:, :, 0:256]).then_inc(S["st_out"], 16)
                                if ml:
                                    sp.dma_start(io["p_n"][l, h], pn[:, :]).then_inc(S["st_out"], 16)
                                else:
                                    sp.sem_inc(S["st_out"], 16)
                            if b >= 1:
                                store(sp, b - 1, n8, l, h, cout)
                        store(sp, 3, n8, l, h, cout)
                        if ml:
                            sp.wait_ge(S["n_out"], CR + 4 * l + h + 1)
                            sp.dma_start(io["s_n"][l, h], mnn[:, :, :]).then_inc(S["st_out"], 16)
                        else:
                            sp.sem_inc(S["st_out"], 16)
                for k in range(KT):
                    if k >= 2:
                        sp.wait_ge(S["xnew"], CR + KT * l + k - 1)
                    else:
                        sp.wait_ge(S["br_done"], CR + 8 * l + 8)
                        sp.wait_ge(S["spill"], 16 * (l + 1))
                    sp.dma_start(xt[k % 2], io["xkeep"][:, k, :]).then_inc(S[f"xt_in{k % 2}"], 16)
                sp.wait_ge(S["out_st"], 96 * (l + 1))
                sp.wait_ge(S["st_out"], CD + 48 * 8 * (l + 1))
                for s in range(2):
                    sp.wait_ge(S[f"cs_st{s}"], CD + 32 * 8 * (l + 1))
                sp.sem_inc(S["sdone"], 1)
            sp.wait_ge(S["ldone"], CR + DEPTH)
            for k in range(KT):
                sp.dma_start(io["y"][k], xm[:, k, :]).then_inc(S["x_in"], 16)
            sp.wait_ge(S["x_in"], 48 * KT)

        @block.gpsimd
        def _(pool):
            open_balance(pool, "pool")
            for s in range(2):
                pool.dma_start(wraw[s][:, :], io["wall"][s]).then_inc(S[f"wraw{s}"], 16)

            def split_pair(i, more):
                for s in range(2):
                    t = 2 * i + s
                    pool.wait_ge(S[f"wraw{s}"], 16 * i + 16)
                    pool.wait_ge(S["mm"], CR + 3 * t - 3)
                    raw = wraw[s][:, :].rearrange("p (k m) -> p k m", k=KT)
                    settle(pool)
                    pool.tensor_scalar(wH[s][:, :, :], raw, 1.0, 1.0, ALU.mult, ALU.mult).then_inc(S["hi_done"], 1)
                    pool.wait_ge(S["hi_done"], CR + t + 1)
                    pool.tensor_tensor(wL[s][:, :, :], raw, wH[s][:, :, :].bitcast(F32), ALU.subtract).then_inc(S["split"], 1)
                    if more:
                        pool.wait_ge(S["split"], CR + t + 1)
                        pool.dma_start(wraw[s][:, :], io["wall"][t + 2]).then_inc(S[f"wraw{s}"], 16)

            with pool.Fori(0, DEPTH * NT // 2 - 1) as i:
                split_pair(i, True)
            split_pair(DEPTH * NT // 2 - 1, False)

        @block.tensor
        def _(pe):
            open_balance(pe, "pe")

            def proj_group(l, t, s, g, hi=uH, lo=uL):
                if g == 0:
                    pe.wait_ge(S["split"], CR + l * NT + t + 1)
                pe.wait_ge(S["evac"], CR + evs(l, t, g) - 3)
                for k in range(KT):
                    for n, (w, x) in enumerate(((wH, hi), (wL, hi), (wH, lo))):
                        mm = pe.matmul(psum[:, g, 0:GW], w[s][:, k, :], x[:, k, g * GW:(g + 1) * GW],
                                       start=(k == 0 and n == 0), stop=(k == KT - 1 and n == 2))
                mm.then_inc(S["mm"], 1)

            def proj(l, t, s):
                for g in range(NG):
                    proj_group(l, t, s, g)

            pe.wait_ge(S["const_in"], 112)
            pe.wait_ge(S["cL_done"], CR + 1)
            pe.wait_ge(S["zeroed"], CR + 1)
            settle(pe)
            with pe.Fori(0, DEPTH) as l:
                for k in range(KT):
                    pe.wait_ge(S["sqr"], CR + KT * l + k + 1)
                    for g in range(NG):
                        mm = pe.matmul(psum[:, g, 0:GW], ones[:, :], tok(sq[k % 2], g), start=(k == 0), stop=(k == KT - 1))
                    mm.then_inc(S["sq_used"], 1)
                settle(pe)
                with pe.Fori(0, NADA // 2) as i:
                    for s in range(2):
                        pe.wait_ge(S["split"], CR + l * NT + 2 * i + s + 1)
                        if s == 0:
                            pe.wait_ge(S["ada_out"], CR + NADA // 2 * l + i)
                        for k in range(KT):
                            for n, (w, x) in enumerate(((wH, cH), (wL, cH), (wH, cL))):
                                mm = pe.matmul(psum[:, TK, 10 * s:10 * s + 10], w[s][:, k, :], x[:, k, :],
                                               start=(k == 0 and n == 0), stop=(k == KT - 1 and n == 2))
                            if k in (2, 5, 7):
                                mm.then_inc(S["mm"], 1)
                pe.wait_ge(S["wif_ready"], CR + l + 1)
                for h in range(HEADS):
                    pe.wait_ge(S[f"wt_in{h % 2}"], 32 * l + 16 * (h // 2) + 16)
                    pe.wait_ge(S["ab_out"], CR + 4 * l + h)
                    if h == 0:
                        pe.wait_ge(S["ada_out"], CR + NADA // 2 * (l + 1))
                    for i in range(2):
                        for n in range(6):
                            m, jj = n // 2, n % 2
                            c = (m // 2) * 16 + i * 8
                            mm = pe.matmul(psum[:, TK, c:c + 8], wt[h % 2][:, m, jj, i * P:(i + 1) * P],
                                           wif[:, 8 * m + 2 * h + jj, :], start=(n in (0, 4)), stop=(n in (3, 5)))
                    mm.then_inc(S["ab_mm"], 1)
                for g in range(NG):
                    pe.matmul(psum[0:HCOL, ST + g, 0:GW], zf[:, :], ones[:, 0:1].to_broadcast([P, GW]), start=True,
                              stop=False, skip_group_check=True)
                pe.wait_ge(S["plane_ready"], CR + 2 * KT * l + KT)
                settle(pe)
                with pe.Fori(0, KT // 2) as i:
                    for s in range(2):
                        proj(l, XML0 + 2 * i + s, s)
                    for s in range(2):
                        pe.wait_ge(S["xc_ready"], CR + KT * l + 2 * i + s + 1)
                        for g in range(NG):
                            pe.matmul(psum[0:HCOL, ST + g, 0:GW], fj[s][:, 0, :], tok(yj[s], g), start=False, stop=False,
                                      skip_group_check=True)
                            mm = pe.matmul(psum[0:HCOL, ST + g, 0:GW], fj[s][:, 1, :], xj[s][:, 3 + g * GW:3 + (g + 1) * GW],
                                           start=False, stop=True, skip_group_check=True)
                        mm.then_inc(S["gp_done"], 1)
                settle(pe)
                with pe.Fori(0, KT // 2) as i:
                    for s in range(2):
                        for m in range(3):
                            proj(l, RG0 + 6 * i + 3 * s + m, (3 * s + m) % 2)
                        n = KT * l + 2 * i + s
                        pe.wait_ge(S["rg_xc"], CR + n + 1)
                        pe.wait_ge(S[f"rgw_in{s}"], 64 * l + 16 * i + 16)
                        if s == 0:
                            pe.wait_ge(S["rows_in"], CR + l + 1)
                        for g in range(NG):
                            pe.wait_ge(S["rg_ev"], CR + 6 * n + (2 if g == 2 else 0))
                            for m in range(2):
                                mm = pe.matmul(psum[:, TK + 2 * m + g % 2, 0:GW], rgw[s][:, m, :], tok(rg["xc"], g),
                                               start=True, stop=True)
                            mm.then_inc(S["rg_mm"], 1)
                pe.wait_ge(S["rg_ev"], CR + 6 * KT * (l + 1))
                pe.wait_ge(S["stk_ready"], CR + l + 1)
                for a in range(2):
                    pe.wait_ge(S["tr_out"], CR + 2 * l + a)
                    for c in range(4):
                        mm = pe.transpose(psum[:, TK, c * P:c * P + 100], stk[0:100, (4 * a + c) * P:(4 * a + c + 1) * P],
                                          ident[0:100, 0:100])
                    mm.then_inc(S["tr_mm"], 1)
                pe.wait_ge(S["exr_exp"], CR + l + 1)
                for h in range(HEADS):
                    mm = pe.matmul(psum[:, PN1, 32 * h:32 * h + 32], sel[:, h * P:(h + 1) * P],
                                   exr[:, :, :].rearrange("p a b -> p (a b)"), start=True, stop=True)
                mm.then_inc(S["bc_mm"], 1)
                pe.wait_ge(S["bc_out"], CR + l + 1)
                pe.wait_ge(S["tr_out"], CR + 2 * l + 2)

                def stage_a(n8, c, ml):
                    cs = slice(c * CH, (c + 1) * CH)
                    pe.wait_ge(S["kv_out"], CR + 8 * n8 + c)
                    for a in range(2):
                        pe.transpose(psum[:, TK, a * P:(a + 1) * P], kt[:, a, cs], ident[:, :])
                    for a in range(2):
                        if ml:
                            mm = pe.matmul(psum[:, TK, 256:512], vt[:, a, cs], wvv[:, a, :], start=(a == 0), stop=(a == 1))
                        else:
                            mm = pe.transpose(psum[:, TK, 256 + a * P:256 + (a + 1) * P], vt[:, a, cs], ident[:, :])
                    mm.then_inc(S["kv_mm"], 1)
                    pe.wait_ge(S["sd_done"], CR + 8 * n8 + c)
                    pe.wait_ge(S["ht_done"], CR + 8 * n8 + c - 2)
                    for a in range(2):
                        mm = pe.matmul(psum[:, ST, 0:CH], kt[:, a, cs], qt[:, a, cs], start=(a == 0), stop=(a == 1))
                    mm.then_inc(S["st_mm"], 1)

                def stage_b(n8, c, ml):
                    cs, e = slice(c * CH, (c + 1) * CH), 257 if ml else 256
                    pe.wait_ge(S["vw_done"], CR + 8 * n8 + c + 1)
                    pe.wait_ge(S["sd_done"], CR + 8 * n8 + c + 1)
                    pe.wait_ge(S["h_ready"], CR + 8 * n8 + c)
                    pe.wait_ge(S["in_done"], CR + 8 * n8 + c)
                    pe.wait_ge(S["stt"], CR + 9 * n8 + c + 1)
                    pe.matmul(psum[:, PN1, 0:e], sd[c % 2], vtok[c % 2][:, 0:e], start=True, stop=True)
                    if ml:
                        for a in range(2):
                            pe.matmul(psum[:, PN1, 300 + a:301 + a], ktok[c % 2][:, a * P:(a + 1) * P], vw[c % 2][:, 256:257],
                                      start=True, stop=True)
                    for a in range(2):
                        mm = pe.matmul(psum[:, PN2, 0:e], qt[:, a, cs], st[:, a, 0:e], start=(a == 0), stop=(a == 1))
                    mm.then_inc(S["num_mm"], 1)
                    for a in range(2):
                        mm = pe.matmul(psum[:, PS, 256 * a:256 * a + 256], ktok[c % 2][:, a * P:(a + 1) * P],
                                       vw[c % 2][:, 0:256], start=True, stop=True)
                    mm.then_inc(S["ps_mm"], 1)

                def stage_c(n8, c):
                    pe.wait_ge(S["hn_ready"], CR + 8 * n8 + c + 1)
                    pe.wait_ge(S["sd_done"], CR + 8 * n8 + min(c + 3, NC))
                    pe.wait_ge(S["ht_done"], CR + 8 * n8 + c)
                    for a in range(2):
                        mm = pe.transpose(psum[:, ST, (a + 1) * P:(a + 2) * P], hn[:, a * P:(a + 1) * P], ident[:, :])
                    mm.then_inc(S["ht_mm"], 1)

                def chunks(l, h, n8, t0, ml):
                    for slot in range(NC + 2):
                        for g in ([slot] if slot < 9 else [9, 10, 11]):
                            proj_group(l, t0 + g // 3, (g // 3) % 2, g % 3)
                        if slot < NC:
                            stage_a(n8, slot, ml)
                        if 1 <= slot <= NC:
                            stage_b(n8, slot - 1, ml)
                        if slot >= 2:
                            stage_c(n8, slot - 2)

                def samples(n8, l, h, ml):
                    for b in range(4):
                        pe.wait_ge(S["dg_done"], CR + 4 * n8 + b + 1)
                        pe.wait_ge(S["cs_new"], CR + 4 * n8 + b)
                        if b == 0:
                            pe.wait_ge(S["h_ready"], CR + 8 * n8 + 8)
                            pe.wait_ge(S["in_done"], CR + 8 * n8 + 8)
                        pe.matmul(psum[:, PN1, 0:512], ones[:, :], dg, start=True, stop=True).then_inc(S["vb_mm"], 1)
                        pe.wait_ge(S["cs_new"], CR + 4 * n8 + b + 1)
                        for e in range(2):
                            for a in range(2):
                                o = a * NB + 2 * b + e
                                for d in range(2):
                                    mm = pe.matmul(psum[:, PN2, o:o + 1], cst[b % 2][:, e, d, a * P:(a + 1) * P],
                                                   qs[:, 0, d, 2 * b + e:2 * b + e + 1], start=(d == 0), stop=(d == 1))
                        mm.then_inc(S["hs_mm"], 1)
                    if ml:
                        pe.wait_ge(S["n_out"], CR + 4 * l + h + 1)
                        for d in range(2):
                            mm = pe.matmul(psum[:, PN1, 0:NB], ones[:, :], sm2[:, 6, 8 * d:8 * d + 8], start=(d == 0), stop=(d == 1))
                        mm.then_inc(S["den_mm"], 1)
                    for r in range(2):
                        pe.wait_ge(S["red_in"], CR + 2 * n8 + 1 + r)
                        for d in range(2):
                            mm = pe.matmul(psum[:, PN1, 32 + 16 * r:40 + 16 * r], ones[:, :], sm2[:, 1 + r, 8 * d:8 * d + 8],
                                           start=(d == 0), stop=(d == 1))
                        mm.then_inc(S["red_mm"], 1)

                settle(pe)
                with pe.Fori(0, HEADS) as h:
                    n8 = 8 * l + h
                    t0 = RET0 + 10 * h
                    for m in range(6):
                        proj(l, t0 + m, m % 2)
                    pe.wait_ge(S["rope_done"], CR + n8 + 1)
                    pe.wait_ge(S["evac"], CR + evs(l, t0 + 5, 2))
                    chunks(l, h, n8, t0 + 6, False)
                    samples(n8, l, h, False)
                settle(pe)
                with pe.Fori(0, HEADS) as h:
                    n8 = 8 * l + 4 + h
                    t0 = ML0 + 4 * h
                    pe.wait_ge(S["ml_in"], 96 * (4 * l + h) + 96)
                    for n in range(12):
                        m, a, g = n // 6, (n // 3) % 2, n % 3
                        pe.wait_ge(S["qk_ev"], CR + 12 * (4 * l + h) + n - 3)
                        if n == 0:
                            pe.wait_ge(S["br_done"], CR + n8)
                        for i in range(2):
                            mm = pe.matmul(psum[:, TK + n % 4, 0:GW], wqk[:, m, i, a * P:(a + 1) * P],
                                           xc2[:, i, g * GW:(g + 1) * GW], start=(i == 0), stop=(i == 1))
                        mm.then_inc(S["qk_mm"], 1)
                    for a in range(2):
                        for i in range(2):
                            mm = pe.matmul(psum[:, PS, a * NB:(a + 1) * NB], wvv[:, i, a * P:(a + 1) * P], vt[:, i, SEQ:T],
                                           start=(i == 0), stop=(i == 1))
                    mm.then_inc(S["vs_mm"], 1)
                    pe.wait_ge(S["selh"], CR + 4 * l + h + 1)
                    pe.wait_ge(S["qk_ev"], CR + 12 * (4 * l + h) + 12)
                    for a in range(2):
                        mm = pe.matmul(psum[:, TK + a, 0:512], selh[:, :], nmrow[:, 512 * a:512 * a + 512], start=True, stop=True)
                    mm.then_inc(S["dm_mm"], 1)
                    pe.wait_ge(S["dm_arg"], CR + 4 * l + h + 1)
                    pe.wait_ge(S["rope_done"], CR + n8 + 1)
                    pe.wait_ge(S["vs_out"], CR + 4 * l + h + 1)
                    chunks(l, h, n8, t0, True)
                    samples(n8, l, h, True)
                for g in range(NG):
                    if g == 0:
                        pe.wait_ge(S["br_done"], CR + 8 * l + 8)
                    pe.matmul(psum[:, ST + g, 0:GW], zf[:, 0:1].to_broadcast([P, P]), ones[:, 0:1].to_broadcast([P, GW]),
                              start=True, stop=False, skip_group_check=True)
                pe.wait_ge(S["plane_ready"], CR + 2 * KT * l + 2 * KT)
                settle(pe)
                with pe.Fori(0, KT // 2) as i:
                    for s in range(2):
                        proj(l, OUT0 + 2 * i + s, s)
                    for s in range(2):
                        pe.wait_ge(S["osq"], CR + KT * l + 2 * i + s + 1)
                        for g in range(NG):
                            mm = pe.matmul(psum[:, ST + g, 0:GW], ones[:, :], tok(sq[s], g), start=False, stop=True,
                                           skip_group_check=True)
                        mm.then_inc(S["osq_used"], 1)

        @block.scalar
        def _(act):
            open_balance(act, "act")

            def activate(*args, **kw):
                made = act.activation(*args, **kw)
                act.drain()
                return made

            def evacuate(l, t, dst, func=ACT.Copy, scale=1.0, groups=(0, 1, 2)):
                for g in groups:
                    act.wait_ge(S["mm"], CR + mms(l, t, g))
                    activate(dst[:, g * GW:(g + 1) * GW], psum[:, g, 0:GW], func, scale=scale).then_inc(S["evac"], 1)

            act.wait_ge(S["const_in"], 112)
            activate(cH[:, :, :], cT[:, :, :], ACT.Copy).then_inc(S["cH_done"], 1)
            act.wait_ge(S["x_in"], 32 * KT)
            with act.Fori(0, DEPTH) as l:
                act.wait_ge(S["ldone"], CR + l)
                act.wait_ge(S["sdone"], CR + l)
                for k in range(KT):
                    act.wait_ge(S["sq_used"], CR + KT * l + k - 1)
                    activate(sq[k % 2], xm[:, k, :], ACT.Square).then_inc(S["sqr"], 1)
                act.wait_ge(S["par_in"], 128 * (l + 1))
                activate(wif[:, 8:16, :], wif[:, 8:16, :], ACT.Copy, scale=DH ** -0.5).then_inc(S["wif_ready"], 1)
                act.wait_ge(S["lam_abs"], CR + l + 1)
                activate(sm[:, 16:24], sm[:, 16:24], ACT.Exp, scale=-1.0).then_inc(S["lam_exp"], 1)
                act.wait_ge(S["rs_var"], CR + l + 1)
                activate(rs, rs, ACT.Sqrt).then_inc(S["rs_sqrt"], 1)
                with act.Fori(0, NADA // 2) as i:
                    act.wait_ge(S["mm"], CR + mms(l, 2 * i + 1, 2))
                    settle(act)
                    activate(ada[:, bass.ds(2 * i, 2), :], psum[:, TK, 0:20].rearrange("p (a c) -> p a c", a=2),
                                   ACT.Copy).then_inc(S["ada_out"], 1)
                act.wait_ge(S["ada_ready"], CR + l + 1)
                for k in range(KT):
                    act.wait_ge(S["tmp_ready"], CR + KT * l + k + 1)
                    activate(tmp_n[k % 2][:, 0:SEQ], tmp_n[k % 2][:, 0:SEQ], ACT.Identity, bias=ada[:, k, 0:1],
                                   scale=s1[:, k, 0:1])
                    activate(uH[:, k, :], tmp_n[k % 2], ACT.Copy).then_inc(S["uH_ready"], 1)
                for h in range(HEADS):
                    act.wait_ge(S["ab_mm"], CR + 4 * l + h + 1)
                    src = psum[:, TK, 0:32].rearrange("p (a i c) -> p a i c", a=2, i=2)
                    activate(fold[:, :, 2 * h:2 * h + 2, 0:4], src[:, :, :, 0:4], ACT.Copy)
                    activate(fold[:, :, 2 * h:2 * h + 2, 32:36], src[:, :, :, 4:8], ACT.Copy).then_inc(S["ab_out"], 1)
                act.wait_ge(S["xj_pad"], CR + l + 1)
                with act.Fori(0, KT // 2) as i:
                    for s in range(2):
                        n = KT * l + 2 * i + s
                        act.wait_ge(S["gp_done"], CR + n - 1)
                        act.wait_ge(S[f"xsp{s}"], CD + 32 * (4 * l + i))
                        evacuate(l, XML0 + 2 * i + s, xj[s][:, 3:3 + T])
                        act.wait_ge(S["conv_done"], CR + n + 1)
                        activate(sg[s], yj[s], ACT.Sigmoid).then_inc(S["sig_done"], 1)
                act.wait_ge(S["gp_done"], CR + KT * (l + 1))
                for s in range(2):
                    act.wait_ge(S[f"xsp{s}"], CD + 128 * (l + 1))
                activate(work[0:HCOL, 0:T].rearrange("p (g t) -> p g t", g=NG), psum[0:HCOL, ST:ST + NG, 0:GW],
                               ACT.Identity, bias=bifp[:, 0:1]).then_inc(S["rows_in"], 1)
                act.wait_ge(S["row_abs"], CR + l + 1)
                activate(row[2], row[2], ACT.Exp, scale=-1.0).then_inc(S["row_exp"], 1)
                act.wait_ge(S["stk_ready"], CR + l + 1)
                activate(exr[:, :, :], exr[:, :, :], ACT.Exp).then_inc(S["exr_exp"], 1)
                with act.Fori(0, KT // 2) as i:
                    for s in range(2):
                        j = 2 * i + s
                        n = KT * l + j
                        t = RG0 + 3 * j
                        act.wait_ge(S["rg_xc"], CR + n)
                        evacuate(l, t, rgx[:, 3:3 + T])
                        act.wait_ge(S["rg_y"], CR + n)
                        evacuate(l, t + 1, rg["z"])
                        evacuate(l, t + 2, rg["sg"], ACT.Sigmoid)
                        activate(rg["sz"], rg["z"], ACT.Sigmoid).then_inc(S["rg_sig"], 1)
                        for g in range(NG):
                            act.wait_ge(S["rg_mm"], CR + 3 * n + g + 1)
                            for m, dst in ((0, "r"), (1, "i")):
                                settle(act)
                                activate(tok(rg[dst], g), psum[:, TK + 2 * m + g % 2, 0:GW], ACT.Sigmoid,
                                               bias=pcol("rg_b_a" if m == 0 else "rg_b_x", j)).then_inc(S["rg_ev"], 1)
                        activate(rg["t"], rg["r"], ACT.Tanh, scale=nsp[:, 1, bass.ds(j, 1)])
                        activate(rg["a"], rg["r"], ACT.Exp, scale=nsp[:, 0, bass.ds(j, 1)])
                        activate(rg["r"], rg["a"], ACT.Square).then_inc(S["rg_sq2"], 1)
                        act.wait_ge(S["rg_fac"], CR + n + 1)
                        activate(rg["t"], rg["r"], ACT.Sqrt, scale=1.0).then_inc(S["rg_sqrt"], 1)
                for a in range(2):
                    act.wait_ge(S["tr_mm"], CR + 2 * l + a + 1)
                    src = psum[:, TK, 0:512].rearrange("p (c q x) -> p c q x", c=4, q=4)
                    activate(ucol[:, 4 * a:4 * a + 4, 0, :], src[:, :, 0, 0:4], ACT.Copy)
                    activate(ucol[:, 4 * a:4 * a + 4, 1:4, :], src[:, :, 1:4, 0:4], ACT.Exp).then_inc(S["tr_out"], 1)
                act.wait_ge(S["bc_mm"], CR + l + 1)
                activate(bc[:, :, :, :].rearrange("p h a b -> p (h a b)"), psum[:, PN1, 0:128], ACT.Copy).then_inc(S["bc_out"], 1)

                def chunks(l, h, n8, t0, ml):
                    e = 257 if ml else 256
                    act.wait_ge(S["cs_st0"], CD + 32 * n8)
                    act.wait_ge(S["cs_st1"], CD + 32 * n8)
                    for slot in range(NC + 2):
                        if slot == 7:
                            activate(tg[1], tg[1], ACT.Sigmoid)
                            activate(tg[2], tg[0], ACT.Sigmoid).then_inc(S["g_sig"], 1)
                        if slot < 6:
                            evacuate(l, t0 + slot // 3, tg[slot // 3], groups=(slot % 3,))
                        if slot == 7:
                            act.wait_ge(S["g_half"], CR + n8 + 1)
                        if slot >= 7:
                            for g in {7: (6, 7), 8: (8,), 9: (9, 10, 11)}[slot]:
                                evacuate(l, t0 + g // 3, tg[g // 3 - 1], groups=(g % 3,))
                        if slot < NC:
                            act.wait_ge(S["kv_mm"], CR + 8 * n8 + slot + 1)
                            act.wait_ge(S["ps_mm"], CR + 8 * n8 + slot - 1)
                            activate(ktok[slot % 2], psum[:, TK, 0:256], ACT.Copy)
                            activate(vtok[slot % 2][:, 0:256], psum[:, TK, 256:512], ACT.Copy).then_inc(S["kv_out"], 1)
                        if 1 <= slot <= NC:
                            c = slot - 1
                            act.wait_ge(S["num_mm"], CR + 8 * n8 + c + 1)
                            act.wait_ge(S["h_ready"], CR + 8 * n8 + c)
                            sc = ucol[:, c, 1, bass.ds(h, 1)] if ml else rcol[:, bass.ds(h, 1)]
                            settle(act)
                            activate(inter[:, 0:e], psum[:, PN2, 0:e], ACT.Copy, scale=sc).then_inc(S["in_done"], 1)
                            act.wait_ge(S["var_ready"], CR + 8 * n8 + c + 1)
                            activate(sm[:, 9:10], sm[:, 8:9], ACT.Sqrt).then_inc(S["sq_done"], 1)

                def samples(n8, l, h, ml):
                    for b in range(4):
                        act.wait_ge(S[f"cs_in{b % 2}"], 32 * n8 + 16 * (b // 2) + 16)
                        settle(act)
                        for e in range(2):
                            sc = bc[:, bass.ds(h, 1), 1, 2 * b + e] if ml else rcol[:, bass.ds(12 + h, 1)]
                            v = cst[b % 2][:, e, :, :].rearrange("p d e -> p (d e)")
                            o = activate(v, v, ACT.Copy, scale=sc)
                        o.then_inc(S["cs_dec"], 1)
                    act.wait_ge(S["red_out"], CR + n8 + 1)
                    activate(sm2[:, 3, 8:16], sm2[:, 3, 0:8], ACT.Sqrt).then_inc(S["red_sqrt"], 1)

                def last_sig(n8, l):
                    activate(qt[:, 0, :], tg[1], ACT.Sigmoid)
                    activate(tg[2], tg[2], ACT.Sigmoid).then_inc(S["g_sig"], 1)

                with act.Fori(0, HEADS) as h:
                    n8 = 8 * l + h
                    t0 = RET0 + 10 * h
                    act.wait_ge(S["br_done"], CR + n8)
                    act.wait_ge(S["rg_y"], CR + KT * (l + 1))
                    for a in range(2):
                        evacuate(l, t0 + a, qt[:, a, :])
                    for a in range(2):
                        evacuate(l, t0 + 2 + a, kt[:, a, :], scale=DH ** -0.5)
                    for a in range(2):
                        evacuate(l, t0 + 4 + a, vt[:, a, :])
                    act.wait_ge(S["rope_done"], CR + n8 + 1)
                    chunks(l, h, n8, t0 + 6, False)
                    samples(n8, l, h, False)
                    last_sig(n8, l)
                with act.Fori(0, HEADS) as h:
                    n8 = 8 * l + 4 + h
                    t0 = ML0 + 4 * h
                    act.wait_ge(S["br_done"], CR + n8)
                    for n in range(12):
                        act.wait_ge(S["qk_mm"], CR + 12 * (4 * l + h) + n + 1)
                        dst = (qt, kt)[n // 6][:, (n // 3) % 2, :]
                        activate(tok(dst, n % 3), psum[:, TK + n % 4, 0:GW], ACT.Copy,
                                       scale=(1.0, DH ** -0.5)[n // 6]).then_inc(S["qk_ev"], 1)
                    for a in range(2):
                        settle(act)
                        activate(xc2[:, a, :], xc2[:, a, :], ACT.Copy, scale=pcol("ml_skip", 2 * h + a))
                    act.wait_ge(S["vs_mm"], CR + 4 * l + h + 1)
                    activate(qs[:, 2, :, :].rearrange("p a b -> p (a b)"), psum[:, PS, 0:16], ACT.Copy).then_inc(S["vs_out"], 1)
                    act.wait_ge(S["dm_arg"], CR + 4 * l + h + 1)
                    activate(dm, dm, ACT.Exp).then_inc(S["dm_exp"], 1)
                    chunks(l, h, n8, t0, True)
                    samples(n8, l, h, True)
                    last_sig(n8, l)
                act.wait_ge(S["br_done"], CR + 8 * l + 8)
                for k in range(KT):
                    activate(uH[:, k, :], xm[:, k, :], ACT.Copy).then_inc(S["uH_ready"], 1)
                act.wait_ge(S["plane_ready"], CR + 2 * KT * (l + 1))
                with act.Fori(0, KT // 2) as i:
                    for s in range(2):
                        j = 2 * i + s
                        n = KT * l + j
                        for g in range(NG):
                            act.wait_ge(S["mm"], CR + mms(l, OUT0 + j, g))
                            settle(act)
                            activate(xm[:, bass.ds(j, 1), g * GW:(g + 1) * GW], psum[:, g, 0:GW].unsqueeze(1), ACT.Copy).then_inc(S["evac"], 1)
                        act.wait_ge(S["osq_used"], CR + n - 1)
                        settle(act)
                        activate(sq[s].unsqueeze(1), xm[:, bass.ds(j, 1), :], ACT.Square).then_inc(S["osq"], 1)
                act.wait_ge(S["ors_var"], CR + l + 1)
                activate(rs, rs, ACT.Sqrt).then_inc(S["ors_sqrt"], 1)

        @block.vector
        def _(dve):
            open_balance(dve, "dve")

            def fenced(op):
                def run(*args, **kw):
                    made = op(*args, **kw)
                    dve.drain()
                    return made
                return run

            tt, ts, stt_, cp, rec, scan, memset, bn_stats, bn_aggr, nop = map(fenced, (
                nc.vector.tensor_tensor, nc.vector.tensor_scalar, nc.vector.scalar_tensor_tensor, nc.vector.tensor_copy,
                nc.vector.reciprocal, nc.vector.tensor_tensor_scan, nc.vector.memset, nc.vector.bn_stats,
                nc.vector.bn_aggr, nc.vector.engine_nop))

            def log1p(z, z2, p):
                ts(p, z2, LOG1P_TERMS[0], None, ALU.mult)
                for c in LOG1P_TERMS[1:]:
                    stt_(p, p, c, z2, ALU.add, ALU.mult)
                stt_(p, p, 1.0, z, ALU.add, ALU.mult)

            def conv(x, y, name, j, state, new, pout):
                w = "rg_conv_w" if name == "rg" else "ml_conv_w"
                b = "rg_conv_b" if name == "rg" else "ml_conv_b"
                ts(y, x[:, 3:3 + T], pcol(w, 3 * KT + j), pcol(b, j), ALU.mult, ALU.add)
                for tap in (2, 1, 0):
                    stt_(y[:, 0:SEQ], x[:, tap:tap + SEQ], pcol(w, tap * KT + j), y[:, 0:SEQ], ALU.mult, ALU.add)
                    stt_(y[:, SEQ:T].unsqueeze(1), state[:, bass.ds(j, 1), tap, :], pcol(w, tap * KT + j),
                         y[:, SEQ:T].unsqueeze(1), ALU.mult, ALU.add)
                cp(new[:, bass.ds(j, 1), 0:2, :], state[:, bass.ds(j, 1), 1:3, :])
                cp(new[:, bass.ds(j, 1), 2, :], x[:, 3 + SEQ:3 + T].unsqueeze(1))
                return cp(pcn[:, pout, bass.ds(j, 1), :], x[:, SEQ:SEQ + 3].unsqueeze(1))

            memset(fold[:, :, :, :], 0.0)
            memset(zf[:, :], 0.0)
            memset(mc[:, 0:1], 0.0)
            memset(work[0:P, 0:1], 0.0).then_inc(S["zeroed"], 1)
            dve.wait_ge(S["cH_done"], CR + 1)
            tt(cL[:, :, :], cT[:, :, :], cH[:, :, :].bitcast(F32), ALU.subtract).then_inc(S["cL_done"], 1)
            with dve.Fori(0, DEPTH) as l:
                dve.wait_ge(S["sdone"], CR + l)
                dve.wait_ge(S["par_in"], 128 * (l + 1))
                lam = pcol("rg_lambda", 0, KT)
                stt_(sm[:, 16:24], lam, -1.0, lam, ALU.mult, ALU.max).then_inc(S["lam_abs"], 1)
                dve.wait_ge(S["lam_exp"], CR + l + 1)
                ts(sm[:, 24:32], sm[:, 16:24], 2.0, None, ALU.add)
                rec(sm[:, 24:32], sm[:, 24:32])
                tt(sm[:, 24:32], sm[:, 24:32], sm[:, 16:24], ALU.mult)
                tt(sm[:, 32:40], sm[:, 24:32], sm[:, 24:32], ALU.mult)
                log1p(sm[:, 24:32], sm[:, 32:40], sm[:, 40:48])
                ts(sm[:, 48:56], lam, -1.0, 0.0, ALU.mult, ALU.max)
                stt_(sm[:, 48:56], sm[:, 40:48], 2.0, sm[:, 48:56], ALU.mult, ALU.add)
                ts(nsp[:, 0, :], sm[:, 48:56], -RG_C, None, ALU.mult)
                ts(nsp[:, 1, :], sm[:, 48:56], RG_C, None, ALU.mult)
                dve.wait_ge(S["sq_used"], CR + KT * (l + 1))
                ts(rs.rearrange("p (g t) -> p g t", g=NG), psum[:, 0:NG, 0:GW], 1.0 / D, EPS, ALU.mult, ALU.add).then_inc(S["rs_var"], 1)
                dve.wait_ge(S["rs_sqrt"], CR + l + 1)
                rec(rs, rs)
                dve.wait_ge(S["ada_out"], CR + NADA // 2 * (l + 1))
                tt(ada[:, :, :], ada[:, :, :], pcol("b_ada", 0, NADA).unsqueeze(2).to_broadcast([P, NADA, 10]), ALU.add)
                stt_(s1[:, :, :], ada[:, KT:2 * KT, :], 1.0, pcol("norm_pre", 0, KT).unsqueeze(2).to_broadcast([P, KT, 10]),
                     ALU.add, ALU.mult)
                tt(gpo[:, :, :], ada[:, 2 * KT:, :], pcol("norm_post", 0, KT).unsqueeze(2).to_broadcast([P, KT, 10]),
                   ALU.mult).then_inc(S["ada_ready"], 1)

                def low(k):
                    dve.wait_ge(S["uH_ready"], CR + 2 * KT * l + k + 1)
                    tt(uL[:, k, :], tmp_n[k % 2], uH[:, k, :].bitcast(F32), ALU.subtract).then_inc(S["plane_ready"], 1)

                for k in range(KT):
                    t_ = tmp_n[k % 2]
                    tt(t_, xm[:, k, :], rs, ALU.mult)
                    tt(t_[:, SEQ:T], t_[:, SEQ:T], s1[:, k, 1:9], ALU.mult)
                    tt(t_[:, SEQ:T], t_[:, SEQ:T], ada[:, k, 1:9], ALU.add).then_inc(S["tmp_ready"], 1)
                    if k >= 1:
                        low(k - 1)
                low(KT - 1)
                dve.wait_ge(S["ab_out"], CR + 4 * (l + 1))
                for s in range(2):
                    o = memset(xj[s][:, 0:3], 0.0)
                o.then_inc(S["xj_pad"], 1)
                settle(dve)
                with dve.Fori(0, KT // 2) as i:
                    for s in range(2):
                        j = 2 * i + s
                        n = KT * l + j
                        dve.wait_ge(S["gp_done"], CR + n - 1)
                        dve.wait_ge(S[f"xsp{s}"], CD + 32 * (4 * l + i))
                        cp(fj[s][:, :, :].unsqueeze(2), fold[:, :, bass.ds(j, 1), :])
                        dve.wait_ge(S["evac"], CR + evs(l, XML0 + j, 2))
                        conv(xj[s], yj[s], "ml", j, mcs, mcsn, 1).then_inc(S["conv_done"], 1)
                        dve.wait_ge(S["sig_done"], CR + n + 1)
                        tt(yj[s], yj[s], sg[s], ALU.mult).then_inc(S["xc_ready"], 1)
                dve.wait_ge(S["rows_in"], CR + l + 1)
                R = row
                R0 = work[0:4, 0:T]
                memset(stk, 0.0)
                cp(R[1], work[32:36, 0:T])
                stt_(R[2], R[1], -1.0, R[1], ALU.mult, ALU.max).then_inc(S["row_abs"], 1)
                ts(R[6], R[1], 0.0, None, ALU.min)
                dve.wait_ge(S["row_exp"], CR + l + 1)
                ts(R[3], R[2], 2.0, None, ALU.add)
                rec(R[3], R[3])
                tt(R[3], R[2], R[3], ALU.mult)
                tt(R[4], R[3], R[3], ALU.mult)
                log1p(R[3], R[4], R[5])
                stt_(R[6], R[5], -2.0, R[6], ALU.mult, ALU.add)
                cs = [slice(c * CH, (c + 1) * CH) for c in range(NC)]
                for c in range(NC):
                    scan(R[7][:, cs[c]], ones[0:4, :], R[6][:, cs[c]], 0.0, ALU.mult, ALU.add)
                tt(R[8][:, 0:SEQ], R0[:, 0:SEQ], R[7][:, 0:SEQ], ALU.subtract)
                for c in range(NC):
                    scan(R[9][:, cs[c]], R[8][:, cs[c]], R[8][:, cs[c]], mc[:, c:c + 1], ALU.max, ALU.max)
                    e = (c + 1) * CH - 1
                    tt(mc[:, c + 1:c + 2], R[9][:, e:e + 1], R[7][:, e:e + 1], ALU.add)
                    ts(stk[32:36, cs[c]], R[9][:, cs[c]], -1.0, mc[:, c:c + 1], ALU.mult, ALU.add)
                    ts(stk[96:100, cs[c]], R[8][:, cs[c]], R[9][:, e:e + 1], None, ALU.subtract)
                ts(nmrow[:, :], R[9][:, 0:SEQ], -1.0, None, ALU.mult)
                cp(stk[0:4, :], R[8][:, 0:SEQ])
                stt_(stk[64:68, :], R[7][:, 0:SEQ], -1.0, R[9][:, 0:SEQ], ALU.mult, ALU.subtract)
                tt(exr[:, 0, :], mc[:, 0:NC], R[9][:, CH - 1:SEQ:CH], ALU.subtract)
                tt(smx[:, 0, :], R[6][:, SEQ:T], mm0[:, :], ALU.add)
                tt(smx[:, 1, :], smx[:, 0, :], R0[:, SEQ:T], ALU.max)
                tt(exr[:, 1, :], smx[:, 0, :], smx[:, 1, :], ALU.subtract)
                tt(exr[:, 2, :], R0[:, SEQ:T], smx[:, 1, :], ALU.subtract)
                ts(exr[:, 3, :], smx[:, 1, :], -1.0, None, ALU.mult).then_inc(S["stk_ready"], 1)
                memset(rgx[:, 0:3], 0.0)
                dve.wait_ge(S["spill"], 16 * (l + 1))
                settle(dve)
                with dve.Fori(0, KT // 2) as i:
                    for s in range(2):
                        j = 2 * i + s
                        n = KT * l + j
                        dve.wait_ge(S["evac"], CR + evs(l, RG0 + 3 * j, 2))
                        dve.wait_ge(S["rg_mm"], CR + 3 * n)
                        conv(rgx, rg["xc"], "rg", j, rcs, rcsn, 0).then_inc(S["rg_xc"], 1)
                        dve.wait_ge(S["rg_sig"], CR + n + 1)
                        tt(rg["z"], rg["z"], rg["sz"], ALU.mult)
                        tt(rg["z"], rg["z"], rg["sg"], ALU.mult)
                        dve.wait_ge(S["rg_sq2"], CR + n + 1)
                        stt_(rg["r"], rg["r"], 1.0, rg["t"], ALU.add, ALU.mult).then_inc(S["rg_fac"], 1)
                        tt(rg["i"], rg["i"], rg["xc"], ALU.mult)
                        dve.wait_ge(S["rg_sqrt"], CR + n + 1)
                        tt(rg["i"], rg["i"], rg["t"], ALU.mult)
                        scan(rg["h"][:, 0:SEQ], rg["a"][:, 0:SEQ], rg["i"][:, 0:SEQ], 0.0, ALU.mult, ALU.add)
                        tt(rg["h"][:, SEQ:T].unsqueeze(1), rg["a"][:, SEQ:T].unsqueeze(1), rh0[:, bass.ds(j, 1), :], ALU.mult)
                        tt(rg["h"][:, SEQ:T], rg["h"][:, SEQ:T], rg["i"][:, SEQ:T], ALU.add)
                        cp(rhn[:, bass.ds(j, 1), :], rg["h"][:, SEQ - 1:T].unsqueeze(1))
                        tt(xm[:, bass.ds(j, 1), :], rg["h"].unsqueeze(1), rg["z"].unsqueeze(1), ALU.mult).then_inc(S["rg_y"], 1)

                def chunks(l, h, n8, ml):
                    e = 257 if ml else 256
                    for slot in range(NC + 2):
                        if slot == 7:
                            dve.wait_ge(S["g_sig"], CR + 2 * n8 + 1)
                            tt(tg[0], tg[0], tg[2], ALU.mult)
                            tt(tg[0], tg[0], tg[1], ALU.mult).then_inc(S["g_half"], 1)
                        if slot < NC:
                            c = slot
                            dve.wait_ge(S["kv_out"], CR + 8 * n8 + c + 1)
                            dve.wait_ge(S["ps_mm"], CR + 8 * n8 + c - 1)
                            if c == 0:
                                dve.wait_ge(S["cs_st0"], CD + 32 * n8)
                                dve.wait_ge(S["cs_st1"], CD + 32 * n8)
                                if ml:
                                    memset(vtok[0][:, 256:257], 1.0)
                                    memset(vtok[1][:, 256:257], 1.0)
                            w = ucol[:, c, 3, bass.ds(h, 1)] if ml else rcol[:, bass.ds(4 + h, 1)]
                            ts(vw[c % 2][:, 0:e], vtok[c % 2][:, 0:e], w, None, ALU.mult).then_inc(S["vw_done"], 1)
                            dve.wait_ge(S["st_mm"], CR + 8 * n8 + c + 1)
                            if ml:
                                tt(sd[c % 2], psum[:, ST, 0:CH], dm[:, c * CH:(c + 1) * CH], ALU.mult).then_inc(S["sd_done"], 1)
                            else:
                                tt(sd[c % 2].unsqueeze(1), psum[:, ST, 0:CH].unsqueeze(1), dret[:, bass.ds(h, 1), :],
                                   ALU.mult).then_inc(S["sd_done"], 1)
                        if 1 <= slot <= NC:
                            c = slot - 1
                            dve.wait_ge(S["ps_mm"], CR + 8 * n8 + c + 1)
                            dec = bc[:, bass.ds(h, 1), 0, c] if ml else rcol[:, bass.ds(8 + h, 1)]
                            if ml:
                                stt_(st[:, :, 256], st[:, :, 256], dec, psum[:, PN1, 300:302], ALU.mult, ALU.add)
                                if c == NC - 1:
                                    cp(pn[:, :], st[:, :, 256])
                            stt_(st[:, :, 0:256], st[:, :, 0:256], dec, psum[:, PS, 0:512].rearrange("p (a e) -> p a e", a=2),
                                 ALU.mult, ALU.add).then_inc(S["stt"], 1)
                            dve.wait_ge(S["in_done"], CR + 8 * n8 + c + 1)
                            dve.wait_ge(S["ht_mm"], CR + 8 * n8 + c)
                            tt(hn[:, 0:e], inter[:, 0:e], psum[:, PN1, 0:e], ALU.add).then_inc(S["h_ready"], 1)
                            bn_stats(sm[:, 0:6], hn[:, 0:256])
                            if ml:
                                stt_(sm[:, 10:11], hn[:, 256:257], -1.0, hn[:, 256:257], ALU.mult, ALU.max)
                            bn_aggr(sm[:, 6:8], sm[:, 0:6])
                            if ml:
                                ts(sm[:, 10:11], sm[:, 10:11], ucol[:, c, 2, bass.ds(h, 1)], None, ALU.max)
                                rec(sm[:, 11:12], sm[:, 10:11])
                            if ml:
                                ts(sm[:, 12:13], sm[:, 7:8], sm[:, 11:12], sm[:, 11:12], ALU.mult, ALU.mult)
                                ts(sm[:, 8:9], sm[:, 12:13], EPS, None, ALU.add).then_inc(S["var_ready"], 1)
                            else:
                                ts(sm[:, 8:9], sm[:, 7:8], EPS, None, ALU.add).then_inc(S["var_ready"], 1)
                            dve.wait_ge(S["sq_done"], CR + 8 * n8 + c + 1)
                            rec(sm[:, 13:14], sm[:, 9:10])
                            if ml:
                                tt(sm[:, 14:15], sm[:, 13:14], sm[:, 11:12], ALU.mult)
                            ts(hn[:, 0:256], hn[:, 0:256], sm[:, 6:7], sm[:, 14:15] if ml else sm[:, 13:14],
                               ALU.subtract, ALU.mult).then_inc(S["hn_ready"], 1)
                        if slot >= 2:
                            c = slot - 2
                            dve.wait_ge(S["ht_mm"], CR + 8 * n8 + c + 1)
                            for a in range(2):
                                src = psum[:, ST, (a + 1) * P:(a + 2) * P]
                                dst = vt[:, a, c * CH:(c + 1) * CH]
                                if ml:
                                    o = stt_(dst, src, pcol("ml_gn", 2 * h + a), xc2[:, a, c * CH:(c + 1) * CH], ALU.mult, ALU.add)
                                else:
                                    o = ts(dst, src, pcol("ret_gn", 2 * h + a), None, ALU.mult)
                            o.then_inc(S["ht_done"], 1)

                def samples(l, h, n8, ml):
                    dve.wait_ge(S["ps_mm"], CR + 8 * n8 + 8)
                    for b in range(4):
                        dve.wait_ge(S["vb_mm"], CR + 4 * n8 + b)
                        v4 = qs[:, 2, :, 2 * b:2 * b + 2].rearrange("p a b -> p b a").unsqueeze(3).to_broadcast([P, 2, 2, P])
                        tt(dg.rearrange("p (b a e) -> p b a e", b=2, a=2),
                           ident[:, :].unsqueeze(1).unsqueeze(1).to_broadcast([P, 2, 2, P]), v4, ALU.mult).then_inc(S["dg_done"], 1)
                        dve.wait_ge(S["vb_mm"], CR + 4 * n8 + b + 1)
                        dve.wait_ge(S["cs_dec"], CR + 4 * n8 + b + 1)
                        for e in range(2):
                            for d in range(2):
                                v = cst[b % 2][:, e, d, :]
                                o = stt_(v, psum[:, PN1, 256 * e:256 * e + 256], qs[:, 1, d, 2 * b + e:2 * b + e + 1], v, ALU.mult, ALU.add)
                        o.then_inc(S["cs_new"], 1)
                    dve.wait_ge(S["hs_mm"], CR + 4 * n8 + 4)
                    hs = sm2[:, 1, :]
                    cp(hs, psum[:, PN2, 0:16])
                    hs3 = hs.rearrange("p (a b) -> p a b", a=2)
                    if ml:
                        dve.wait_ge(S["den_mm"], CR + 4 * l + h + 1)
                        cp(sm2[:, 4, 8:16], psum[:, PN1, 0:8])
                        stt_(sm2[:, 4, 0:8], sm2[:, 4, 8:16], -1.0, sm2[:, 4, 8:16], ALU.mult, ALU.max)
                        tt(sm2[:, 4, 0:8].unsqueeze(1), sm2[:, 4, 0:8].unsqueeze(1), bc[:, bass.ds(h, 1), 3, :], ALU.max)
                        rec(sm2[:, 4, 8:16], sm2[:, 4, 0:8])
                        tt(hs3, hs3, sm2[:, 4, 8:16].unsqueeze(1).to_broadcast([P, 2, NB]), ALU.mult)
                    nop().then_inc(S["red_in"], 1)
                    dve.wait_ge(S["red_mm"], CR + 2 * n8 + 1)
                    ts(sm2[:, 5, 0:8], psum[:, PN1, 32:40], 1.0 / DH, None, ALU.mult)
                    tt(hs3, hs3, sm2[:, 5, 0:8].unsqueeze(1).to_broadcast([P, 2, NB]), ALU.subtract)
                    tt(sm2[:, 2, :], hs, hs, ALU.mult).then_inc(S["red_in"], 1)
                    dve.wait_ge(S["red_mm"], CR + 2 * n8 + 2)
                    ts(sm2[:, 3, 0:8], psum[:, PN1, 48:56], 1.0 / DH, EPS, ALU.mult, ALU.add).then_inc(S["red_out"], 1)
                    dve.wait_ge(S["red_sqrt"], CR + n8 + 1)
                    rec(sm2[:, 5, 8:16], sm2[:, 3, 8:16])
                    tt(hs3, hs3, sm2[:, 5, 8:16].unsqueeze(1).to_broadcast([P, 2, NB]), ALU.mult)
                    for a in range(2):
                        if ml:
                            stt_(vt[:, a, SEQ:T], hs[:, 8 * a:8 * a + 8], pcol("ml_gn", 2 * h + a), xc2[:, a, SEQ:T], ALU.mult, ALU.add)
                        else:
                            ts(vt[:, a, SEQ:T], hs[:, 8 * a:8 * a + 8], pcol("ret_gn", 2 * h + a), None, ALU.mult)

                def merge(l, h, n8):
                    dve.wait_ge(S["g_sig"], CR + 2 * n8 + 2)
                    tt(tg[1], tg[1], tg[2], ALU.mult)
                    tt(vt[:, 0, :], vt[:, 0, :], tg[0], ALU.mult)
                    tt(tg[1], tg[1], qt[:, 0, :], ALU.mult)
                    tt(vt[:, 1, :], vt[:, 1, :], tg[1], ALU.mult)
                    x2 = xm[:, bass.ds(2 * h, 2), :]
                    tt(x2, x2, vt, ALU.add).then_inc(S["br_done"], 1)

                settle(dve)
                with dve.Fori(0, HEADS) as h:
                    n8 = 8 * l + h
                    t0 = RET0 + 10 * h
                    dve.wait_ge(S["rope_in"], 16 * (l + 1))
                    dve.wait_ge(S["st_out"], CD + 48 * n8)
                    for q, x in ((1, qt), (3, kt)):
                        dve.wait_ge(S["evac"], CR + evs(l, t0 + q, 2))
                        tt(tg[0], x[:, 0, :], rope[:, 0, :], ALU.mult)
                        tt(tg[1], x[:, 1, :], rope[:, 1, :], ALU.mult)
                        tt(x[:, 0, :], x[:, 0, :], rope[:, 1, :], ALU.mult)
                        tt(x[:, 1, :], x[:, 1, :], rope[:, 0, :], ALU.mult)
                        tt(x[:, 1, :], x[:, 0, :], x[:, 1, :], ALU.add)
                        tt(x[:, 0, :], tg[0], tg[1], ALU.subtract)
                    cp(qs[:, 0, :, :], qt[:, :, SEQ:T])
                    cp(qs[:, 1, :, :], kt[:, :, SEQ:T])
                    dve.wait_ge(S["evac"], CR + evs(l, t0 + 5, 2))
                    cp(qs[:, 2, :, :], vt[:, :, SEQ:T])
                    memset(st, 0.0).then_inc(S["stt"], 1)
                    nop().then_inc(S["rope_done"], 1)
                    chunks(l, h, n8, False)
                    samples(l, h, n8, False)
                    merge(l, h, n8)
                settle(dve)
                with dve.Fori(0, HEADS) as h:
                    n8 = 8 * l + 4 + h
                    hh = 4 * l + h
                    dve.wait_ge(S["st_out"], CD + 48 * n8)
                    cp(selh[:, :], sel[:, bass.ds(h * P, P)]).then_inc(S["selh"], 1)
                    dve.wait_ge(S["vs_out"], CR + hh + 1)
                    cp(qs[:, 0, :, :], qt[:, :, SEQ:T])
                    cp(qs[:, 1, :, :], kt[:, :, SEQ:T])
                    nn3 = sm2[:, 6, :].rearrange("p (a b) -> p a b", a=2)
                    d8 = bc[:, bass.ds(h, 1), 1, :].to_broadcast([P, 2, NB])
                    w8 = bc[:, bass.ds(h, 1), 2, :].to_broadcast([P, 2, NB])
                    tt(mnn[:, :, :], mn0[:, bass.ds(h, 1), :, :].rearrange("p o a b -> p (o a) b"), d8, ALU.mult)
                    tt(nn3, qs[:, 1, :, :], w8, ALU.mult)
                    tt(qs[:, 2, :, :], qs[:, 2, :, :], w8, ALU.mult)
                    tt(mnn[:, :, :], mnn[:, :, :], nn3, ALU.add)
                    tt(nn3, mnn[:, :, :], qs[:, 0, :, :], ALU.mult).then_inc(S["n_out"], 1)
                    dve.wait_ge(S["dm_mm"], CR + hh + 1)
                    for c in range(NC):
                        o = ts(dm[:, c * CH:(c + 1) * CH], psum[:, TK + c // 4, (c % 4) * CH:(c % 4 + 1) * CH],
                               ucol[:, c, 0, bass.ds(h, 1)], 0.0, ALU.add, ALU.min)
                    o.then_inc(S["dm_arg"], 1)
                    memset(st, 0.0).then_inc(S["stt"], 1)
                    dve.wait_ge(S["dm_exp"], CR + hh + 1)
                    d3 = dm.rearrange("p (c t) -> p c t", c=NC)
                    tt(d3, d3, mask[:, :].unsqueeze(1).to_broadcast([P, NC, CH]), ALU.mult)
                    nop().then_inc(S["rope_done"], 1)
                    chunks(l, h, n8, True)
                    samples(l, h, n8, True)
                    merge(l, h, n8)
                for k in range(KT):
                    dve.wait_ge(S["uH_ready"], CR + 2 * KT * l + KT + k + 1)
                    tt(uL[:, k, :], xm[:, k, :], uH[:, k, :].bitcast(F32), ALU.subtract).then_inc(S["plane_ready"], 1)
                dve.wait_ge(S["osq_used"], CR + KT * (l + 1))
                ts(rs.rearrange("p (g t) -> p g t", g=NG), psum[:, ST:ST + NG, 0:GW], 1.0 / D, EPS, ALU.mult, ALU.add).then_inc(S["ors_var"], 1)
                dve.wait_ge(S["ors_sqrt"], CR + l + 1)
                rec(rs, rs)
                for k in range(KT):
                    x = xm[:, k, :]
                    dve.wait_ge(S[f"xt_in{k % 2}"], 64 * l + 16 * (k // 2) + 16)
                    tt(x, x, rs, ALU.mult)
                    stt_(x[:, 0:SEQ], x[:, 0:SEQ], gpo[:, k, 0:1], xt[k % 2][:, 0:SEQ], ALU.mult, ALU.add)
                    tt(x[:, SEQ:T], x[:, SEQ:T], gpo[:, k, 1:9], ALU.mult)
                    tt(x[:, SEQ:T], x[:, SEQ:T], xt[k % 2][:, SEQ:T], ALU.add).then_inc(S["xnew"], 1)
                nop().then_inc(S["ldone"], 1)


_OUTS = {
    "y": (KT, P, T), "rg_h": (DEPTH, P, KT, 9), "p_conv": (DEPTH, P, 2, KT, 3), "p_C": (DEPTH, HEADS, P, 2, DH),
    "p_n": (DEPTH, HEADS, P, 2), "p_m": (DEPTH, 4, 1), "p_S": (DEPTH, HEADS, P, 2, DH),
    "s_rconv": (DEPTH, P, KT, 3, NB), "s_C": (DEPTH, HEADS, P, NB, 2, DH), "s_n": (DEPTH, HEADS, P, 2, NB),
    "s_m": (DEPTH, 4, NB), "s_mconv": (DEPTH, P, KT, 3, NB), "s_S": (DEPTH, HEADS, P, NB, 2, DH),
}
_SCRATCH = {"xkeep": (P, KT, T), "xml_d": (KT, P, T), "xc_d": (KT, P, T)}


def tables():
    f = np.float32
    t = {"ident": np.eye(P, dtype=f), "ones": np.ones((P, P), f), "mask": np.triu(np.ones((P, P), f))}
    sel = np.zeros((4, 4, P), f)
    for h in range(4):
        sel[h, h] = 1.0
    t["sel"] = sel.reshape(4, 4 * P)
    lg = np.log1p(-np.exp2(-5.0 - np.arange(HEADS, dtype=f))).astype(f)
    i = np.arange(CH, dtype=f)
    rel = i[None, :] - i[:, None]
    t["dret"] = np.ascontiguousarray(np.where(rel[:, None, :] >= 0, np.exp(np.maximum(rel, 0)[:, None, :] * lg[None, :, None]), 0).astype(f))
    rc = np.zeros((P, 16), f)
    rc[:, 0:4] = np.exp((i + 1)[:, None] * lg)
    rc[:, 4:8] = np.exp((CH - 1 - i)[:, None] * lg)
    rc[:, 8:12] = np.exp(CH * lg)
    rc[:, 12:16] = np.exp(lg)
    t["rcol"] = rc
    half = DH // 2
    step = np.arange(half, dtype=f) / f(half - 1)
    inv = np.power(f(10000.0), -step, dtype=f)
    pos = np.concatenate([np.arange(SEQ, dtype=f), np.full(NB, PAST, f)])
    ang = (inv[:, None] * pos[None, :]).astype(f)
    t["rope"] = np.ascontiguousarray(np.stack([np.cos(ang), np.sin(ang)], 1).astype(f))
    return t


def layouts(a):
    c = np.ascontiguousarray
    chan = lambda x: c(np.moveaxis(x.reshape(x.shape[:-1] + (KT, P)), -1, 1))
    tiles = lambda w: w.reshape(DEPTH, KT, P, -1, P).transpose(0, 3, 2, 1, 4)
    win = tiles(a["w_in"])[:, weight_order()]
    wall = np.concatenate([tiles(a["w_ada"]), win, tiles(a["w_out"])], 1).reshape(DEPTH * NT, P, KT * P)
    b_ada = a["b_ada"].reshape(DEPTH, NADA, P).transpose(0, 2, 1)
    par = np.concatenate([b_ada if n == "b_ada" else chan(a[n]).reshape(DEPTH, P, -1) for n in PAR], 2)
    o = dict(tables())
    o["xp"] = c(a["x_prompt"][0].T.reshape(KT, P, SEQ))
    o["xs"] = c(a["x_sample"][:, 0].T.reshape(KT, P, NB))
    cT = np.zeros((P, KT, 10), np.float32)
    cT[:, :, 0] = a["c_prompt"][0].reshape(KT, P).T
    cT[:, :, 1:9] = a["c_sample"].reshape(NB, KT, P).transpose(2, 1, 0)
    o["cT"] = cT
    o["wall"] = c(wall)
    o["par"] = c(par)
    o["wif"] = c(a["ml_w_if"].reshape(DEPTH, 24, P, 8).transpose(0, 2, 1, 3))
    bif = np.zeros((DEPTH, HCOL, 1), np.float32)
    bif[:, 0:4, 0], bif[:, 32:36, 0] = a["ml_b_if"][:, 0:4], a["ml_b_if"][:, 4:8]
    o["bif"] = bif
    conv = lambda x: c(x.reshape(DEPTH, NB, 3, KT, P).transpose(0, 4, 3, 2, 1))
    o["rcs"], o["mcs"] = conv(a["state_rg_conv"]), conv(a["state_ml_conv"])
    o["rh0"] = c(a["state_rg_h"].reshape(DEPTH, NB, KT, P).transpose(0, 3, 2, 1))
    o["mn0"] = c(a["state_ml_n"].reshape(DEPTH, NB, HEADS, 2, P).transpose(0, 4, 2, 3, 1))
    o["mm0"] = c(a["state_ml_m"].transpose(0, 2, 1))
    mat = lambda x: c(x.reshape(DEPTH, NB, HEADS, 2, P, DH).transpose(0, 2, 4, 1, 3, 5))
    o["ml_C"], o["ret_S"] = mat(a["state_ml_C"]), mat(a["state_ret_S"])
    qkv = np.stack([a["ml_w_q"], a["ml_w_k"], a["ml_w_v"]], 2)
    o["wqkvT"] = c(qkv.reshape(DEPTH, HEADS, 3, DH, 2, P).transpose(0, 1, 5, 2, 4, 3).reshape(DEPTH, HEADS, P, 1536))
    nat = qkv.reshape(DEPTH, HEADS, 3, 2, P, DH).transpose(0, 1, 4, 2, 3, 5)
    o["wqk"] = c(nat[:, :, :, 0:2].reshape(DEPTH, HEADS, P, 1024))
    o["wv"] = c(nat[:, :, :, 2].reshape(DEPTH, HEADS, P, 512))
    o["rgw"] = c(np.stack([a["rg_w_a"], a["rg_w_x"]], 3).reshape(DEPTH, KT, P, 2 * P))
    return o


def kernel(**inputs):
    import concourse.bacc as bacc
    from concourse.bass_utils import run_bass_kernel_spmd as run

    arrays = layouts({k: np.asarray(v) for k, v in inputs.items()})
    nc = bacc.Bacc("TRN2", target_bir_lowering=False, num_devices=1)
    io = {n: nc.dram_tensor("in_" + n, x.shape, mybir.dt.from_np(x.dtype), kind="ExternalInput").ap() for n, x in arrays.items()}
    io |= {n: nc.dram_tensor("out_" + n, s, F32, kind="ExternalOutput").ap() for n, s in _OUTS.items()}
    io |= {n: nc.dram_tensor("tmp_" + n, s, F32, kind="Internal").ap() for n, s in _SCRATCH.items()}
    build(nc, io)
    r = run(nc, [{"in_" + n: x for n, x in arrays.items()}], core_ids=[0]).results[0]
    g = {n: r["out_" + n] for n in _OUTS}
    c = np.ascontiguousarray
    y = g["y"].reshape(D, T)
    rgh = g["rg_h"].transpose(0, 3, 2, 1).reshape(DEPTH, 9, D)
    pconv = g["p_conv"].transpose(0, 2, 4, 3, 1).reshape(DEPTH, 2, 1, 3, D)
    sconv = lambda x: c(x.transpose(0, 4, 3, 2, 1).reshape(DEPTH, NB, 3, D))
    pmat = lambda x: c(x.transpose(0, 1, 3, 2, 4).reshape(DEPTH, 1, HEADS, DH, DH))
    smat = lambda x: c(x.transpose(0, 3, 1, 4, 2, 5).reshape(DEPTH, NB, HEADS, DH, DH))
    return (c(y[:, :SEQ].T)[None], c(y[:, SEQ:].T)[:, None],
            c(rgh[:, 0:1]), c(pconv[:, 0]), pmat(g["p_C"]), c(g["p_n"].transpose(0, 1, 3, 2).reshape(DEPTH, 1, HEADS, DH)),
            c(g["p_m"].reshape(DEPTH, 1, HEADS)), c(pconv[:, 1]), pmat(g["p_S"]),
            c(rgh[:, 1:9]), sconv(g["s_rconv"]), smat(g["s_C"]), c(g["s_n"].transpose(0, 4, 1, 3, 2).reshape(DEPTH, NB, HEADS, DH)),
            c(g["s_m"].transpose(0, 2, 1)), sconv(g["s_mconv"]), smat(g["s_S"]))
```

```python
from contextlib import ExitStack

import numpy as np

import concourse.bass as bass
from concourse import mybir

F32 = mybir.dt.float32
F32R = mybir.dt.float32r
ACT = mybir.ActivationFunctionType
ALU = mybir.AluOpType

P = 128
DEPTH, D, SEQ, NB = 2, 1024, 1024, 8
T = SEQ + NB
KT = D // P
NG, GW = 3, T // 3
HEADS, DH, CONV = 4, 256, 4
CH, NC = 128, SEQ // 128
EPS = 1e-6
RG_C = 8.0
PAST = 8192
NADA, NIN, NOUT = 3 * KT, 11 * KT, KT
NT = NADA + NIN + NOUT
XML0, RG0, RET0, ML0, OUT0 = 24, 32, 56, 96, 112
HCOL = 36
LOG1P_TERMS = [1.0 / n for n in (15, 13, 11, 9, 7, 5, 3)]

PAR = {}
_o = 0
for _n, _w in (("b_ada", 24), ("norm_pre", 8), ("norm_post", 8), ("rg_conv_w", 32), ("rg_conv_b", 8),
               ("rg_b_a", 8), ("rg_b_x", 8), ("rg_lambda", 8), ("ml_conv_w", 32), ("ml_conv_b", 8),
               ("ml_skip", 8), ("ml_gn", 8), ("ret_gn", 8)):
    PAR[_n] = (_o, _w)
    _o += _w
NPAR = _o

CR, CD = 8, 64
DMA_CREDIT = ("xsp0", "xsp1", "cs_st0", "cs_st1", "st_out")
N_PROJ = 3 * (NIN + NOUT)


def weight_order():
    xrg, zrg, xml, zml, q, k, v, g, ga, gb, gc = (range(8 * i, 8 * i + 8) for i in range(11))
    order = list(xml)
    for j in range(8):
        order += [xrg[j], zrg[j], ga[j]]
    for h in range(4):
        a, b = 2 * h, 2 * h + 1
        order += [q[a], q[b], k[a], k[b], v[a], v[b], g[a], gc[a], g[b], gc[b]]
    for h in range(4):
        a, b = 2 * h, 2 * h + 1
        order += [zml[a], gb[a], zml[b], gb[b]]
    return order


def build(nc, io):
    with ExitStack() as ctx:
        def sb(name, shape, dt=F32):
            return ctx.enter_context(nc.sbuf_tensor(name, shape, dt))

        def sem(name):
            return ctx.enter_context(nc.semaphore(name))

        ident = sb("ident", [P, P])
        ones = sb("ones", [P, P])
        mask = sb("mask", [P, P])
        dret = sb("dret", [P, 4, P])
        rcol = sb("rcol", [P, 16])
        uH = sb("uH", [P, KT, T], F32R)
        uL = sb("uL", [P, KT, T], F32R)
        xm = sb("xm", [P, KT, T])
        wraw = [sb(f"wraw{s}", [P, KT * P]) for s in range(2)]
        wH = [sb(f"wH{s}", [P, KT, P], F32R) for s in range(2)]
        wL = [sb(f"wL{s}", [P, KT, P], F32R) for s in range(2)]
        par = sb("par", [P, NPAR])
        wif = sb("wif", [P, 24, 8])
        cT = sb("cT", [P, KT, 10])
        cH = sb("cH", [P, KT, 10], F32R)
        cL = sb("cL", [P, KT, 10], F32R)
        ada = sb("ada", [P, NADA, 10])
        s1 = sb("s1", [P, KT, 10])
        gpo = sb("gpo", [P, KT, 10])
        nsp = sb("nsp", [P, 2, KT])
        rcs = sb("rcs", [P, KT, 3, NB])
        mcs = sb("mcs", [P, KT, 3, NB])
        rcsn = sb("rcsn", [P, KT, 3, NB])
        mcsn = sb("mcsn", [P, KT, 3, NB])
        pcn = sb("pcn", [P, 2, KT, 3])
        rh0 = sb("rh0", [P, KT, NB])
        rhn = sb("rhn", [P, KT, 9])
        mn0 = sb("mn0", [P, HEADS, 2, NB])
        mnn = sb("mnn", [P, 2, NB])
        mm0 = sb("mm0", [4, NB])
        pn = sb("pn", [P, 2])
        mc = sb("mc", [4, 10])
        mcols = sb("mcols", [4, 3, NC])
        exr = sb("exr", [4, 4, NB])
        smx = sb("smx", [4, 4, NB])
        ucol = sb("ucol", [P, NC, 4, 4])
        bc = sb("bc", [P, 4, 4, NB])
        nmrow = sb("nmrow", [4, SEQ])
        selh = sb("selh", [4, P])
        fj = [sb(f"fj{s}", [P, 2, HCOL]) for s in range(2)]
        zf = sb("zf", [P, HCOL])
        bifp = sb("bifp", [HCOL, 1])
        qs = sb("qs", [P, 3, 2, NB])
        sm = sb("sm", [P, 64])
        sm2 = sb("sm2", [P, 8, 16])
        cst = [sb(f"cst{s}", [P, 2, DH]) for s in range(2)]
        dg = sb("dg", [P, DH])
        W_SIZE = 15720
        work = sb("work", [P, W_SIZE])

        def wv(off, n):
            assert off + n <= W_SIZE
            return work[:, off:off + n]

        tmp_n = [wv(T * i, T) for i in range(2)]
        sq = [wv(T * (2 + i), T) for i in range(2)]
        rs = wv(T * 4, T)
        xt = [wv(T * (5 + i), T) for i in range(2)]
        wt = [wv(12000 + 1536 * i, 1536).rearrange("p (m j i) -> p m j i", m=3, j=2) for i in range(2)]
        xj = [wv(1036 * i, 1035) for i in range(2)]
        yj = [wv(2072 + T * i, T) for i in range(2)]
        sg = [wv(2072 + T * (2 + i), T) for i in range(2)]
        fold = wv(11000, 576).rearrange("p (m k c) -> p m k c", m=2, k=KT)
        row = [work[0:4, T * i:T * i + T] for i in range(12)]
        stk = wv(T * 12, SEQ)
        rgx = wv(0, 1035)
        rg = {n: wv(1036 + T * i, T) for i, n in enumerate(("xc", "r", "i", "a", "t", "z", "sz", "sg", "h"))}
        rgw = [wv(14500 + 256 * i, 256).rearrange("p (m j) -> p m j", m=2) for i in range(2)]
        qt = wv(0, 2 * T).rearrange("p (a t) -> p a t", a=2)
        kt = wv(2 * T, 2 * T).rearrange("p (a t) -> p a t", a=2)
        vt = wv(4 * T, 2 * T).rearrange("p (a t) -> p a t", a=2)
        tg = [wv((6 + i) * T, T) for i in range(3)]
        tg01 = wv(6 * T, 2 * T).rearrange("p (a t) -> p a t", a=2)
        rope = wv(9 * T, 2 * T).rearrange("p (a t) -> p a t", a=2)
        xc2 = wv(9 * T, 2 * T).rearrange("p (a t) -> p a t", a=2)
        dm = wv(11 * T, SEQ)
        B0 = 12 * T
        st = wv(B0, 514).rearrange("p (a e) -> p a e", a=2)
        wvv = wv(B0 + 514, 512).rearrange("p (i e) -> p i e", i=2)
        B1 = B0 + 514 + 512
        ktok = [wv(B1 + 256 * i, 256) for i in range(2)]
        vtok = [wv(B1 + 512 + 257 * i, 257) for i in range(2)]
        vw = [wv(B1 + 1026 + 257 * i, 257) for i in range(2)]
        sd = [wv(B1 + 1540 + 128 * i, 128) for i in range(2)]
        inter = wv(B1 + 1796, 257)
        hn = wv(B1 + 2053, 257)
        wqk = wv(B1, 1024).rearrange("p (m i j) -> p m i j", m=2, i=2)
        rtmp = [wv(B1 + T * i, T) for i in range(2)]

        psum = ctx.enter_context(nc.psum_tensor("psum", [P, 8, 512], F32))
        TK, ST, PN1, PN2, PS = 3, 4, 5, 6, 7

        own = {
            "pe": "mm sq_used ab_mm gp_done tr_mm bc_mm rg_mm kv_mm st_mm num_mm ps_mm ht_mm qk_mm dm_mm vs_mm "
                  "vb_mm hs_mm red_mm osq_used",
            "act": "evac cH_done ada_out sqr rs_sqrt uH_ready wif_ready ab_out sig_done rows_in row_exp lam_exp "
                   "tr_out exr_exp bc_out rg_sig rg_ev rg_sq2 rg_sqrt kv_out in_done qk_ev vs_out "
                   "dm_exp cs_dec sq_done red_sqrt osq ors_sqrt",
            "dve": "cL_done ada_ready rs_var tmp_ready plane_ready zeroed xj_pad conv_done xc_ready row_abs lam_abs "
                   "stk_ready rg_xc rg_fac rg_y rope_done stt vw_done sd_done h_ready var_ready hn_ready ht_done "
                   "fold_zero g_mul br_done selh dm_arg dm_done dg_done cs_new red_in red_out ors_var xnew ldone",
            "pool": "hi_done split",
            "sp": "xsp0 xsp1 cs_st0 cs_st1 st_out sdone",
        }
        S = {n: sem(n) for names in own.values() for n in names.split()}
        for n in "settled const_in x_in par_in wraw0 wraw1 wt_in0 wt_in1 rgw_in0 rgw_in1 rope_in ml_in cs_in0 cs_in1 xt_in0 xt_in1 spill out_st".split():
            S[n] = sem(n)

        def open_balance(eng, who):
            for n in own[who].split():
                eng.sem_inc(S[n], CD if n in DMA_CREDIT else CR)

        def settle(eng):
            eng.sem_inc(S["settled"], 1)

        def pcol(name, i, n=1):
            return par[:, bass.ds(PAR[name][0] + i, n)]

        def tok(ap, g):
            return ap[:, g * GW:(g + 1) * GW]

        def evs(l, t, g):
            return l * N_PROJ + 3 * (t - NADA) + g + 1

        def mms(l, t, g):
            return (l * NT + t) * 3 + g + 1

        block = ctx.enter_context(nc.Block())

        def load_state(sp, n8, b):
            sp.wait_ge(S[f"cs_st{b % 2}"], CD + 64 * n8 + 16 * (b // 2))
            settle(sp)
            sp.wait_ge(S["hs_mm"], CR + 8 * n8 + b - 1)
            settle(sp)
            sp.dma_start(cst[b % 2][:, :, :], io["st_in"][n8, :, b]).then_inc(S[f"cs_in{b % 2}"], 16)

        @block.sync
        def _(sp):
            open_balance(sp, "sp")
            for dst, name in ((ident, "ident"), (ones, "ones"), (mask, "mask"), (rcol, "rcol"),
                              (cT, "cT")):
                sp.dma_start(dst[:], io[name]).then_inc(S["const_in"], 16)
            sp.dma_start(dret[:, :, :], io["dret"]).then_inc(S["const_in"], 16)
            for k in range(KT):
                sp.dma_start(xm[:, k, 0:SEQ], io["xp"][k]).then_inc(S["x_in"], 16)
                sp.dma_start(xm[:, k, SEQ:T], io["xs"][k]).then_inc(S["x_in"], 16)
            sp.wait_ge(S["x_in"], 32 * KT)
            with sp.Fori(0, DEPTH) as l:
                sp.wait_ge(S["ldone"], CR + l)
                for dst, name in ((par, "par"), (wif, "wif"), (rcs, "rcs"), (mcs, "mcs"), (rh0, "rh0"),
                                  (mn0, "mn0"), (mm0, "mm0"), (bifp, "bif")):
                    sp.dma_start(dst[:], io[name][l]).then_inc(S["par_in"], 16)
                sp.dma_start(io["xkeep"], xm[:, :, :]).then_inc(S["spill"], 16)
                for h in range(HEADS):
                    sp.wait_ge(S["ab_mm"], CR + 4 * l + h - 1)
                    sp.dma_start(wt[h % 2].rearrange("p m j i -> p (m j i)"), io["wqkvT"][l, h]).then_inc(S[f"wt_in{h % 2}"], 16)
                with sp.Fori(0, KT // 2) as i:
                    for s in range(2):
                        j = 2 * i + s
                        sp.wait_ge(S["evac"], CR + evs(l, XML0 + j, 2))
                        sp.dma_start(io["xml_d"][j], xj[s][:, 3:3 + T]).then_inc(S[f"xsp{s}"], 16)
                        sp.wait_ge(S["xc_ready"], CR + KT * l + j + 1)
                        sp.dma_start(io["xc_d"][j], yj[s]).then_inc(S[f"xsp{s}"], 16)
                sp.wait_ge(S["stk_ready"], CR + l + 1)
                settle(sp)
                sp.dma_start(io["p_m"][l], mc[:, NC:NC + 1]).then_inc(S["out_st"], 16)
                sp.dma_start(io["s_m"][l], smx[:, 1, :]).then_inc(S["out_st"], 16)
                sp.dma_start(io["s_mconv"][l], mcsn[:, :, :, :]).then_inc(S["out_st"], 16)
                with sp.Fori(0, KT // 2) as i:
                    for s in range(2):
                        j = 2 * i + s
                        sp.wait_ge(S["rg_mm"], CR + 3 * (KT * l + j - 1))
                        sp.dma_start(rgw[s].rearrange("p m j -> p (m j)"), io["rgw"][l, j]).then_inc(S[f"rgw_in{s}"], 16)
                sp.wait_ge(S["rg_y"], CR + KT * l + KT)
                sp.dma_start(rope[:, :, :], io["rope"]).then_inc(S["rope_in"], 16)
                sp.dma_start(io["rg_h"][l], rhn[:, :, :]).then_inc(S["out_st"], 16)
                sp.dma_start(io["s_rconv"][l], rcsn[:, :, :, :]).then_inc(S["out_st"], 16)
                sp.dma_start(io["p_conv"][l], pcn[:, :, :, :]).then_inc(S["out_st"], 16)
                for ml in (False, True):
                    with sp.Fori(0, HEADS) as h:
                        n8 = 8 * l + 4 * ml + h
                        for b in range(2):
                            load_state(sp, n8, b)
                        if ml:
                            sp.wait_ge(S["br_done"], CR + n8)
                            sp.wait_ge(S["xsp0"], CD + 128 * (l + 1))
                            sp.wait_ge(S["xsp1"], CD + 128 * (l + 1))
                            settle(sp)
                            for a in range(2):
                                sp.dma_start(vt[:, a, :], io["xml_d"][2 * h + a]).then_inc(S["ml_in"], 16)
                                sp.dma_start(xc2[:, a, :], io["xc_d"][2 * h + a]).then_inc(S["ml_in"], 16)
                            sp.dma_start(wqk.rearrange("p m i j -> p (m i j)"), io["wqk"][l, h]).then_inc(S["ml_in"], 16)
                            sp.dma_start(wvv.rearrange("p i e -> p (i e)"), io["wv"][l, h]).then_inc(S["ml_in"], 16)
                        for b in range(NB):
                            sp.wait_ge(S["cs_new"], CR + 8 * n8 + b + 1)
                            settle(sp)
                            sp.dma_start(io["s_st"][n8, :, b], cst[b % 2][:, :, :]).then_inc(S[f"cs_st{b % 2}"], 16)
                            if b + 2 < NB:
                                load_state(sp, n8, b + 2)
                        sp.wait_ge(S["stt"], CR + 9 * n8 + 9)
                        settle(sp)
                        sp.dma_start(io["p_st"][n8], st[:, :, 0:256]).then_inc(S["st_out"], 16)
                        if ml:
                            sp.dma_start(io["p_n"][l, h], pn[:, :]).then_inc(S["st_out"], 16)
                            sp.dma_start(io["s_n"][l, h], mnn[:, :, :]).then_inc(S["st_out"], 16)
                        else:
                            sp.sem_inc(S["st_out"], 32)
                for k in range(KT):
                    if k >= 2:
                        sp.wait_ge(S["xnew"], CR + KT * l + k - 1)
                    else:
                        sp.wait_ge(S["br_done"], CR + 8 * l + 8)
                        sp.wait_ge(S["spill"], 16 * (l + 1))
                    sp.dma_start(xt[k % 2], io["xkeep"][:, k, :]).then_inc(S[f"xt_in{k % 2}"], 16)
                sp.wait_ge(S["out_st"], 96 * (l + 1))
                sp.wait_ge(S["st_out"], CD + 48 * 8 * (l + 1))
                for s in range(2):
                    sp.wait_ge(S[f"cs_st{s}"], CD + 64 * 8 * (l + 1))
                sp.sem_inc(S["sdone"], 1)
            sp.wait_ge(S["ldone"], CR + DEPTH)
            for k in range(KT):
                sp.dma_start(io["y"][k], xm[:, k, :]).then_inc(S["x_in"], 16)
            sp.wait_ge(S["x_in"], 48 * KT)

        @block.gpsimd
        def _(pool):
            open_balance(pool, "pool")
            for s in range(2):
                pool.dma_start(wraw[s][:, :], io["wall"][s]).then_inc(S[f"wraw{s}"], 16)

            def split_pair(i, more):
                for s in range(2):
                    t = 2 * i + s
                    pool.wait_ge(S[f"wraw{s}"], 16 * i + 16)
                    pool.wait_ge(S["mm"], CR + 3 * t - 3)
                    raw = wraw[s][:, :].rearrange("p (k m) -> p k m", k=KT)
                    settle(pool)
                    pool.tensor_scalar(wH[s][:, :, :], raw, 1.0, 1.0, ALU.mult, ALU.mult).then_inc(S["hi_done"], 1)
                    pool.wait_ge(S["hi_done"], CR + t + 1)
                    pool.tensor_tensor(wL[s][:, :, :], raw, wH[s][:, :, :].bitcast(F32), ALU.subtract).then_inc(S["split"], 1)
                    if more:
                        pool.wait_ge(S["split"], CR + t + 1)
                        pool.dma_start(wraw[s][:, :], io["wall"][t + 2]).then_inc(S[f"wraw{s}"], 16)

            with pool.Fori(0, DEPTH * NT // 2 - 1) as i:
                split_pair(i, True)
            split_pair(DEPTH * NT // 2 - 1, False)

        @block.tensor
        def _(pe):
            open_balance(pe, "pe")

            def proj_group(l, t, s, g, hi=uH, lo=uL, bank=None, lag=3):
                if g == 0:
                    pe.wait_ge(S["split"], CR + l * NT + t + 1)
                pe.wait_ge(S["evac"], CR + evs(l, t, g) - lag)
                for k in range(KT):
                    for n, (w, x) in enumerate(((wH, hi), (wL, hi), (wH, lo))):
                        mm = pe.matmul(psum[:, g if bank is None else bank, 0:GW], w[s][:, k, :], x[:, k, g * GW:(g + 1) * GW],
                                       start=(k == 0 and n == 0), stop=(k == KT - 1 and n == 2))
                mm.then_inc(S["mm"], 1)

            def proj(l, t, s, lag=3):
                for g in range(NG):
                    proj_group(l, t, s, g, lag=lag)

            def gate_group(l, t0, n):
                proj_group(l, t0 + n // 3, (n // 3) % 2, n % 3, bank=n % 2, lag=2)

            pe.wait_ge(S["const_in"], 96)
            pe.wait_ge(S["cL_done"], CR + 1)
            pe.wait_ge(S["zeroed"], CR + 1)
            settle(pe)
            with pe.Fori(0, DEPTH) as l:
                for k in range(KT):
                    pe.wait_ge(S["sqr"], CR + KT * l + k + 1)
                    for g in range(NG):
                        mm = pe.matmul(psum[:, g, 0:GW], ones[:, :], tok(sq[k % 2], g), start=(k == 0), stop=(k == KT - 1))
                    mm.then_inc(S["sq_used"], 1)
                settle(pe)
                with pe.Fori(0, NADA // 2) as i:
                    for s in range(2):
                        pe.wait_ge(S["split"], CR + l * NT + 2 * i + s + 1)
                        if s == 0:
                            pe.wait_ge(S["ada_out"], CR + NADA // 2 * l + i)
                        for k in range(KT):
                            for n, (w, x) in enumerate(((wH, cH), (wL, cH), (wH, cL))):
                                mm = pe.matmul(psum[:, TK, 10 * s:10 * s + 10], w[s][:, k, :], x[:, k, :],
                                               start=(k == 0 and n == 0), stop=(k == KT - 1 and n == 2))
                            if k in (2, 5, 7):
                                mm.then_inc(S["mm"], 1)
                pe.wait_ge(S["wif_ready"], CR + l + 1)
                for h in range(HEADS):
                    pe.wait_ge(S[f"wt_in{h % 2}"], 32 * l + 16 * (h // 2) + 16)
                    pe.wait_ge(S["ab_out"], CR + 4 * l + h)
                    if h == 0:
                        pe.wait_ge(S["ada_out"], CR + NADA // 2 * (l + 1))
                    for i in range(2):
                        for n in range(6):
                            m, jj = n // 2, n % 2
                            c = (m // 2) * 16 + i * 8
                            mm = pe.matmul(psum[:, TK, c:c + 8], wt[h % 2][:, m, jj, i * P:(i + 1) * P],
                                           wif[:, 8 * m + 2 * h + jj, :], start=(n in (0, 4)), stop=(n in (3, 5)))
                    mm.then_inc(S["ab_mm"], 1)
                for g in range(NG):
                    pe.matmul(psum[0:HCOL, ST + g, 0:GW], zf[:, :], ones[:, 0:1].to_broadcast([P, GW]), start=True,
                              stop=False, skip_group_check=True)
                pe.wait_ge(S["plane_ready"], CR + 2 * KT * l + KT)
                settle(pe)
                with pe.Fori(0, KT // 2) as i:
                    for s in range(2):
                        proj(l, XML0 + 2 * i + s, s)
                    for s in range(2):
                        pe.wait_ge(S["xc_ready"], CR + KT * l + 2 * i + s + 1)
                        for g in range(NG):
                            pe.matmul(psum[0:HCOL, ST + g, 0:GW], fj[s][:, 0, :], tok(yj[s], g), start=False, stop=False,
                                      skip_group_check=True)
                            mm = pe.matmul(psum[0:HCOL, ST + g, 0:GW], fj[s][:, 1, :], xj[s][:, 3 + g * GW:3 + (g + 1) * GW],
                                           start=False, stop=True, skip_group_check=True)
                        mm.then_inc(S["gp_done"], 1)
                settle(pe)
                with pe.Fori(0, KT // 2) as i:
                    for s in range(2):
                        for m in range(3):
                            proj(l, RG0 + 6 * i + 3 * s + m, (3 * s + m) % 2)
                        n = KT * l + 2 * i + s
                        pe.wait_ge(S["rg_xc"], CR + n + 1)
                        pe.wait_ge(S[f"rgw_in{s}"], 64 * l + 16 * i + 16)
                        if s == 0:
                            pe.wait_ge(S["rows_in"], CR + l + 1)
                        for g in range(NG):
                            pe.wait_ge(S["rg_ev"], CR + 6 * n + (2 if g == 2 else 0))
                            for m in range(2):
                                mm = pe.matmul(psum[:, TK + 2 * m + g % 2, 0:GW], rgw[s][:, m, :], tok(rg["xc"], g),
                                               start=True, stop=True)
                            mm.then_inc(S["rg_mm"], 1)
                pe.wait_ge(S["rg_ev"], CR + 6 * KT * (l + 1))
                pe.wait_ge(S["stk_ready"], CR + l + 1)
                for a in range(2):
                    pe.wait_ge(S["tr_out"], CR + 2 * l + a)
                    for c in range(4):
                        mm = pe.transpose(psum[:, TK, c * P:c * P + 100], stk[0:100, (4 * a + c) * P:(4 * a + c + 1) * P],
                                          ident[0:100, 0:100])
                    mm.then_inc(S["tr_mm"], 1)
                pe.wait_ge(S["exr_exp"], CR + l + 1)
                for h in range(HEADS):
                    mm = pe.matmul(psum[:, PN1, 32 * h:32 * h + 32], ident[0:4, h:h + 1].to_broadcast([4, P]),
                                   exr[:, :, :].rearrange("p a b -> p (a b)"), start=True, stop=True)
                mm.then_inc(S["bc_mm"], 1)
                pe.wait_ge(S["bc_out"], CR + l + 1)
                pe.wait_ge(S["tr_out"], CR + 2 * l + 2)

                def stage_a(n8, c, ml):
                    cs = slice(c * CH, (c + 1) * CH)
                    pe.wait_ge(S["kv_out"], CR + 8 * n8 + c)
                    for a in range(2):
                        pe.transpose(psum[:, TK, a * P:(a + 1) * P], kt[:, a, cs], ident[:, :])
                    for a in range(2):
                        if ml:
                            mm = pe.matmul(psum[:, TK, 256:512], vt[:, a, cs], wvv[:, a, :], start=(a == 0), stop=(a == 1))
                        else:
                            mm = pe.transpose(psum[:, TK, 256 + a * P:256 + (a + 1) * P], vt[:, a, cs], ident[:, :])
                    mm.then_inc(S["kv_mm"], 1)
                    pe.wait_ge(S["sd_done"], CR + 8 * n8 + c)
                    pe.wait_ge(S["ht_done"], CR + 8 * n8 + c - 2)
                    for a in range(2):
                        mm = pe.matmul(psum[:, ST, 0:CH], kt[:, a, cs], qt[:, a, cs], start=(a == 0), stop=(a == 1))
                    mm.then_inc(S["st_mm"], 1)

                def stage_b(n8, c, ml):
                    cs, e = slice(c * CH, (c + 1) * CH), 257 if ml else 256
                    pe.wait_ge(S["vw_done"], CR + 8 * n8 + c + 1)
                    pe.wait_ge(S["sd_done"], CR + 8 * n8 + c + 1)
                    pe.wait_ge(S["h_ready"], CR + 8 * n8 + c)
                    pe.wait_ge(S["in_done"], CR + 8 * n8 + c)
                    pe.wait_ge(S["stt"], CR + 9 * n8 + c + 1)
                    pe.matmul(psum[:, PN1, 0:e], sd[c % 2], vtok[c % 2][:, 0:e], start=True, stop=True)
                    if ml:
                        for a in range(2):
                            pe.matmul(psum[:, PN1, 300 + a:301 + a], ktok[c % 2][:, a * P:(a + 1) * P], vw[c % 2][:, 256:257],
                                      start=True, stop=True)
                    for a in range(2):
                        mm = pe.matmul(psum[:, PN2, 0:e], qt[:, a, cs], st[:, a, 0:e], start=(a == 0), stop=(a == 1))
                    mm.then_inc(S["num_mm"], 1)
                    for a in range(2):
                        mm = pe.matmul(psum[:, PS, 256 * a:256 * a + 256], ktok[c % 2][:, a * P:(a + 1) * P],
                                       vw[c % 2][:, 0:256], start=True, stop=True)
                    mm.then_inc(S["ps_mm"], 1)

                def stage_c(n8, c):
                    pe.wait_ge(S["hn_ready"], CR + 8 * n8 + c + 1)
                    pe.wait_ge(S["sd_done"], CR + 8 * n8 + min(c + 3, NC))
                    pe.wait_ge(S["ht_done"], CR + 8 * n8 + c)
                    for a in range(2):
                        mm = pe.transpose(psum[:, ST, (a + 1) * P:(a + 2) * P], hn[:, a * P:(a + 1) * P], ident[:, :])
                    mm.then_inc(S["ht_mm"], 1)

                def sample_rows(n8, b):
                    pe.wait_ge(S["dg_done"], CR + 8 * n8 + b + 1)
                    pe.matmul(psum[:, 2, 0:DH], ones[:, :], dg[:, :], start=True, stop=True).then_inc(S["vb_mm"], 1)

                def sample_query(n8, b):
                    pe.wait_ge(S["cs_new"], CR + 8 * n8 + b + 1)
                    for a in range(2):
                        o = 256 + a * NB + b
                        for d in range(2):
                            mm = pe.matmul(psum[:, 2, o:o + 1], cst[b % 2][:, d, a * P:(a + 1) * P], qs[:, 0, d, b:b + 1],
                                           start=(d == 0), stop=(d == 1))
                    mm.then_inc(S["hs_mm"], 1)

                def sample_sum(n8, r):
                    pe.wait_ge(S["red_in"], CR + 2 * n8 + 1 + r)
                    for d in range(2):
                        mm = pe.matmul(psum[:, TK, 16 * r:16 * r + 8], ones[:, :], sm2[:, 1 + r, 8 * d:8 * d + 8],
                                       start=(d == 0), stop=(d == 1))
                    mm.then_inc(S["red_mm"], 1)

                def chunks(l, h, n8, t0, ml):
                    for slot in range(NC + 2):
                        if slot < NC:
                            stage_a(n8, slot, ml)
                        gate_group(l, t0, slot + 2)
                        if 1 <= slot <= NC:
                            stage_b(n8, slot - 1, ml)
                            sample_query(n8, slot - 1)
                        if slot == 0 and ml:
                            for d in range(2):
                                mm = pe.matmul(psum[:, 2, 300:308], ones[:, :], sm2[:, 6, 8 * d:8 * d + 8],
                                               start=(d == 0), stop=(d == 1))
                        if slot < NC:
                            sample_rows(n8, slot)
                        if slot >= 2:
                            stage_c(n8, slot - 2)
                        if slot >= NC:
                            if slot == NC:
                                pe.wait_ge(S["kv_out"], CR + 8 * n8 + NC)
                            sample_sum(n8, slot - NC)

                settle(pe)
                with pe.Fori(0, HEADS) as h:
                    n8 = 8 * l + h
                    t0 = RET0 + 10 * h
                    for m in range(6):
                        proj(l, t0 + m, m % 2, lag=2 if m == 0 else 3)
                    for n in range(2):
                        gate_group(l, t0 + 6, n)
                    pe.wait_ge(S["rope_done"], CR + n8 + 1)
                    pe.wait_ge(S["evac"], CR + evs(l, t0 + 5, 2))
                    chunks(l, h, n8, t0 + 6, False)
                settle(pe)
                with pe.Fori(0, HEADS) as h:
                    n8 = 8 * l + 4 + h
                    t0 = ML0 + 4 * h
                    pe.wait_ge(S["selh"], CR + 4 * l + h + 1)
                    pe.wait_ge(S["ht_done"], CR + 8 * n8)
                    pe.wait_ge(S["red_out"], CR + n8)
                    for a in range(2):
                        mm = pe.matmul(psum[:, TK + a, 0:512], selh[:, :], nmrow[:, 512 * a:512 * a + 512], start=True, stop=True)
                    mm.then_inc(S["dm_mm"], 1)
                    for n in range(2):
                        gate_group(l, t0, n)
                    pe.wait_ge(S["ml_in"], 96 * (4 * l + h) + 96)
                    pe.wait_ge(S["dm_arg"], CR + 4 * l + h + 1)
                    for n in range(12):
                        m, a, g = n // 6, (n // 3) % 2, n % 3
                        pe.wait_ge(S["qk_ev"], CR + 12 * (4 * l + h) + n - 3)
                        for i in range(2):
                            mm = pe.matmul(psum[:, TK + n % 4, 0:GW], wqk[:, m, i, a * P:(a + 1) * P],
                                           xc2[:, i, g * GW:(g + 1) * GW], start=(i == 0), stop=(i == 1))
                        mm.then_inc(S["qk_mm"], 1)
                    for a in range(2):
                        for i in range(2):
                            mm = pe.matmul(psum[:, PS, a * NB:(a + 1) * NB], wvv[:, i, a * P:(a + 1) * P], vt[:, i, SEQ:T],
                                           start=(i == 0), stop=(i == 1))
                    mm.then_inc(S["vs_mm"], 1)
                    pe.wait_ge(S["qk_ev"], CR + 12 * (4 * l + h) + 12)
                    pe.wait_ge(S["rope_done"], CR + n8 + 1)
                    pe.wait_ge(S["vs_out"], CR + 4 * l + h + 1)
                    chunks(l, h, n8, t0, True)
                for g in range(NG):
                    if g == 0:
                        pe.wait_ge(S["br_done"], CR + 8 * l + 8)
                    pe.matmul(psum[:, ST + g, 0:GW], zf[:, 0:1].to_broadcast([P, P]), ones[:, 0:1].to_broadcast([P, GW]),
                              start=True, stop=False, skip_group_check=True)
                pe.wait_ge(S["plane_ready"], CR + 2 * KT * l + 2 * KT)
                settle(pe)
                with pe.Fori(0, KT // 2) as i:
                    for s in range(2):
                        proj(l, OUT0 + 2 * i + s, s)
                    for s in range(2):
                        pe.wait_ge(S["osq"], CR + KT * l + 2 * i + s + 1)
                        for g in range(NG):
                            mm = pe.matmul(psum[:, ST + g, 0:GW], ones[:, :], tok(sq[s], g), start=False, stop=True,
                                           skip_group_check=True)
                        mm.then_inc(S["osq_used"], 1)

        @block.scalar
        def _(act):
            open_balance(act, "act")

            def activate(*args, **kw):
                made = act.activation(*args, **kw)
                act.drain()
                return made

            def evacuate(l, t, dst, func=ACT.Copy, scale=1.0, groups=(0, 1, 2)):
                for g in groups:
                    act.wait_ge(S["mm"], CR + mms(l, t, g))
                    activate(dst[:, g * GW:(g + 1) * GW], psum[:, g, 0:GW], func, scale=scale).then_inc(S["evac"], 1)

            act.wait_ge(S["const_in"], 96)
            activate(cH[:, :, :], cT[:, :, :], ACT.Copy).then_inc(S["cH_done"], 1)
            act.wait_ge(S["x_in"], 32 * KT)
            with act.Fori(0, DEPTH) as l:
                act.wait_ge(S["ldone"], CR + l)
                act.wait_ge(S["sdone"], CR + l)
                for k in range(KT):
                    act.wait_ge(S["sq_used"], CR + KT * l + k - 1)
                    activate(sq[k % 2], xm[:, k, :], ACT.Square).then_inc(S["sqr"], 1)
                act.wait_ge(S["par_in"], 128 * (l + 1))
                activate(wif[:, 8:16, :], wif[:, 8:16, :], ACT.Copy, scale=DH ** -0.5).then_inc(S["wif_ready"], 1)
                act.wait_ge(S["lam_abs"], CR + l + 1)
                activate(sm[:, 16:24], sm[:, 16:24], ACT.Exp, scale=-1.0).then_inc(S["lam_exp"], 1)
                act.wait_ge(S["rs_var"], CR + l + 1)
                activate(rs, rs, ACT.Sqrt).then_inc(S["rs_sqrt"], 1)
                with act.Fori(0, NADA // 2) as i:
                    act.wait_ge(S["mm"], CR + mms(l, 2 * i + 1, 2))
                    settle(act)
                    activate(ada[:, bass.ds(2 * i, 2), :], psum[:, TK, 0:20].rearrange("p (a c) -> p a c", a=2),
                                   ACT.Copy).then_inc(S["ada_out"], 1)
                act.wait_ge(S["ada_ready"], CR + l + 1)
                for k in range(KT):
                    act.wait_ge(S["tmp_ready"], CR + KT * l + k + 1)
                    activate(tmp_n[k % 2][:, 0:SEQ], tmp_n[k % 2][:, 0:SEQ], ACT.Identity, bias=ada[:, k, 0:1],
                                   scale=s1[:, k, 0:1])
                    activate(uH[:, k, :], tmp_n[k % 2], ACT.Copy).then_inc(S["uH_ready"], 1)
                act.wait_ge(S["fold_zero"], CR + l + 1)
                for h in range(HEADS):
                    act.wait_ge(S["ab_mm"], CR + 4 * l + h + 1)
                    src = psum[:, TK, 0:32].rearrange("p (a i c) -> p a i c", a=2, i=2)
                    activate(fold[:, :, 2 * h:2 * h + 2, 0:4], src[:, :, :, 0:4], ACT.Copy)
                    activate(fold[:, :, 2 * h:2 * h + 2, 32:36], src[:, :, :, 4:8], ACT.Copy).then_inc(S["ab_out"], 1)
                act.wait_ge(S["xj_pad"], CR + l + 1)
                with act.Fori(0, KT // 2) as i:
                    for s in range(2):
                        n = KT * l + 2 * i + s
                        act.wait_ge(S["gp_done"], CR + n - 1)
                        act.wait_ge(S[f"xsp{s}"], CD + 32 * (4 * l + i))
                        evacuate(l, XML0 + 2 * i + s, xj[s][:, 3:3 + T])
                        act.wait_ge(S["conv_done"], CR + n + 1)
                        activate(sg[s], yj[s], ACT.Sigmoid).then_inc(S["sig_done"], 1)
                act.wait_ge(S["gp_done"], CR + KT * (l + 1))
                for s in range(2):
                    act.wait_ge(S[f"xsp{s}"], CD + 128 * (l + 1))
                activate(work[0:HCOL, 0:T].rearrange("p (g t) -> p g t", g=NG), psum[0:HCOL, ST:ST + NG, 0:GW],
                               ACT.Identity, bias=bifp[:, 0:1]).then_inc(S["rows_in"], 1)
                act.wait_ge(S["row_abs"], CR + l + 1)
                activate(row[2], row[2], ACT.Exp, scale=-1.0).then_inc(S["row_exp"], 1)
                act.wait_ge(S["stk_ready"], CR + l + 1)
                activate(exr[:, :, :], exr[:, :, :], ACT.Exp).then_inc(S["exr_exp"], 1)
                with act.Fori(0, KT // 2) as i:
                    for s in range(2):
                        j = 2 * i + s
                        n = KT * l + j
                        t = RG0 + 3 * j
                        act.wait_ge(S["rg_xc"], CR + n)
                        evacuate(l, t, rgx[:, 3:3 + T])
                        act.wait_ge(S["rg_y"], CR + n)
                        evacuate(l, t + 1, rg["z"])
                        evacuate(l, t + 2, rg["sg"], ACT.Sigmoid)
                        activate(rg["sz"], rg["z"], ACT.Sigmoid).then_inc(S["rg_sig"], 1)
                        for g in range(NG):
                            act.wait_ge(S["rg_mm"], CR + 3 * n + g + 1)
                            for m, dst in ((0, "r"), (1, "i")):
                                settle(act)
                                activate(tok(rg[dst], g), psum[:, TK + 2 * m + g % 2, 0:GW], ACT.Sigmoid,
                                               bias=pcol("rg_b_a" if m == 0 else "rg_b_x", j)).then_inc(S["rg_ev"], 1)
                        activate(rg["t"], rg["r"], ACT.Tanh, scale=nsp[:, 1, bass.ds(j, 1)])
                        activate(rg["a"], rg["r"], ACT.Exp, scale=nsp[:, 0, bass.ds(j, 1)])
                        activate(rg["r"], rg["a"], ACT.Square).then_inc(S["rg_sq2"], 1)
                        act.wait_ge(S["rg_fac"], CR + n + 1)
                        activate(rg["t"], rg["r"], ACT.Sqrt, scale=1.0).then_inc(S["rg_sqrt"], 1)
                for a in range(2):
                    act.wait_ge(S["tr_mm"], CR + 2 * l + a + 1)
                    src = psum[:, TK, 0:512].rearrange("p (c q x) -> p c q x", c=4, q=4)
                    activate(ucol[:, 4 * a:4 * a + 4, 0, :], src[:, :, 0, 0:4], ACT.Copy)
                    activate(ucol[:, 4 * a:4 * a + 4, 1:4, :], src[:, :, 1:4, 0:4], ACT.Exp).then_inc(S["tr_out"], 1)
                act.wait_ge(S["bc_mm"], CR + l + 1)
                activate(bc[:, :, :, :].rearrange("p h a b -> p (h a b)"), psum[:, PN1, 0:128], ACT.Copy).then_inc(S["bc_out"], 1)

                def gate_out(l, n8, t0, n):
                    q, cs = n // 3, slice((n % 3) * GW, (n % 3 + 1) * GW)
                    if n == 0:
                        act.wait_ge(S["br_done"], CR + n8)
                    if n >= 3:
                        act.wait_ge(S["g_mul"], CR + 12 * n8 + n - 2)
                    act.wait_ge(S["mm"], CR + mms(l, t0 + q, n % 3))
                    if q % 2 == 0:
                        activate(tg[q // 2][:, cs], psum[:, n % 2, 0:GW], ACT.Copy)
                    activate(tg[2][:, cs], psum[:, n % 2, 0:GW], ACT.Sigmoid).then_inc(S["evac"], 1)

                def chunks(l, h, n8, t0, ml):
                    e = 257 if ml else 256
                    for slot in range(NC + 2):
                        if slot < NC:
                            b = slot
                            act.wait_ge(S["kv_mm"], CR + 8 * n8 + slot + 1)
                            act.wait_ge(S["ps_mm"], CR + 8 * n8 + slot - 1)
                            activate(ktok[slot % 2], psum[:, TK, 0:256], ACT.Copy)
                            activate(vtok[slot % 2][:, 0:256], psum[:, TK, 256:512], ACT.Copy).then_inc(S["kv_out"], 1)
                            act.wait_ge(S[f"cs_in{b % 2}"], 64 * n8 + 16 * (b // 2) + 16)
                            settle(act)
                            sc = bc[:, bass.ds(h, 1), 1, b] if ml else rcol[:, bass.ds(12 + h, 1)]
                            activate(cst[b % 2][:, :, :], cst[b % 2][:, :, :], ACT.Copy, scale=sc).then_inc(S["cs_dec"], 1)
                        gate_out(l, n8, t0, slot + 2)
                        if 1 <= slot <= NC:
                            c = slot - 1
                            act.wait_ge(S["num_mm"], CR + 8 * n8 + c + 1)
                            act.wait_ge(S["h_ready"], CR + 8 * n8 + c)
                            sc = ucol[:, c, 1, bass.ds(h, 1)] if ml else rcol[:, bass.ds(h, 1)]
                            settle(act)
                            activate(inter[:, 0:e], psum[:, PN2, 0:e], ACT.Copy, scale=sc).then_inc(S["in_done"], 1)
                            act.wait_ge(S["var_ready"], CR + 8 * n8 + c + 1)
                            activate(sm[:, 13:14], sm[:, 12:13], ACT.Sqrt).then_inc(S["sq_done"], 1)
                    act.wait_ge(S["red_out"], CR + n8 + 1)
                    activate(sm2[:, 3, 8:16], sm2[:, 3, 0:8], ACT.Sqrt).then_inc(S["red_sqrt"], 1)

                with act.Fori(0, HEADS) as h:
                    n8 = 8 * l + h
                    t0 = RET0 + 10 * h
                    act.wait_ge(S["ps_mm"], CR + 8 * n8)
                    act.wait_ge(S["rg_y"], CR + KT * (l + 1))
                    for a in range(2):
                        evacuate(l, t0 + a, qt[:, a, :])
                    for a in range(2):
                        evacuate(l, t0 + 2 + a, kt[:, a, :], scale=DH ** -0.5)
                    act.wait_ge(S["br_done"], CR + n8)
                    for a in range(2):
                        evacuate(l, t0 + 4 + a, vt[:, a, :])
                    for n in range(2):
                        gate_out(l, n8, t0 + 6, n)
                    act.wait_ge(S["rope_done"], CR + n8 + 1)
                    chunks(l, h, n8, t0 + 6, False)
                with act.Fori(0, HEADS) as h:
                    n8 = 8 * l + 4 + h
                    t0 = ML0 + 4 * h
                    act.wait_ge(S["dm_arg"], CR + 4 * l + h + 1)
                    activate(dm, dm, ACT.Exp).then_inc(S["dm_exp"], 1)
                    for n in range(2):
                        gate_out(l, n8, t0, n)
                    for n in range(12):
                        act.wait_ge(S["qk_mm"], CR + 12 * (4 * l + h) + n + 1)
                        dst = (qt, kt)[n // 6][:, (n // 3) % 2, :]
                        activate(tok(dst, n % 3), psum[:, TK + n % 4, 0:GW], ACT.Copy,
                                       scale=(1.0, DH ** -0.5)[n // 6]).then_inc(S["qk_ev"], 1)
                    act.wait_ge(S["vs_mm"], CR + 4 * l + h + 1)
                    activate(qs[:, 2, :, :].rearrange("p a b -> p (a b)"), psum[:, PS, 0:16], ACT.Copy).then_inc(S["vs_out"], 1)
                    for a in range(2):
                        settle(act)
                        activate(xc2[:, a, :], xc2[:, a, :], ACT.Copy, scale=pcol("ml_skip", 2 * h + a))
                    act.wait_ge(S["rope_done"], CR + n8 + 1)
                    chunks(l, h, n8, t0, True)
                act.wait_ge(S["br_done"], CR + 8 * l + 8)
                for k in range(KT):
                    activate(uH[:, k, :], xm[:, k, :], ACT.Copy).then_inc(S["uH_ready"], 1)
                act.wait_ge(S["plane_ready"], CR + 2 * KT * (l + 1))
                with act.Fori(0, KT // 2) as i:
                    for s in range(2):
                        j = 2 * i + s
                        n = KT * l + j
                        for g in range(NG):
                            act.wait_ge(S["mm"], CR + mms(l, OUT0 + j, g))
                            settle(act)
                            activate(xm[:, bass.ds(j, 1), g * GW:(g + 1) * GW], psum[:, g, 0:GW].unsqueeze(1), ACT.Copy).then_inc(S["evac"], 1)
                        act.wait_ge(S["osq_used"], CR + n - 1)
                        settle(act)
                        activate(sq[s].unsqueeze(1), xm[:, bass.ds(j, 1), :], ACT.Square).then_inc(S["osq"], 1)
                act.wait_ge(S["ors_var"], CR + l + 1)
                activate(rs, rs, ACT.Sqrt).then_inc(S["ors_sqrt"], 1)

        @block.vector
        def _(dve):
            open_balance(dve, "dve")

            def fenced(op):
                def run(*args, **kw):
                    made = op(*args, **kw)
                    dve.drain()
                    return made
                return run

            tt, ts, stt_, cp, rec, scan, memset, bn_stats, bn_aggr, nop = map(fenced, (
                nc.vector.tensor_tensor, nc.vector.tensor_scalar, nc.vector.scalar_tensor_tensor, nc.vector.tensor_copy,
                nc.vector.reciprocal, nc.vector.tensor_tensor_scan, nc.vector.memset, nc.vector.bn_stats,
                nc.vector.bn_aggr, nc.vector.engine_nop))

            def log1p(z, z2, p):
                ts(p, z2, LOG1P_TERMS[0], None, ALU.mult)
                for c in LOG1P_TERMS[1:]:
                    stt_(p, p, c, z2, ALU.add, ALU.mult)
                stt_(p, p, 1.0, z, ALU.add, ALU.mult)

            def conv(x, y, name, j, state, new, pout):
                w = "rg_conv_w" if name == "rg" else "ml_conv_w"
                b = "rg_conv_b" if name == "rg" else "ml_conv_b"
                ts(y, x[:, 3:3 + T], pcol(w, 3 * KT + j), pcol(b, j), ALU.mult, ALU.add)
                for tap in (2, 1, 0):
                    stt_(y[:, 0:SEQ], x[:, tap:tap + SEQ], pcol(w, tap * KT + j), y[:, 0:SEQ], ALU.mult, ALU.add)
                    stt_(y[:, SEQ:T].unsqueeze(1), state[:, bass.ds(j, 1), tap, :], pcol(w, tap * KT + j),
                         y[:, SEQ:T].unsqueeze(1), ALU.mult, ALU.add)
                cp(new[:, bass.ds(j, 1), 0:2, :], state[:, bass.ds(j, 1), 1:3, :])
                cp(new[:, bass.ds(j, 1), 2, :], x[:, 3 + SEQ:3 + T].unsqueeze(1))
                return cp(pcn[:, pout, bass.ds(j, 1), :], x[:, SEQ:SEQ + 3].unsqueeze(1))

            memset(zf[:, :], 0.0)
            memset(mc[:, 0:1], 0.0)
            memset(work[0:P, 0:1], 0.0).then_inc(S["zeroed"], 1)
            dve.wait_ge(S["cH_done"], CR + 1)
            tt(cL[:, :, :], cT[:, :, :], cH[:, :, :].bitcast(F32), ALU.subtract).then_inc(S["cL_done"], 1)
            with dve.Fori(0, DEPTH) as l:
                dve.wait_ge(S["sdone"], CR + l)
                dve.wait_ge(S["par_in"], 128 * (l + 1))
                memset(fold, 0.0).then_inc(S["fold_zero"], 1)
                lam = pcol("rg_lambda", 0, KT)
                stt_(sm[:, 16:24], lam, -1.0, lam, ALU.mult, ALU.max).then_inc(S["lam_abs"], 1)
                dve.wait_ge(S["lam_exp"], CR + l + 1)
                ts(sm[:, 24:32], sm[:, 16:24], 2.0, None, ALU.add)
                rec(sm[:, 24:32], sm[:, 24:32])
                tt(sm[:, 24:32], sm[:, 24:32], sm[:, 16:24], ALU.mult)
                tt(sm[:, 32:40], sm[:, 24:32], sm[:, 24:32], ALU.mult)
                log1p(sm[:, 24:32], sm[:, 32:40], sm[:, 40:48])
                ts(sm[:, 48:56], lam, -1.0, 0.0, ALU.mult, ALU.max)
                stt_(sm[:, 48:56], sm[:, 40:48], 2.0, sm[:, 48:56], ALU.mult, ALU.add)
                ts(nsp[:, 0, :], sm[:, 48:56], -RG_C, None, ALU.mult)
                ts(nsp[:, 1, :], sm[:, 48:56], RG_C, None, ALU.mult)
                dve.wait_ge(S["sq_used"], CR + KT * (l + 1))
                ts(rs.rearrange("p (g t) -> p g t", g=NG), psum[:, 0:NG, 0:GW], 1.0 / D, EPS, ALU.mult, ALU.add).then_inc(S["rs_var"], 1)
                dve.wait_ge(S["rs_sqrt"], CR + l + 1)
                rec(rs, rs)
                dve.wait_ge(S["ada_out"], CR + NADA // 2 * (l + 1))
                tt(ada[:, :, :], ada[:, :, :], pcol("b_ada", 0, NADA).unsqueeze(2).to_broadcast([P, NADA, 10]), ALU.add)
                stt_(s1[:, :, :], ada[:, KT:2 * KT, :], 1.0, pcol("norm_pre", 0, KT).unsqueeze(2).to_broadcast([P, KT, 10]),
                     ALU.add, ALU.mult)
                tt(gpo[:, :, :], ada[:, 2 * KT:, :], pcol("norm_post", 0, KT).unsqueeze(2).to_broadcast([P, KT, 10]),
                   ALU.mult).then_inc(S["ada_ready"], 1)

                def low(k):
                    dve.wait_ge(S["uH_ready"], CR + 2 * KT * l + k + 1)
                    tt(uL[:, k, :], tmp_n[k % 2], uH[:, k, :].bitcast(F32), ALU.subtract).then_inc(S["plane_ready"], 1)

                for k in range(KT):
                    t_ = tmp_n[k % 2]
                    tt(t_, xm[:, k, :], rs, ALU.mult)
                    tt(t_[:, SEQ:T], t_[:, SEQ:T], s1[:, k, 1:9], ALU.mult)
                    tt(t_[:, SEQ:T], t_[:, SEQ:T], ada[:, k, 1:9], ALU.add).then_inc(S["tmp_ready"], 1)
                    if k >= 1:
                        low(k - 1)
                low(KT - 1)
                dve.wait_ge(S["ab_out"], CR + 4 * (l + 1))
                for s in range(2):
                    o = memset(xj[s][:, 0:3], 0.0)
                o.then_inc(S["xj_pad"], 1)
                settle(dve)
                with dve.Fori(0, KT // 2) as i:
                    for s in range(2):
                        j = 2 * i + s
                        n = KT * l + j
                        dve.wait_ge(S["gp_done"], CR + n - 1)
                        dve.wait_ge(S[f"xsp{s}"], CD + 32 * (4 * l + i))
                        cp(fj[s][:, :, :].unsqueeze(2), fold[:, :, bass.ds(j, 1), :])
                        dve.wait_ge(S["evac"], CR + evs(l, XML0 + j, 2))
                        conv(xj[s], yj[s], "ml", j, mcs, mcsn, 1).then_inc(S["conv_done"], 1)
                        dve.wait_ge(S["sig_done"], CR + n + 1)
                        tt(yj[s], yj[s], sg[s], ALU.mult).then_inc(S["xc_ready"], 1)
                dve.wait_ge(S["rows_in"], CR + l + 1)
                R = row
                R0 = work[0:4, 0:T]
                memset(stk, 0.0)
                cp(R[1], work[32:36, 0:T])
                stt_(R[2], R[1], -1.0, R[1], ALU.mult, ALU.max).then_inc(S["row_abs"], 1)
                ts(R[6], R[1], 0.0, None, ALU.min)
                dve.wait_ge(S["row_exp"], CR + l + 1)
                ts(R[3], R[2], 2.0, None, ALU.add)
                rec(R[3], R[3])
                tt(R[3], R[2], R[3], ALU.mult)
                tt(R[4], R[3], R[3], ALU.mult)
                log1p(R[3], R[4], R[5])
                stt_(R[6], R[5], -2.0, R[6], ALU.mult, ALU.add)
                cs = [slice(c * CH, (c + 1) * CH) for c in range(NC)]
                for c in range(NC):
                    scan(R[7][:, cs[c]], ones[0:4, :], R[6][:, cs[c]], 0.0, ALU.mult, ALU.add)
                tt(R[8][:, 0:SEQ], R0[:, 0:SEQ], R[7][:, 0:SEQ], ALU.subtract)
                for c in range(NC):
                    scan(R[9][:, cs[c]], R[8][:, cs[c]], R[8][:, cs[c]], mc[:, c:c + 1], ALU.max, ALU.max)
                    e = (c + 1) * CH - 1
                    tt(mc[:, c + 1:c + 2], R[9][:, e:e + 1], R[7][:, e:e + 1], ALU.add)
                    ts(stk[32:36, cs[c]], R[9][:, cs[c]], -1.0, mc[:, c:c + 1], ALU.mult, ALU.add)
                    ts(stk[96:100, cs[c]], R[8][:, cs[c]], R[9][:, e:e + 1], None, ALU.subtract)
                ts(nmrow[:, :], R[9][:, 0:SEQ], -1.0, None, ALU.mult)
                cp(stk[0:4, :], R[8][:, 0:SEQ])
                stt_(stk[64:68, :], R[7][:, 0:SEQ], -1.0, R[9][:, 0:SEQ], ALU.mult, ALU.subtract)
                tt(exr[:, 0, :], mc[:, 0:NC], R[9][:, CH - 1:SEQ:CH], ALU.subtract)
                tt(smx[:, 0, :], R[6][:, SEQ:T], mm0[:, :], ALU.add)
                tt(smx[:, 1, :], smx[:, 0, :], R0[:, SEQ:T], ALU.max)
                tt(exr[:, 1, :], smx[:, 0, :], smx[:, 1, :], ALU.subtract)
                tt(exr[:, 2, :], R0[:, SEQ:T], smx[:, 1, :], ALU.subtract)
                ts(exr[:, 3, :], smx[:, 1, :], -1.0, None, ALU.mult).then_inc(S["stk_ready"], 1)
                memset(rgx[:, 0:3], 0.0)
                dve.wait_ge(S["spill"], 16 * (l + 1))
                settle(dve)
                with dve.Fori(0, KT // 2) as i:
                    for s in range(2):
                        j = 2 * i + s
                        n = KT * l + j
                        dve.wait_ge(S["evac"], CR + evs(l, RG0 + 3 * j, 2))
                        dve.wait_ge(S["rg_mm"], CR + 3 * n)
                        conv(rgx, rg["xc"], "rg", j, rcs, rcsn, 0).then_inc(S["rg_xc"], 1)
                        dve.wait_ge(S["rg_sig"], CR + n + 1)
                        tt(rg["z"], rg["z"], rg["sz"], ALU.mult)
                        tt(rg["z"], rg["z"], rg["sg"], ALU.mult)
                        dve.wait_ge(S["rg_sq2"], CR + n + 1)
                        stt_(rg["r"], rg["r"], 1.0, rg["t"], ALU.add, ALU.mult).then_inc(S["rg_fac"], 1)
                        tt(rg["i"], rg["i"], rg["xc"], ALU.mult)
                        dve.wait_ge(S["rg_sqrt"], CR + n + 1)
                        tt(rg["i"], rg["i"], rg["t"], ALU.mult)
                        scan(rg["h"][:, 0:SEQ], rg["a"][:, 0:SEQ], rg["i"][:, 0:SEQ], 0.0, ALU.mult, ALU.add)
                        tt(rg["h"][:, SEQ:T].unsqueeze(1), rg["a"][:, SEQ:T].unsqueeze(1), rh0[:, bass.ds(j, 1), :], ALU.mult)
                        tt(rg["h"][:, SEQ:T], rg["h"][:, SEQ:T], rg["i"][:, SEQ:T], ALU.add)
                        cp(rhn[:, bass.ds(j, 1), :], rg["h"][:, SEQ - 1:T].unsqueeze(1))
                        tt(xm[:, bass.ds(j, 1), :], rg["h"].unsqueeze(1), rg["z"].unsqueeze(1), ALU.mult).then_inc(S["rg_y"], 1)

                def chunks(l, h, n8, t0, ml):
                    e = 257 if ml else 256
                    for slot in range(NC + 2):
                        if slot < NC:
                            sample_value(n8, slot)
                        if slot < NC:
                            c = slot
                            dve.wait_ge(S["kv_out"], CR + 8 * n8 + c + 1)
                            dve.wait_ge(S["ps_mm"], CR + 8 * n8 + c - 1)
                            if c == 0 and ml:
                                memset(vtok[0][:, 256:257], 1.0)
                                memset(vtok[1][:, 256:257], 1.0)
                            w = ucol[:, c, 3, bass.ds(h, 1)] if ml else rcol[:, bass.ds(4 + h, 1)]
                            ts(vw[c % 2][:, 0:e], vtok[c % 2][:, 0:e], w, None, ALU.mult).then_inc(S["vw_done"], 1)
                            dve.wait_ge(S["st_mm"], CR + 8 * n8 + c + 1)
                            if ml:
                                tt(sd[c % 2], psum[:, ST, 0:CH], dm[:, c * CH:(c + 1) * CH], ALU.mult).then_inc(S["sd_done"], 1)
                            else:
                                tt(sd[c % 2].unsqueeze(1), psum[:, ST, 0:CH].unsqueeze(1), dret[:, bass.ds(h, 1), :],
                                   ALU.mult).then_inc(S["sd_done"], 1)
                        if 1 <= slot <= NC:
                            c = slot - 1
                            dve.wait_ge(S["ps_mm"], CR + 8 * n8 + c + 1)
                            dec = bc[:, bass.ds(h, 1), 0, c] if ml else rcol[:, bass.ds(8 + h, 1)]
                            if ml:
                                stt_(st[:, :, 256], st[:, :, 256], dec, psum[:, PN1, 300:302], ALU.mult, ALU.add)
                                if c == NC - 1:
                                    cp(pn[:, :], st[:, :, 256])
                            stt_(st[:, :, 0:256], st[:, :, 0:256], dec, psum[:, PS, 0:512].rearrange("p (a e) -> p a e", a=2),
                                 ALU.mult, ALU.add).then_inc(S["stt"], 1)
                            dve.wait_ge(S["in_done"], CR + 8 * n8 + c + 1)
                            dve.wait_ge(S["ht_mm"], CR + 8 * n8 + c)
                            tt(hn[:, 0:e], inter[:, 0:e], psum[:, PN1, 0:e], ALU.add).then_inc(S["h_ready"], 1)
                            bn_stats(sm[:, 0:6], hn[:, 0:256])
                            if ml:
                                stt_(sm[:, 10:11], hn[:, 256:257], -1.0, hn[:, 256:257], ALU.mult, ALU.max)
                            bn_aggr(sm[:, 6:8], sm[:, 0:6])
                            if ml:
                                ts(sm[:, 10:11], sm[:, 10:11], ucol[:, c, 2, bass.ds(h, 1)], None, ALU.max)
                                ts(sm[:, 11:12], sm[:, 10:11], sm[:, 10:11], EPS, ALU.mult, ALU.mult)
                            ts(sm[:, 12:13], sm[:, 7:8], sm[:, 11:12] if ml else EPS, None, ALU.add).then_inc(S["var_ready"], 1)
                        if slot >= 2:
                            c = slot - 2
                            dve.wait_ge(S["ht_mm"], CR + 8 * n8 + c + 1)
                            for a in range(2):
                                src = psum[:, ST, (a + 1) * P:(a + 2) * P]
                                dst = vt[:, a, c * CH:(c + 1) * CH]
                                if ml:
                                    o = stt_(dst, src, pcol("ml_gn", 2 * h + a), xc2[:, a, c * CH:(c + 1) * CH], ALU.mult, ALU.add)
                                else:
                                    o = ts(dst, src, pcol("ret_gn", 2 * h + a), None, ALU.mult)
                            o.then_inc(S["ht_done"], 1)
                        gate_mul(l, n8, t0, slot + 2)
                        if slot < NC:
                            sample_update(n8, slot)
                        if 1 <= slot <= NC:
                            dve.wait_ge(S["sq_done"], CR + 8 * n8 + slot)
                            rec(sm[:, 14:15], sm[:, 13:14])
                            ts(hn[:, 0:256], hn[:, 0:256], sm[:, 6:7], sm[:, 14:15], ALU.subtract, ALU.mult).then_inc(S["hn_ready"], 1)
                        if slot == NC:
                            sample_heads(l, h, n8, ml)
                        if slot == NC + 1:
                            sample_norm(l, h, n8, ml)

                def gate_mul(l, n8, t0, n):
                    cs = slice((n % 3) * GW, (n % 3 + 1) * GW)
                    dve.wait_ge(S["evac"], CR + evs(l, t0 + n // 3, n % 3))
                    x = tg[n // 6][:, cs]
                    tt(x, x, tg[2][:, cs], ALU.mult).then_inc(S["g_mul"], 1)

                def sample_value(n8, b):
                    dve.wait_ge(S["vb_mm"], CR + 8 * n8 + b)
                    tt(dg[:, :].rearrange("p (a e) -> p a e", a=2), ident[:, :].unsqueeze(1).to_broadcast([P, 2, P]),
                       qs[:, 2, :, b:b + 1].to_broadcast([P, 2, P]), ALU.mult).then_inc(S["dg_done"], 1)

                def sample_update(n8, b):
                    dve.wait_ge(S["vb_mm"], CR + 8 * n8 + b + 1)
                    dve.wait_ge(S["cs_dec"], CR + 8 * n8 + b + 1)
                    for d in range(2):
                        v = cst[b % 2][:, d, :]
                        o = stt_(v, psum[:, 2, 0:DH], qs[:, 1, d, b:b + 1], v, ALU.mult, ALU.add)
                    o.then_inc(S["cs_new"], 1)

                def sample_heads(l, h, n8, ml):
                    hs = sm2[:, 1, :]
                    hs3 = hs.rearrange("p (a b) -> p a b", a=2)
                    dve.wait_ge(S["hs_mm"], CR + 8 * n8 + NB)
                    o = cp(hs, psum[:, 2, 256:272])
                    if ml:
                        o = cp(sm2[:, 4, 8:16], psum[:, 2, 300:308])
                    o.then_inc(S["red_in"], 1)
                    if ml:
                        stt_(sm2[:, 4, 0:8], sm2[:, 4, 8:16], -1.0, sm2[:, 4, 8:16], ALU.mult, ALU.max)
                        tt(sm2[:, 4, 0:8].unsqueeze(1), sm2[:, 4, 0:8].unsqueeze(1), bc[:, bass.ds(h, 1), 3, :], ALU.max)
                        tt(sm2[:, 4, 8:16], sm2[:, 4, 0:8], sm2[:, 4, 0:8], ALU.mult)
                    dve.wait_ge(S["red_mm"], CR + 2 * n8 + 1)
                    ts(sm2[:, 5, 0:8], psum[:, TK, 0:8], 1.0 / DH, None, ALU.mult)
                    tt(hs3, hs3, sm2[:, 5, 0:8].unsqueeze(1).to_broadcast([P, 2, NB]), ALU.subtract)
                    tt(sm2[:, 2, :], hs, hs, ALU.mult).then_inc(S["red_in"], 1)

                def sample_norm(l, h, n8, ml):
                    hs = sm2[:, 1, :]
                    hs3 = hs.rearrange("p (a b) -> p a b", a=2)
                    dve.wait_ge(S["red_mm"], CR + 2 * n8 + 2)
                    if ml:
                        ts(sm2[:, 3, 0:8], psum[:, TK, 16:24], 1.0 / DH, None, ALU.mult)
                        stt_(sm2[:, 3, 0:8], sm2[:, 4, 8:16], EPS, sm2[:, 3, 0:8], ALU.mult, ALU.add).then_inc(S["red_out"], 1)
                    else:
                        ts(sm2[:, 3, 0:8], psum[:, TK, 16:24], 1.0 / DH, EPS, ALU.mult, ALU.add).then_inc(S["red_out"], 1)
                    dve.wait_ge(S["red_sqrt"], CR + n8 + 1)
                    rec(sm2[:, 5, 8:16], sm2[:, 3, 8:16])
                    tt(hs3, hs3, sm2[:, 5, 8:16].unsqueeze(1).to_broadcast([P, 2, NB]), ALU.mult)
                    for a in range(2):
                        if ml:
                            stt_(vt[:, a, SEQ:T], hs[:, 8 * a:8 * a + 8], pcol("ml_gn", 2 * h + a), xc2[:, a, SEQ:T], ALU.mult, ALU.add)
                        else:
                            ts(vt[:, a, SEQ:T], hs[:, 8 * a:8 * a + 8], pcol("ret_gn", 2 * h + a), None, ALU.mult)

                def merge(l, h, n8):
                    tt(vt, vt, tg01, ALU.mult)
                    x2 = xm[:, bass.ds(2 * h, 2), :]
                    tt(x2, x2, vt, ALU.add).then_inc(S["br_done"], 1)

                settle(dve)
                with dve.Fori(0, HEADS) as h:
                    n8 = 8 * l + h
                    t0 = RET0 + 10 * h
                    dve.wait_ge(S["rope_in"], 16 * (l + 1))
                    dve.wait_ge(S["st_out"], CD + 48 * n8)
                    for q, x in ((1, qt), (3, kt)):
                        dve.wait_ge(S["evac"], CR + evs(l, t0 + q, 2))
                        tt(rtmp[0], x[:, 0, :], rope[:, 0, :], ALU.mult)
                        tt(rtmp[1], x[:, 1, :], rope[:, 1, :], ALU.mult)
                        tt(x[:, 0, :], x[:, 0, :], rope[:, 1, :], ALU.mult)
                        tt(x[:, 1, :], x[:, 1, :], rope[:, 0, :], ALU.mult)
                        tt(x[:, 1, :], x[:, 0, :], x[:, 1, :], ALU.add)
                        tt(x[:, 0, :], rtmp[0], rtmp[1], ALU.subtract)
                    cp(qs[:, 0, :, :], qt[:, :, SEQ:T])
                    cp(qs[:, 1, :, :], kt[:, :, SEQ:T])
                    dve.wait_ge(S["evac"], CR + evs(l, t0 + 5, 2))
                    cp(qs[:, 2, :, :], vt[:, :, SEQ:T])
                    memset(st, 0.0).then_inc(S["stt"], 1)
                    nop().then_inc(S["rope_done"], 1)
                    for n in range(2):
                        gate_mul(l, n8, t0 + 6, n)
                    chunks(l, h, n8, t0 + 6, False)
                    merge(l, h, n8)
                settle(dve)
                with dve.Fori(0, HEADS) as h:
                    n8 = 8 * l + 4 + h
                    hh = 4 * l + h
                    t0 = ML0 + 4 * h
                    cp(selh[:, :], ident[0:4, bass.ds(h, 1)].to_broadcast([4, P])).then_inc(S["selh"], 1)
                    dve.wait_ge(S["dm_mm"], CR + hh + 1)
                    for c in range(NC):
                        o = ts(dm[:, c * CH:(c + 1) * CH], psum[:, TK + c // 4, (c % 4) * CH:(c % 4 + 1) * CH],
                               ucol[:, c, 0, bass.ds(h, 1)], 0.0, ALU.add, ALU.min)
                    o.then_inc(S["dm_arg"], 1)
                    dve.wait_ge(S["st_out"], CD + 48 * n8)
                    memset(st, 0.0).then_inc(S["stt"], 1)
                    dve.wait_ge(S["dm_exp"], CR + hh + 1)
                    d3 = dm.rearrange("p (c t) -> p c t", c=NC)
                    tt(d3, d3, mask[:, :].unsqueeze(1).to_broadcast([P, NC, CH]), ALU.mult)
                    dve.wait_ge(S["vs_out"], CR + hh + 1)
                    cp(qs[:, 0, :, :], qt[:, :, SEQ:T])
                    cp(qs[:, 1, :, :], kt[:, :, SEQ:T])
                    nn3 = sm2[:, 6, :].rearrange("p (a b) -> p a b", a=2)
                    d8 = bc[:, bass.ds(h, 1), 1, :].to_broadcast([P, 2, NB])
                    w8 = bc[:, bass.ds(h, 1), 2, :].to_broadcast([P, 2, NB])
                    tt(mnn[:, :, :], mn0[:, bass.ds(h, 1), :, :].rearrange("p o a b -> p (o a) b"), d8, ALU.mult)
                    tt(nn3, qs[:, 1, :, :], w8, ALU.mult)
                    tt(qs[:, 2, :, :], qs[:, 2, :, :], w8, ALU.mult)
                    tt(mnn[:, :, :], mnn[:, :, :], nn3, ALU.add)
                    tt(nn3, mnn[:, :, :], qs[:, 0, :, :], ALU.mult)
                    nop().then_inc(S["rope_done"], 1)
                    for n in range(2):
                        gate_mul(l, n8, t0, n)
                    chunks(l, h, n8, t0, True)
                    merge(l, h, n8)
                for k in range(KT):
                    dve.wait_ge(S["uH_ready"], CR + 2 * KT * l + KT + k + 1)
                    tt(uL[:, k, :], xm[:, k, :], uH[:, k, :].bitcast(F32), ALU.subtract).then_inc(S["plane_ready"], 1)
                dve.wait_ge(S["osq_used"], CR + KT * (l + 1))
                ts(rs.rearrange("p (g t) -> p g t", g=NG), psum[:, ST:ST + NG, 0:GW], 1.0 / D, EPS, ALU.mult, ALU.add).then_inc(S["ors_var"], 1)
                dve.wait_ge(S["ors_sqrt"], CR + l + 1)
                rec(rs, rs)
                for k in range(KT):
                    x = xm[:, k, :]
                    dve.wait_ge(S[f"xt_in{k % 2}"], 64 * l + 16 * (k // 2) + 16)
                    tt(x, x, rs, ALU.mult)
                    stt_(x[:, 0:SEQ], x[:, 0:SEQ], gpo[:, k, 0:1], xt[k % 2][:, 0:SEQ], ALU.mult, ALU.add)
                    tt(x[:, SEQ:T], x[:, SEQ:T], gpo[:, k, 1:9], ALU.mult)
                    tt(x[:, SEQ:T], x[:, SEQ:T], xt[k % 2][:, SEQ:T], ALU.add).then_inc(S["xnew"], 1)
                nop().then_inc(S["ldone"], 1)


_OUTS = {
    "y": (KT, P, T), "rg_h": (DEPTH, P, KT, 9), "p_conv": (DEPTH, P, 2, KT, 3), "p_st": (DEPTH * 8, P, 2, DH),
    "p_n": (DEPTH, HEADS, P, 2), "p_m": (DEPTH, 4, 1),
    "s_rconv": (DEPTH, P, KT, 3, NB), "s_st": (DEPTH * 8, P, NB, 2, DH), "s_n": (DEPTH, HEADS, P, 2, NB),
    "s_m": (DEPTH, 4, NB), "s_mconv": (DEPTH, P, KT, 3, NB),
}
_SCRATCH = {"xkeep": (P, KT, T), "xml_d": (KT, P, T), "xc_d": (KT, P, T)}


def tables():
    f = np.float32
    t = {"ident": np.eye(P, dtype=f), "ones": np.ones((P, P), f), "mask": np.triu(np.ones((P, P), f))}
    lg = np.log1p(-np.exp2(-5.0 - np.arange(HEADS, dtype=f))).astype(f)
    i = np.arange(CH, dtype=f)
    rel = i[None, :] - i[:, None]
    t["dret"] = np.ascontiguousarray(np.where(rel[:, None, :] >= 0, np.exp(np.maximum(rel, 0)[:, None, :] * lg[None, :, None]), 0).astype(f))
    rc = np.zeros((P, 16), f)
    rc[:, 0:4] = np.exp((i + 1)[:, None] * lg)
    rc[:, 4:8] = np.exp((CH - 1 - i)[:, None] * lg)
    rc[:, 8:12] = np.exp(CH * lg)
    rc[:, 12:16] = np.exp(lg)
    t["rcol"] = rc
    half = DH // 2
    step = np.arange(half, dtype=f) / f(half - 1)
    inv = np.power(f(10000.0), -step, dtype=f)
    pos = np.concatenate([np.arange(SEQ, dtype=f), np.full(NB, PAST, f)])
    ang = (inv[:, None] * pos[None, :]).astype(f)
    t["rope"] = np.ascontiguousarray(np.stack([np.cos(ang), np.sin(ang)], 1).astype(f))
    return t


def layouts(a):
    c = np.ascontiguousarray
    chan = lambda x: c(np.moveaxis(x.reshape(x.shape[:-1] + (KT, P)), -1, 1))
    tiles = lambda w: w.reshape(DEPTH, KT, P, -1, P).transpose(0, 3, 2, 1, 4)
    win = tiles(a["w_in"])[:, weight_order()]
    wall = np.concatenate([tiles(a["w_ada"]), win, tiles(a["w_out"])], 1).reshape(DEPTH * NT, P, KT * P)
    b_ada = a["b_ada"].reshape(DEPTH, NADA, P).transpose(0, 2, 1)
    par = np.concatenate([b_ada if n == "b_ada" else chan(a[n]).reshape(DEPTH, P, -1) for n in PAR], 2)
    o = dict(tables())
    o["xp"] = c(a["x_prompt"][0].T.reshape(KT, P, SEQ))
    o["xs"] = c(a["x_sample"][:, 0].T.reshape(KT, P, NB))
    cT = np.zeros((P, KT, 10), np.float32)
    cT[:, :, 0] = a["c_prompt"][0].reshape(KT, P).T
    cT[:, :, 1:9] = a["c_sample"].reshape(NB, KT, P).transpose(2, 1, 0)
    o["cT"] = cT
    o["wall"] = c(wall)
    o["par"] = c(par)
    o["wif"] = c(a["ml_w_if"].reshape(DEPTH, 24, P, 8).transpose(0, 2, 1, 3))
    bif = np.zeros((DEPTH, HCOL, 1), np.float32)
    bif[:, 0:4, 0], bif[:, 32:36, 0] = a["ml_b_if"][:, 0:4], a["ml_b_if"][:, 4:8]
    o["bif"] = bif
    conv = lambda x: c(x.reshape(DEPTH, NB, 3, KT, P).transpose(0, 4, 3, 2, 1))
    o["rcs"], o["mcs"] = conv(a["state_rg_conv"]), conv(a["state_ml_conv"])
    o["rh0"] = c(a["state_rg_h"].reshape(DEPTH, NB, KT, P).transpose(0, 3, 2, 1))
    o["mn0"] = c(a["state_ml_n"].reshape(DEPTH, NB, HEADS, 2, P).transpose(0, 4, 2, 3, 1))
    o["mm0"] = c(a["state_ml_m"].transpose(0, 2, 1))
    mat = lambda x: c(x.reshape(DEPTH, NB, HEADS, 2, P, DH).transpose(0, 2, 4, 1, 3, 5))
    o["st_in"] = np.stack([mat(a["state_ret_S"]), mat(a["state_ml_C"])], 1).reshape(DEPTH * 8, P, NB, 2, DH)
    qkv = np.stack([a["ml_w_q"], a["ml_w_k"], a["ml_w_v"]], 2)
    o["wqkvT"] = c(qkv.reshape(DEPTH, HEADS, 3, DH, 2, P).transpose(0, 1, 5, 2, 4, 3).reshape(DEPTH, HEADS, P, 1536))
    nat = qkv.reshape(DEPTH, HEADS, 3, 2, P, DH).transpose(0, 1, 4, 2, 3, 5)
    o["wqk"] = c(nat[:, :, :, 0:2].reshape(DEPTH, HEADS, P, 1024))
    o["wv"] = c(nat[:, :, :, 2].reshape(DEPTH, HEADS, P, 512))
    o["rgw"] = c(np.stack([a["rg_w_a"], a["rg_w_x"]], 3).reshape(DEPTH, KT, P, 2 * P))
    return o


def kernel(**inputs):
    import concourse.bacc as bacc
    from concourse.bass_utils import run_bass_kernel_spmd as run

    arrays = layouts({k: np.asarray(v) for k, v in inputs.items()})
    nc = bacc.Bacc("TRN2", target_bir_lowering=False, num_devices=1)
    io = {n: nc.dram_tensor("in_" + n, x.shape, mybir.dt.from_np(x.dtype), kind="ExternalInput").ap() for n, x in arrays.items()}
    io |= {n: nc.dram_tensor("out_" + n, s, F32, kind="ExternalOutput").ap() for n, s in _OUTS.items()}
    io |= {n: nc.dram_tensor("tmp_" + n, s, F32, kind="Internal").ap() for n, s in _SCRATCH.items()}
    build(nc, io)
    r = run(nc, [{"in_" + n: x for n, x in arrays.items()}], core_ids=[0]).results[0]
    g = {n: r["out_" + n] for n in _OUTS}
    c = np.ascontiguousarray
    y = g["y"].reshape(D, T)
    rgh = g["rg_h"].transpose(0, 3, 2, 1).reshape(DEPTH, 9, D)
    pconv = g["p_conv"].transpose(0, 2, 4, 3, 1).reshape(DEPTH, 2, 1, 3, D)
    sconv = lambda x: c(x.transpose(0, 4, 3, 2, 1).reshape(DEPTH, NB, 3, D))
    pst = g["p_st"].reshape(DEPTH, 2, HEADS, P, 2, DH)
    sst = g["s_st"].reshape(DEPTH, 2, HEADS, P, NB, 2, DH)
    pmat = lambda x: c(x.transpose(0, 1, 3, 2, 4).reshape(DEPTH, 1, HEADS, DH, DH))
    smat = lambda x: c(x.transpose(0, 3, 1, 4, 2, 5).reshape(DEPTH, NB, HEADS, DH, DH))
    return (c(y[:, :SEQ].T)[None], c(y[:, SEQ:].T)[:, None],
            c(rgh[:, 0:1]), c(pconv[:, 0]), pmat(pst[:, 1]), c(g["p_n"].transpose(0, 1, 3, 2).reshape(DEPTH, 1, HEADS, DH)),
            c(g["p_m"].reshape(DEPTH, 1, HEADS)), c(pconv[:, 1]), pmat(pst[:, 0]),
            c(rgh[:, 1:9]), sconv(g["s_rconv"]), smat(sst[:, 1]), c(g["s_n"].transpose(0, 4, 1, 3, 2).reshape(DEPTH, NB, HEADS, DH)),
            c(g["s_m"].transpose(0, 2, 1)), sconv(g["s_mconv"]), smat(sst[:, 0]))
```

```python
from contextlib import ExitStack

import numpy as np

import concourse.bass as bass
from concourse import mybir

F32 = mybir.dt.float32
F32R = mybir.dt.float32r
ACT = mybir.ActivationFunctionType
ALU = mybir.AluOpType

P = 128
DEPTH, D, SEQ, NB = 2, 1024, 1024, 8
T = SEQ + NB
KT = D // P
NG, GW = 3, T // 3
HEADS, DH, CONV = 4, 256, 4
CH, NC = 128, SEQ // 128
EPS = 1e-6
RG_C = 8.0
PAST = 8192
NADA, NIN, NOUT = 3 * KT, 11 * KT, KT
NT = NIN + NOUT
XML0, RG0, RET0, ML0, OUT0 = 0, 8, 32, 72, 88
HCOL = 36
LOG1P_TERMS = [1.0 / n for n in (15, 13, 11, 9, 7, 5, 3)]

PAR = {}
_o = 0
for _n, _w in (("b_ada", 24), ("norm_pre", 8), ("norm_post", 8), ("rg_conv_w", 32), ("rg_conv_b", 8),
               ("rg_b_a", 8), ("rg_b_x", 8), ("rg_lambda", 8), ("ml_conv_w", 32), ("ml_conv_b", 8),
               ("ml_skip", 8), ("ml_gn", 8), ("ret_gn", 8)):
    PAR[_n] = (_o, _w)
    _o += _w
NPAR = _o

CR, CD = 8, 64
DMA_CREDIT = ("xsp0", "xsp1", "cs_st0", "cs_st1", "st_out")
N_PROJ = 3 * (NIN + NOUT)


def weight_order():
    xrg, zrg, xml, zml, q, k, v, g, ga, gb, gc = (range(8 * i, 8 * i + 8) for i in range(11))
    order = list(xml)
    for j in range(8):
        order += [xrg[j], zrg[j], ga[j]]
    for h in range(4):
        a, b = 2 * h, 2 * h + 1
        order += [q[a], q[b], k[a], k[b], v[a], v[b], g[a], gc[a], g[b], gc[b]]
    for h in range(4):
        a, b = 2 * h, 2 * h + 1
        order += [zml[a], gb[a], zml[b], gb[b]]
    return order


def build(nc, io):
    with ExitStack() as ctx:
        def sb(name, shape, dt=F32):
            return ctx.enter_context(nc.sbuf_tensor(name, shape, dt))

        def sem(name):
            return ctx.enter_context(nc.semaphore(name))

        ident = sb("ident", [P, P])
        ones = sb("ones", [P, P])
        mask = sb("mask", [P, P])
        dret = sb("dret", [P, 4, P])
        rcol = sb("rcol", [P, 16])
        uH = sb("uH", [P, KT, T], F32R)
        uL = sb("uL", [P, KT, T], F32R)
        xm = sb("xm", [P, KT, T])
        wraw = [sb(f"wraw{s}", [P, KT * P]) for s in range(2)]
        wH = [sb(f"wH{s}", [P, KT, P], F32R) for s in range(2)]
        wL = [sb(f"wL{s}", [P, KT, P], F32R) for s in range(2)]
        par = sb("par", [P, NPAR])
        wif = sb("wif", [P, 24, 8])
        cT = sb("cT", [P, KT, 10])
        ada = sb("ada", [P, NADA, 10])
        s1 = sb("s1", [P, KT, 10])
        gpo = sb("gpo", [P, KT, 10])
        nsp = sb("nsp", [P, 2, KT])
        rcs = sb("rcs", [P, KT, 3, NB])
        mcs = sb("mcs", [P, KT, 3, NB])
        rcsn = sb("rcsn", [P, KT, 3, NB])
        mcsn = sb("mcsn", [P, KT, 3, NB])
        pcn = sb("pcn", [P, 2, KT, 3])
        rh0 = sb("rh0", [P, KT, NB])
        rhn = sb("rhn", [P, KT, 9])
        mn0 = sb("mn0", [P, HEADS, 2, NB])
        mnn = sb("mnn", [P, 2, NB])
        mm0 = sb("mm0", [4, NB])
        pn = sb("pn", [P, 2])
        mc = sb("mc", [4, 10])
        mcols = sb("mcols", [4, 3, NC])
        exr = sb("exr", [4, 4, NB])
        smx = sb("smx", [4, 4, NB])
        ucol = sb("ucol", [P, NC, 4, 4])
        bc = sb("bc", [P, 4, 4, NB])
        nmrow = sb("nmrow", [4, SEQ])
        selh = sb("selh", [4, P])
        fj = [sb(f"fj{s}", [P, 2, HCOL]) for s in range(2)]
        zf = sb("zf", [P, HCOL])
        bifp = sb("bifp", [HCOL, 1])
        qs = sb("qs", [P, 3, 2, NB])
        sm = sb("sm", [P, 64])
        sm2 = sb("sm2", [P, 8, 16])
        cst = [sb(f"cst{s}", [P, 2, DH]) for s in range(2)]
        dg = sb("dg", [P, DH])
        W_SIZE = 15720
        work = sb("work", [P, W_SIZE])

        def wv(off, n):
            assert off + n <= W_SIZE
            return work[:, off:off + n]

        wada = [wv(0, KT * P), wv(T, KT * P), wraw[0][:, :], wraw[1][:, :]]
        arow = wv(7 * T, 3 * D)
        NWA = len(wada)
        tmp_n = [wv(T * i, T) for i in range(2)]
        sq = [wv(T * (2 + i), T) for i in range(2)]
        rs = wv(T * 4, T)
        xt = [wv(T * (5 + i), T) for i in range(2)]
        wt = [wv(12000 + 1536 * i, 1536).rearrange("p (m j i) -> p m j i", m=3, j=2) for i in range(2)]
        xj = [wv(1036 * i, 1035) for i in range(2)]
        yj = [wv(2072 + T * i, T) for i in range(2)]
        sg = [wv(2072 + T * (2 + i), T) for i in range(2)]
        fold = wv(11000, 576).rearrange("p (m k c) -> p m k c", m=2, k=KT)
        ROW0 = 1036 + 9 * T
        row = [work[0:4, ROW0 + T * i:ROW0 + T * i + T] for i in range(3)] + [xm[0:4, k, :] for k in range(KT - 1, 2, -1)]
        stk = wv(ROW0 + 3 * T, SEQ)
        rgx = wv(0, 1035)
        rg = {n: wv(1036 + T * i, T) for i, n in enumerate(("xc", "r", "i", "a", "t", "z", "sz", "sg", "h"))}
        rgw = [wv(14500 + 256 * i, 256).rearrange("p (m j) -> p m j", m=2) for i in range(2)]
        qt = wv(0, 2 * T).rearrange("p (a t) -> p a t", a=2)
        kt = wv(2 * T, 2 * T).rearrange("p (a t) -> p a t", a=2)
        vt = wv(4 * T, 2 * T).rearrange("p (a t) -> p a t", a=2)
        tg = [wv((6 + i) * T, T) for i in range(3)]
        tg01 = wv(6 * T, 2 * T).rearrange("p (a t) -> p a t", a=2)
        rope = wv(9 * T, 2 * T).rearrange("p (a t) -> p a t", a=2)
        xc2 = wv(9 * T, 2 * T).rearrange("p (a t) -> p a t", a=2)
        dm = wv(11 * T, SEQ)
        B0 = 12 * T
        st = wv(B0, 514).rearrange("p (a e) -> p a e", a=2)
        wvv = wv(B0 + 514, 512).rearrange("p (i e) -> p i e", i=2)
        B1 = B0 + 514 + 512
        ktok = [wv(B1 + 256 * i, 256) for i in range(2)]
        vtok = [wv(B1 + 512 + 257 * i, 257) for i in range(2)]
        vw = [wv(B1 + 1026 + 257 * i, 257) for i in range(2)]
        sd = [wv(B1 + 1540 + 128 * i, 128) for i in range(2)]
        inter = wv(B1 + 1796, 257)
        hn = wv(B1 + 2053, 257)
        wqk = wv(B1, 1024).rearrange("p (m i j) -> p m i j", m=2, i=2)
        rtmp = [wv(B1 + T * i, T) for i in range(2)]

        psum = ctx.enter_context(nc.psum_tensor("psum", [P, 8, 512], F32))
        TK, ST, PN1, PN2, PS = 3, 4, 5, 6, 7
        ADA_BANKS = (0, 1, 2, TK, ST, PS)

        own = {
            "pe": "mm ada_mm ada_tr sq_used ab_mm gp_done tr_mm bc_mm rg_mm kv_mm st_mm num_mm ps_mm ht_mm qk_mm dm_mm vs_mm "
                  "vb_mm hs_mm red_mm osq_used",
            "act": "evac ada_rows ada_out sqr rs_sqrt uH_ready wif_ready ab_out sig_done rows_in row_exp lam_exp "
                   "tr_out exr_exp bc_out rg_sig rg_ev rg_sq2 rg_sqrt kv_out vw_done in_done qk_ev vs_out "
                   "dm_exp cs_dec sq_done red_sqrt osq ors_sqrt",
            "dve": "ada_ready rs_var tmp_ready plane_ready zeroed xj_pad conv_done xc_ready row_abs lam_abs "
                   "stk_ready rg_xc rg_fac rg_y rope_done stt sd_done h_ready var_ready hn_ready ht_done "
                   "fold_zero g_mul xc_used br_done selh dm_arg dm_done dg_done cs_new red_in red_out ors_var xnew ldone",
            "pool": "hi_done split",
            "sp": "xsp0 xsp1 cs_st0 cs_st1 st_out sdone",
        }
        S = {n: sem(n) for names in own.values() for n in names.split()}
        for n in "settled ada_in0 ada_in1 ada_in2 ada_in3 const_in x_in par_in wraw0 wraw1 wt_in0 wt_in1 rgw_in0 rgw_in1 rope_in xc_in ml_in cs_in0 cs_in1 xt_in0 xt_in1 spill out_st y_out".split():
            S[n] = sem(n)

        def open_balance(eng, who):
            for n in own[who].split():
                eng.sem_inc(S[n], CD if n in DMA_CREDIT else CR)

        def settle(eng):
            eng.sem_inc(S["settled"], 1)

        def pcol(name, i, n=1):
            return par[:, bass.ds(PAR[name][0] + i, n)]

        def tok(ap, g):
            return ap[:, g * GW:(g + 1) * GW]

        def gate_bank(n):
            return n if n < 3 else n % 2

        def evs(l, t, g):
            return l * N_PROJ + 3 * t + g + 1

        def mms(l, t, g):
            return (l * NT + t) * 3 + g + 1

        block = ctx.enter_context(nc.Block())

        def load_state(sp, n8, b):
            sp.wait_ge(S[f"cs_st{b % 2}"], CD + 64 * n8 + 16 * (b // 2))
            settle(sp)
            sp.wait_ge(S["hs_mm"], CR + 8 * n8 + b - 1)
            settle(sp)
            sp.dma_start(cst[b % 2][:, :, :], io["st_in"][n8, :, b]).then_inc(S[f"cs_in{b % 2}"], 16)

        @block.sync
        def _(sp):
            open_balance(sp, "sp")
            for dst, name in ((ident, "ident"), (ones, "ones"), (mask, "mask"), (rcol, "rcol"),
                              (cT, "cT")):
                sp.dma_start(dst[:], io[name]).then_inc(S["const_in"], 16)
            sp.dma_start(dret[:, :, :], io["dret"]).then_inc(S["const_in"], 16)
            with sp.Fori(0, DEPTH) as l:
                sp.wait_ge(S["mm"], CR + 3 * NT * l)
                settle(sp)
                with sp.Fori(0, NADA // NWA) as i:
                    for s in range(NWA):
                        sp.wait_ge(S["ada_mm"], CR + NADA * l + NWA * i + s - NWA + 1)
                        settle(sp)
                        sp.dma_start(wada[s], io["wada"][NADA * l + NWA * i + s]).then_inc(S[f"ada_in{s}"], 16)
                sp.wait_ge(S["x_in"], 32 * KT)
                sp.wait_ge(S["ldone"], CR + l)
                for dst, name in ((par, "par"), (wif, "wif"), (rcs, "rcs"), (mcs, "mcs"), (rh0, "rh0"),
                                  (mn0, "mn0"), (mm0, "mm0"), (bifp, "bif")):
                    sp.dma_start(dst[:], io[name][l]).then_inc(S["par_in"], 16)
                sp.dma_start(io["xkeep"], xm[:, :, :]).then_inc(S["spill"], 16)
                for h in range(HEADS):
                    sp.wait_ge(S["ab_mm"], CR + 4 * l + h - 1)
                    sp.dma_start(wt[h % 2].rearrange("p m j i -> p (m j i)"), io["wqkvT"][l, h]).then_inc(S[f"wt_in{h % 2}"], 16)
                with sp.Fori(0, KT // 2) as i:
                    for s in range(2):
                        j = 2 * i + s
                        sp.wait_ge(S["evac"], CR + evs(l, XML0 + j, 2))
                        sp.dma_start(io["xml_d"][j], xj[s][:, 3:3 + T]).then_inc(S[f"xsp{s}"], 16)
                        sp.wait_ge(S["xc_ready"], CR + KT * l + j + 1)
                        sp.dma_start(io["xc_d"][j], yj[s]).then_inc(S[f"xsp{s}"], 16)
                with sp.Fori(0, KT // 2) as i:
                    for s in range(2):
                        j = 2 * i + s
                        sp.wait_ge(S["rg_mm"], CR + 3 * (KT * l + j - 1))
                        sp.dma_start(rgw[s].rearrange("p m j -> p (m j)"), io["rgw"][l, j]).then_inc(S[f"rgw_in{s}"], 16)
                sp.wait_ge(S["rg_y"], CR + KT * l + KT)
                settle(sp)
                sp.dma_start(io["p_m"][l], mc[:, NC:NC + 1]).then_inc(S["out_st"], 16)
                sp.dma_start(io["s_m"][l], smx[:, 1, :]).then_inc(S["out_st"], 16)
                sp.dma_start(io["s_mconv"][l], mcsn[:, :, :, :]).then_inc(S["out_st"], 16)
                sp.dma_start(rope[:, :, :], io["rope"]).then_inc(S["rope_in"], 16)
                sp.dma_start(io["rg_h"][l], rhn[:, :, :]).then_inc(S["out_st"], 16)
                sp.dma_start(io["s_rconv"][l], rcsn[:, :, :, :]).then_inc(S["out_st"], 16)
                sp.dma_start(io["p_conv"][l], pcn[:, :, :, :]).then_inc(S["out_st"], 16)
                for ml in (False, True):
                    with sp.Fori(0, HEADS) as h:
                        n8 = 8 * l + 4 * ml + h
                        for b in range(2):
                            load_state(sp, n8, b)
                        if ml:
                            sp.wait_ge(S["xc_used"], CR + n8)
                            sp.wait_ge(S["xsp0"], CD + 128 * (l + 1))
                            sp.wait_ge(S["xsp1"], CD + 128 * (l + 1))
                            settle(sp)
                            sp.dma_start(wqk.rearrange("p m i j -> p (m i j)"), io["wqk"][l, h]).then_inc(S["xc_in"], 16)
                            for a in range(2):
                                sp.dma_start(xc2[:, a, :], io["xc_d"][2 * h + a]).then_inc(S["xc_in"], 16)
                            sp.dma_start(wvv.rearrange("p i e -> p (i e)"), io["wv"][l, h]).then_inc(S["ml_in"], 16)
                            sp.wait_ge(S["br_done"], CR + n8)
                            settle(sp)
                            for a in range(2):
                                sp.dma_start(vt[:, a, :], io["xml_d"][2 * h + a]).then_inc(S["ml_in"], 16)
                        for b in range(NB):
                            sp.wait_ge(S["cs_new"], CR + 8 * n8 + b + 1)
                            settle(sp)
                            sp.dma_start(io["s_st"][n8, :, b], cst[b % 2][:, :, :]).then_inc(S[f"cs_st{b % 2}"], 16)
                            if b + 2 < NB:
                                load_state(sp, n8, b + 2)
                        sp.wait_ge(S["stt"], CR + 9 * n8 + 9)
                        settle(sp)
                        sp.dma_start(io["p_st"][n8], st[:, :, 0:256]).then_inc(S["st_out"], 16)
                        if ml:
                            sp.dma_start(io["p_n"][l, h], pn[:, :]).then_inc(S["st_out"], 16)
                            sp.dma_start(io["s_n"][l, h], mnn[:, :, :]).then_inc(S["st_out"], 16)
                        else:
                            sp.sem_inc(S["st_out"], 32)
                sp.wait_ge(S["out_st"], 96 * (l + 1))
                sp.wait_ge(S["st_out"], CD + 48 * 8 * (l + 1))
                for s in range(2):
                    sp.wait_ge(S[f"cs_st{s}"], CD + 64 * 8 * (l + 1))
                sp.sem_inc(S["sdone"], 1)
            for k in range(KT):
                sp.wait_ge(S["xnew"], CR + KT * (DEPTH - 1) + k + 1)
                sp.dma_start(io["y"][k], xm[:, k, :]).then_inc(S["y_out"], 16)
            sp.wait_ge(S["y_out"], 16 * KT)

        @block.gpsimd
        def _(pool):
            open_balance(pool, "pool")
            for k in range(KT):
                pool.dma_start(xm[:, k, 0:SEQ], io["xp"][k]).then_inc(S["x_in"], 16)
                pool.dma_start(xm[:, k, SEQ:T], io["xs"][k]).then_inc(S["x_in"], 16)

            def split_pair(l, i, more):
                for s in range(2):
                    t = NT * l + 2 * i + s
                    pool.wait_ge(S[f"wraw{s}"], 16 * (NT // 2 * l + i) + 16)
                    pool.wait_ge(S["mm"], CR + 3 * t - 3)
                    raw = wraw[s][:, :].rearrange("p (k m) -> p k m", k=KT)
                    settle(pool)
                    pool.tensor_scalar(wH[s][:, :, :], raw, 1.0, 1.0, ALU.mult, ALU.mult).then_inc(S["hi_done"], 1)
                    pool.wait_ge(S["hi_done"], CR + t + 1)
                    pool.tensor_tensor(wL[s][:, :, :], raw, wH[s][:, :, :].bitcast(F32), ALU.subtract).then_inc(S["split"], 1)
                    if more:
                        pool.wait_ge(S["split"], CR + t + 1)
                        settle(pool)
                        pool.dma_start(wraw[s][:, :], io["wall"][t + 2]).then_inc(S[f"wraw{s}"], 16)

            with pool.Fori(0, DEPTH) as l:
                pool.wait_ge(S["ada_mm"], CR + NADA * (l + 1))
                settle(pool)
                for s in range(2):
                    pool.dma_start(wraw[s][:, :], io["wall"][NT * l + s]).then_inc(S[f"wraw{s}"], 16)
                with pool.Fori(0, NT // 2 - 1) as i:
                    split_pair(l, i, True)
                split_pair(l, NT // 2 - 1, False)
                pool.wait_ge(S["br_done"], CR + 8 * l + 8)
                pool.wait_ge(S["spill"], 16 * (l + 1))
                settle(pool)
                for k in range(KT):
                    if k >= 2:
                        pool.wait_ge(S["xnew"], CR + KT * l + k - 1)
                        settle(pool)
                    pool.dma_start(xt[k % 2], io["xkeep"][:, k, :]).then_inc(S[f"xt_in{k % 2}"], 16)

        @block.tensor
        def _(pe):
            open_balance(pe, "pe")

            def proj_group(l, t, s, g, hi=uH, lo=uL, bank=None, lag=3):
                if g == 0:
                    pe.wait_ge(S["split"], CR + l * NT + t + 1)
                pe.wait_ge(S["evac"], CR + evs(l, t, g) - lag)
                for k in range(KT):
                    for n, (w, x) in enumerate(((wH, hi), (wL, hi), (wH, lo))):
                        mm = pe.matmul(psum[:, g if bank is None else bank, 0:GW], w[s][:, k, :], x[:, k, g * GW:(g + 1) * GW],
                                       start=(k == 0 and n == 0), stop=(k == KT - 1 and n == 2))
                mm.then_inc(S["mm"], 1)

            def proj(l, t, s, lag=3):
                for g in range(NG):
                    proj_group(l, t, s, g, lag=lag)

            def proj_rising(l, t, first):
                pe.wait_ge(S["split"], CR + l * NT + t + 1)
                pe.wait_ge(S["evac"], CR + evs(l, t, 0) - 1)
                for k in range(KT):
                    pe.wait_ge(S["plane_ready"], CR + first + k + 1)
                    for g in range(NG):
                        for n, (w, x) in enumerate(((wH, uH), (wL, uH), (wH, uL))):
                            mm = pe.matmul(psum[:, g, 0:GW], w[0][:, k, :], x[:, k, g * GW:(g + 1) * GW],
                                           start=(k == 0 and n == 0), stop=(k == KT - 1 and n == 2))
                        if k == KT - 1:
                            mm.then_inc(S["mm"], 1)

            def gate_group(l, t0, n):
                proj_group(l, t0 + n // 3, (n // 3) % 2, n % 3, bank=gate_bank(n), lag=3 if n == 2 else 2)

            pe.wait_ge(S["const_in"], 96)
            pe.wait_ge(S["zeroed"], CR + 1)
            settle(pe)
            with pe.Fori(0, DEPTH) as l:
                pe.wait_ge(S["evac"], CR + N_PROJ * l)
                pe.wait_ge(S["ors_var"], CR + l)
                for t in range(NADA):
                    k, part, buf = t // 3, t % 3, t % NWA
                    pe.wait_ge(S[f"ada_in{buf}"], 16 * (NADA // NWA * l + t // NWA) + 16)
                    for half in range(2):
                        mm = pe.matmul(psum[0:10, ADA_BANKS[2 * part + half], 0:512], cT[:, k, :],
                                       wada[buf][:, 512 * half:512 * half + 512], start=(k == 0), stop=(k == KT - 1))
                    mm.then_inc(S["ada_mm"], 1)
                pe.wait_ge(S["ada_rows"], CR + l + 1)
                settle(pe)
                for t in range(NADA):
                    mm = pe.transpose(psum[:, TK, 10 * t:10 * t + 10], arow[0:10, P * t:P * t + P], ident[0:10, 0:10])
                mm.then_inc(S["ada_tr"], 1)
                for k in range(KT):
                    pe.wait_ge(S["sqr"], CR + KT * l + k + 1)
                    for g in range(NG):
                        mm = pe.matmul(psum[:, g, 0:GW], ones[:, :], tok(sq[k % 2], g), start=(k == 0), stop=(k == KT - 1))
                    mm.then_inc(S["sq_used"], 1)
                pe.wait_ge(S["wif_ready"], CR + l + 1)
                for h in range(HEADS):
                    pe.wait_ge(S[f"wt_in{h % 2}"], 32 * l + 16 * (h // 2) + 16)
                    pe.wait_ge(S["ab_out"], CR + 4 * l + h)
                    if h == 0:
                        pe.wait_ge(S["ada_out"], CR + l + 1)
                    for i in range(2):
                        for n in range(6):
                            m, jj = n // 2, n % 2
                            c = (m // 2) * 16 + i * 8
                            mm = pe.matmul(psum[:, TK, c:c + 8], wt[h % 2][:, m, jj, i * P:(i + 1) * P],
                                           wif[:, 8 * m + 2 * h + jj, :], start=(n in (0, 4)), stop=(n in (3, 5)))
                    mm.then_inc(S["ab_mm"], 1)
                for g in range(NG):
                    pe.matmul(psum[0:HCOL, ST + g, 0:GW], zf[:, :], ones[:, 0:1].to_broadcast([P, GW]), start=True,
                              stop=False, skip_group_check=True)
                def gate_sums(n, s):
                    pe.wait_ge(S["xc_ready"], CR + n + 1)
                    for g in range(NG):
                        pe.matmul(psum[0:HCOL, ST + g, 0:GW], fj[s][:, 0, :], tok(yj[s], g), start=False, stop=False,
                                  skip_group_check=True)
                        mm = pe.matmul(psum[0:HCOL, ST + g, 0:GW], fj[s][:, 1, :], xj[s][:, 3 + g * GW:3 + (g + 1) * GW],
                                       start=False, stop=True, skip_group_check=True)
                    mm.then_inc(S["gp_done"], 1)

                proj_rising(l, XML0, 2 * KT * l)
                settle(pe)
                with pe.Fori(0, KT // 2 - 1) as i:
                    for s in range(2):
                        proj(l, XML0 + 2 * i + s + 1, 1 - s)
                        gate_sums(KT * l + 2 * i + s, s)
                proj(l, XML0 + KT - 1, 1)
                gate_sums(KT * l + KT - 2, 0)
                gate_sums(KT * l + KT - 1, 1)
                settle(pe)
                with pe.Fori(0, KT // 2) as i:
                    for s in range(2):
                        for m in range(3):
                            proj(l, RG0 + 6 * i + 3 * s + m, (3 * s + m) % 2)
                        n = KT * l + 2 * i + s
                        pe.wait_ge(S["rg_xc"], CR + n + 1)
                        pe.wait_ge(S[f"rgw_in{s}"], 64 * l + 16 * i + 16)
                        if s == 0:
                            pe.wait_ge(S["rows_in"], CR + l + 1)
                        for g in range(NG):
                            pe.wait_ge(S["rg_ev"], CR + 6 * n + (2 if g == 2 else 0))
                            for m in range(2):
                                mm = pe.matmul(psum[:, TK + 2 * m + g % 2, 0:GW], rgw[s][:, m, :], tok(rg["xc"], g),
                                               start=True, stop=True)
                            mm.then_inc(S["rg_mm"], 1)
                pe.wait_ge(S["rg_ev"], CR + 6 * KT * (l + 1))
                pe.wait_ge(S["stk_ready"], CR + l + 1)
                for a in range(2):
                    pe.wait_ge(S["tr_out"], CR + 2 * l + a)
                    for c in range(4):
                        mm = pe.transpose(psum[:, TK, c * P:c * P + 100], stk[0:100, (4 * a + c) * P:(4 * a + c + 1) * P],
                                          ident[0:100, 0:100])
                    mm.then_inc(S["tr_mm"], 1)
                pe.wait_ge(S["exr_exp"], CR + l + 1)
                for h in range(HEADS):
                    mm = pe.matmul(psum[:, PN1, 32 * h:32 * h + 32], ident[0:4, h:h + 1].to_broadcast([4, P]),
                                   exr[:, :, :].rearrange("p a b -> p (a b)"), start=True, stop=True)
                mm.then_inc(S["bc_mm"], 1)
                pe.wait_ge(S["bc_out"], CR + l + 1)
                pe.wait_ge(S["tr_out"], CR + 2 * l + 2)

                def stage_a(n8, c, ml):
                    cs = slice(c * CH, (c + 1) * CH)
                    pe.wait_ge(S["kv_out"], CR + 8 * n8 + c)
                    for a in range(2):
                        pe.transpose(psum[:, TK, a * P:(a + 1) * P], kt[:, a, cs], ident[:, :])
                    for a in range(2):
                        if ml:
                            mm = pe.matmul(psum[:, TK, 256:512], vt[:, a, cs], wvv[:, a, :], start=(a == 0), stop=(a == 1))
                        else:
                            mm = pe.transpose(psum[:, TK, 256 + a * P:256 + (a + 1) * P], vt[:, a, cs], ident[:, :])
                    mm.then_inc(S["kv_mm"], 1)
                    pe.wait_ge(S["sd_done"], CR + 8 * n8 + c)
                    pe.wait_ge(S["ht_done"], CR + 8 * n8 + c - 2)
                    for a in range(2):
                        mm = pe.matmul(psum[:, ST, 0:CH], kt[:, a, cs], qt[:, a, cs], start=(a == 0), stop=(a == 1))
                    mm.then_inc(S["st_mm"], 1)

                def stage_b(n8, c, ml):
                    cs, e = slice(c * CH, (c + 1) * CH), 257 if ml else 256
                    pe.wait_ge(S["vw_done"], CR + 8 * n8 + c + 1)
                    pe.wait_ge(S["sd_done"], CR + 8 * n8 + c + 1)
                    pe.wait_ge(S["h_ready"], CR + 8 * n8 + c)
                    pe.wait_ge(S["in_done"], CR + 8 * n8 + c)
                    pe.wait_ge(S["stt"], CR + 9 * n8 + c + 1)
                    pe.matmul(psum[:, PN1, 0:e], sd[c % 2], vtok[c % 2][:, 0:e], start=True, stop=True)
                    if ml:
                        for a in range(2):
                            pe.matmul(psum[:, PN1, 300 + a:301 + a], ktok[c % 2][:, a * P:(a + 1) * P], vw[c % 2][:, 256:257],
                                      start=True, stop=True)
                    for a in range(2):
                        mm = pe.matmul(psum[:, PN2, 0:e], qt[:, a, cs], st[:, a, 0:e], start=(a == 0), stop=(a == 1))
                    mm.then_inc(S["num_mm"], 1)
                    for a in range(2):
                        mm = pe.matmul(psum[:, PS, 256 * a:256 * a + 256], ktok[c % 2][:, a * P:(a + 1) * P],
                                       vw[c % 2][:, 0:256], start=True, stop=True)
                    mm.then_inc(S["ps_mm"], 1)

                def stage_c(n8, c):
                    pe.wait_ge(S["hn_ready"], CR + 8 * n8 + c + 1)
                    pe.wait_ge(S["sd_done"], CR + 8 * n8 + min(c + 3, NC))
                    pe.wait_ge(S["ht_done"], CR + 8 * n8 + c)
                    for a in range(2):
                        mm = pe.transpose(psum[:, ST, (a + 1) * P:(a + 2) * P], hn[:, a * P:(a + 1) * P], ident[:, :])
                    mm.then_inc(S["ht_mm"], 1)

                def sample_rows(n8, b):
                    pe.wait_ge(S["dg_done"], CR + 8 * n8 + b + 1)
                    pe.matmul(psum[:, 2, 0:DH], ones[:, :], dg[:, :], start=True, stop=True).then_inc(S["vb_mm"], 1)

                def sample_query(n8, b):
                    pe.wait_ge(S["cs_new"], CR + 8 * n8 + b + 1)
                    for a in range(2):
                        o = 256 + a * NB + b
                        for d in range(2):
                            mm = pe.matmul(psum[:, 2, o:o + 1], cst[b % 2][:, d, a * P:(a + 1) * P], qs[:, 0, d, b:b + 1],
                                           start=(d == 0), stop=(d == 1))
                    mm.then_inc(S["hs_mm"], 1)

                def sample_sum(n8, r):
                    pe.wait_ge(S["red_in"], CR + 2 * n8 + 1 + r)
                    for d in range(2):
                        mm = pe.matmul(psum[:, TK, 16 * r:16 * r + 8], ones[:, :], sm2[:, 1 + r, 8 * d:8 * d + 8],
                                       start=(d == 0), stop=(d == 1))
                    mm.then_inc(S["red_mm"], 1)

                def chunks(l, h, n8, t0, ml):
                    for slot in range(NC + 2):
                        if slot < NC:
                            stage_a(n8, slot, ml)
                        if slot < NC:
                            gate_group(l, t0, slot + 3)
                        if slot >= 2:
                            stage_c(n8, slot - 2)
                        if 1 <= slot <= NC:
                            stage_b(n8, slot - 1, ml)
                            sample_query(n8, slot - 1)
                        if slot == 0 and ml:
                            pe.wait_ge(S["dg_done"], CR + 8 * n8 + 1)
                            for d in range(2):
                                mm = pe.matmul(psum[:, 2, 300:308], ones[:, :], sm2[:, 6, 8 * d:8 * d + 8],
                                               start=(d == 0), stop=(d == 1))
                        if slot < NC:
                            sample_rows(n8, slot)
                        if slot >= NC:
                            if slot == NC:
                                gate_group(l, t0, slot + 3)
                                pe.wait_ge(S["kv_out"], CR + 8 * n8 + NC)
                            sample_sum(n8, slot - NC)

                settle(pe)
                with pe.Fori(0, HEADS) as h:
                    n8 = 8 * l + h
                    t0 = RET0 + 10 * h
                    for m in range(6):
                        proj(l, t0 + m, m % 2, lag=2 if m == 0 else 3)
                    for n in range(3):
                        gate_group(l, t0 + 6, n)
                    pe.wait_ge(S["rope_done"], CR + n8 + 1)
                    pe.wait_ge(S["evac"], CR + evs(l, t0 + 5, 2))
                    chunks(l, h, n8, t0 + 6, False)
                settle(pe)
                with pe.Fori(0, HEADS) as h:
                    n8 = 8 * l + 4 + h
                    t0 = ML0 + 4 * h
                    for n in range(2):
                        gate_group(l, t0, n)
                    pe.wait_ge(S["selh"], CR + 5 * l + h + 1)
                    pe.wait_ge(S["ht_done"], CR + 8 * n8)
                    for a in range(2):
                        mm = pe.matmul(psum[:, PN2 + a, 0:512], selh[:, :], nmrow[:, 512 * a:512 * a + 512], start=True, stop=True)
                    mm.then_inc(S["dm_mm"], 1)
                    pe.wait_ge(S["xc_in"], 48 * (4 * l + h) + 48)
                    pe.wait_ge(S["red_out"], CR + n8)
                    for n in range(12):
                        m, a, g = n // 6, (n // 3) % 2, n % 3
                        pe.wait_ge(S["qk_ev"], CR + 12 * (4 * l + h) + n - 2)
                        for i in range(2):
                            mm = pe.matmul(psum[:, TK + n % 3, 0:GW], wqk[:, m, i, a * P:(a + 1) * P],
                                           xc2[:, i, g * GW:(g + 1) * GW], start=(i == 0), stop=(i == 1))
                        mm.then_inc(S["qk_mm"], 1)
                    pe.wait_ge(S["ml_in"], 48 * (4 * l + h) + 48)
                    pe.wait_ge(S["dm_arg"], CR + 4 * l + h + 1)
                    for a in range(2):
                        for i in range(2):
                            mm = pe.matmul(psum[:, PS, a * NB:(a + 1) * NB], wvv[:, i, a * P:(a + 1) * P], vt[:, i, SEQ:T],
                                           start=(i == 0), stop=(i == 1))
                    mm.then_inc(S["vs_mm"], 1)
                    gate_group(l, t0, 2)
                    pe.wait_ge(S["qk_ev"], CR + 12 * (4 * l + h) + 12)
                    pe.wait_ge(S["rope_done"], CR + n8 + 1)
                    pe.wait_ge(S["vs_out"], CR + 4 * l + h + 1)
                    chunks(l, h, n8, t0, True)
                for g in range(NG):
                    if g == 0:
                        pe.wait_ge(S["br_done"], CR + 8 * l + 8)
                    pe.matmul(psum[:, ST + g, 0:GW], zf[:, 0:1].to_broadcast([P, P]), ones[:, 0:1].to_broadcast([P, GW]),
                              start=True, stop=False, skip_group_check=True)

                def square_sums(n, s):
                    pe.wait_ge(S["osq"], CR + n + 1)
                    for g in range(NG):
                        mm = pe.matmul(psum[:, ST + g, 0:GW], ones[:, :], tok(sq[s], g), start=False, stop=True,
                                       skip_group_check=True)
                    mm.then_inc(S["osq_used"], 1)

                proj_rising(l, OUT0, 2 * KT * l + KT)
                settle(pe)
                with pe.Fori(0, KT // 2 - 1) as i:
                    for s in range(2):
                        proj(l, OUT0 + 2 * i + s + 1, 1 - s)
                        square_sums(KT * l + 2 * i + s, s)
                proj(l, OUT0 + KT - 1, 1)
                square_sums(KT * l + KT - 2, 0)
                square_sums(KT * l + KT - 1, 1)

        @block.scalar
        def _(act):
            open_balance(act, "act")

            def activate(*args, **kw):
                made = act.activation(*args, **kw)
                act.drain()
                return made

            def evacuate(l, t, dst, func=ACT.Copy, scale=1.0, groups=(0, 1, 2)):
                for g in groups:
                    act.wait_ge(S["mm"], CR + mms(l, t, g))
                    activate(dst[:, g * GW:(g + 1) * GW], psum[:, g, 0:GW], func, scale=scale).then_inc(S["evac"], 1)

            act.wait_ge(S["const_in"], 96)
            with act.Fori(0, DEPTH) as l:
                act.wait_ge(S["ada_mm"], CR + NADA * (l + 1))
                for n, bank in enumerate(ADA_BANKS):
                    o = activate(arow[0:10, 512 * n:512 * n + 512], psum[0:10, bank, 0:512], ACT.Copy)
                o.then_inc(S["ada_rows"], 1)
                act.wait_ge(S["ada_tr"], CR + l + 1)
                settle(act)
                activate(ada[:, :, :], psum[:, TK, 0:10 * NADA].rearrange("p (a c) -> p a c", a=NADA),
                               ACT.Copy).then_inc(S["ada_out"], 1)
                act.wait_ge(S["x_in"], 32 * KT)
                for k in range(KT):
                    act.wait_ge(S["xnew"], CR + KT * l + k + 1 - KT)
                    act.wait_ge(S["sq_used"], CR + KT * l + k - 1)
                    activate(sq[k % 2], xm[:, k, :], ACT.Square).then_inc(S["sqr"], 1)
                act.wait_ge(S["ldone"], CR + l)
                act.wait_ge(S["sdone"], CR + l)
                act.wait_ge(S["par_in"], 128 * (l + 1))
                activate(wif[:, 8:16, :], wif[:, 8:16, :], ACT.Copy, scale=DH ** -0.5).then_inc(S["wif_ready"], 1)
                act.wait_ge(S["lam_abs"], CR + l + 1)
                activate(sm[:, 16:24], sm[:, 16:24], ACT.Exp, scale=-1.0).then_inc(S["lam_exp"], 1)
                act.wait_ge(S["rs_var"], CR + l + 1)
                activate(rs, rs, ACT.Sqrt).then_inc(S["rs_sqrt"], 1)
                act.wait_ge(S["fold_zero"], CR + l + 1)
                for h in range(HEADS):
                    act.wait_ge(S["ab_mm"], CR + 4 * l + h + 1)
                    src = psum[:, TK, 0:32].rearrange("p (a i c) -> p a i c", a=2, i=2)
                    activate(fold[:, :, 2 * h:2 * h + 2, 0:4], src[:, :, :, 0:4], ACT.Copy)
                    activate(fold[:, :, 2 * h:2 * h + 2, 32:36], src[:, :, :, 4:8], ACT.Copy).then_inc(S["ab_out"], 1)
                act.wait_ge(S["ada_ready"], CR + l + 1)
                for k in range(KT):
                    act.wait_ge(S["tmp_ready"], CR + KT * l + k + 1)
                    activate(tmp_n[k % 2][:, 0:SEQ], tmp_n[k % 2][:, 0:SEQ], ACT.Identity, bias=ada[:, k, 0:1],
                                   scale=s1[:, k, 0:1])
                    activate(uH[:, k, :], tmp_n[k % 2], ACT.Copy).then_inc(S["uH_ready"], 1)
                act.wait_ge(S["xj_pad"], CR + l + 1)
                with act.Fori(0, KT // 2) as i:
                    for s in range(2):
                        n = KT * l + 2 * i + s
                        act.wait_ge(S["gp_done"], CR + n - 1)
                        act.wait_ge(S[f"xsp{s}"], CD + 32 * (4 * l + i))
                        evacuate(l, XML0 + 2 * i + s, xj[s][:, 3:3 + T])
                        act.wait_ge(S["conv_done"], CR + n + 1)
                        activate(sg[s], yj[s], ACT.Sigmoid).then_inc(S["sig_done"], 1)
                act.wait_ge(S["gp_done"], CR + KT * (l + 1))
                activate(work[0:HCOL, ROW0:ROW0 + T].rearrange("p (g t) -> p g t", g=NG), psum[0:HCOL, ST:ST + NG, 0:GW],
                               ACT.Identity, bias=bifp[:, 0:1]).then_inc(S["rows_in"], 1)
                act.wait_ge(S["row_abs"], CR + l + 1)
                activate(row[2], row[2], ACT.Exp, scale=-1.0).then_inc(S["row_exp"], 1)
                for s in range(2):
                    act.wait_ge(S[f"xsp{s}"], CD + 128 * (l + 1))
                with act.Fori(0, KT // 2) as i:
                    for s in range(2):
                        j = 2 * i + s
                        n = KT * l + j
                        t = RG0 + 3 * j
                        act.wait_ge(S["rg_xc"], CR + n)
                        evacuate(l, t, rgx[:, 3:3 + T])
                        act.wait_ge(S["rg_y"], CR + n)
                        evacuate(l, t + 1, rg["z"])
                        evacuate(l, t + 2, rg["sg"], ACT.Sigmoid)
                        activate(rg["sz"], rg["z"], ACT.Sigmoid).then_inc(S["rg_sig"], 1)
                        for g in range(NG):
                            act.wait_ge(S["rg_mm"], CR + 3 * n + g + 1)
                            for m, dst in ((0, "r"), (1, "i")):
                                settle(act)
                                activate(tok(rg[dst], g), psum[:, TK + 2 * m + g % 2, 0:GW], ACT.Sigmoid,
                                               bias=pcol("rg_b_a" if m == 0 else "rg_b_x", j)).then_inc(S["rg_ev"], 1)
                        activate(rg["t"], rg["r"], ACT.Tanh, scale=nsp[:, 1, bass.ds(j, 1)])
                        activate(rg["a"], rg["r"], ACT.Exp, scale=nsp[:, 0, bass.ds(j, 1)])
                        activate(rg["r"], rg["a"], ACT.Square).then_inc(S["rg_sq2"], 1)
                        act.wait_ge(S["rg_fac"], CR + n + 1)
                        activate(rg["t"], rg["r"], ACT.Sqrt, scale=1.0).then_inc(S["rg_sqrt"], 1)
                for a in range(2):
                    act.wait_ge(S["tr_mm"], CR + 2 * l + a + 1)
                    src = psum[:, TK, 0:512].rearrange("p (c q x) -> p c q x", c=4, q=4)
                    activate(ucol[:, 4 * a:4 * a + 4, 0, :], src[:, :, 0, 0:4], ACT.Copy)
                    activate(ucol[:, 4 * a:4 * a + 4, 1:4, :], src[:, :, 1:4, 0:4], ACT.Exp).then_inc(S["tr_out"], 1)
                act.wait_ge(S["stk_ready"], CR + l + 1)
                activate(exr[:, :, :], exr[:, :, :], ACT.Exp).then_inc(S["exr_exp"], 1)
                act.wait_ge(S["bc_mm"], CR + l + 1)
                activate(bc[:, :, :, :].rearrange("p h a b -> p (h a b)"), psum[:, PN1, 0:128], ACT.Copy).then_inc(S["bc_out"], 1)

                def gate_out(l, n8, t0, n):
                    q, cs = n // 3, slice((n % 3) * GW, (n % 3 + 1) * GW)
                    if n == 0:
                        act.wait_ge(S["br_done"], CR + n8)
                    if n >= 3:
                        act.wait_ge(S["g_mul"], CR + 12 * n8 + n - 2)
                    act.wait_ge(S["mm"], CR + mms(l, t0 + q, n % 3))
                    if q % 2 == 0:
                        activate(tg[q // 2][:, cs], psum[:, gate_bank(n), 0:GW], ACT.Copy)
                    activate(tg[2][:, cs], psum[:, gate_bank(n), 0:GW], ACT.Sigmoid).then_inc(S["evac"], 1)

                def chunks(l, h, n8, t0, ml):
                    e = 257 if ml else 256
                    for slot in range(NC + 2):
                        if slot < NC:
                            b = slot
                            act.wait_ge(S["kv_mm"], CR + 8 * n8 + slot + 1)
                            act.wait_ge(S["ps_mm"], CR + 8 * n8 + slot - 1)
                            activate(ktok[slot % 2], psum[:, TK, 0:256], ACT.Copy)
                            activate(vtok[slot % 2][:, 0:256], psum[:, TK, 256:512], ACT.Copy).then_inc(S["kv_out"], 1)
                            w = ucol[:, slot, 3, bass.ds(h, 1)] if ml else rcol[:, bass.ds(4 + h, 1)]
                            activate(vw[slot % 2][:, 0:e], vtok[slot % 2][:, 0:e], ACT.Copy, scale=w).then_inc(S["vw_done"], 1)
                        if slot >= 2:
                            act.wait_ge(S["var_ready"], CR + 8 * n8 + slot - 1)
                            activate(sm[:, 13:14], sm[:, 12:13], ACT.Sqrt).then_inc(S["sq_done"], 1)
                        if slot < NC:
                            act.wait_ge(S[f"cs_in{b % 2}"], 64 * n8 + 16 * (b // 2) + 16)
                            settle(act)
                            sc = bc[:, bass.ds(h, 1), 1, b] if ml else rcol[:, bass.ds(12 + h, 1)]
                            activate(cst[b % 2][:, :, :], cst[b % 2][:, :, :], ACT.Copy, scale=sc).then_inc(S["cs_dec"], 1)
                        if slot <= NC:
                            gate_out(l, n8, t0, slot + 3)
                        if 1 <= slot <= NC:
                            c = slot - 1
                            act.wait_ge(S["num_mm"], CR + 8 * n8 + c + 1)
                            act.wait_ge(S["h_ready"], CR + 8 * n8 + c)
                            sc = ucol[:, c, 1, bass.ds(h, 1)] if ml else rcol[:, bass.ds(h, 1)]
                            settle(act)
                            activate(inter[:, 0:e], psum[:, PN2, 0:e], ACT.Copy, scale=sc).then_inc(S["in_done"], 1)
                    act.wait_ge(S["red_out"], CR + n8 + 1)
                    activate(sm2[:, 3, 8:16], sm2[:, 3, 0:8], ACT.Sqrt).then_inc(S["red_sqrt"], 1)

                with act.Fori(0, HEADS) as h:
                    n8 = 8 * l + h
                    t0 = RET0 + 10 * h
                    act.wait_ge(S["ps_mm"], CR + 8 * n8)
                    act.wait_ge(S["rg_y"], CR + KT * (l + 1))
                    for a in range(2):
                        evacuate(l, t0 + a, qt[:, a, :])
                    for a in range(2):
                        evacuate(l, t0 + 2 + a, kt[:, a, :], scale=DH ** -0.5)
                    act.wait_ge(S["br_done"], CR + n8)
                    for a in range(2):
                        evacuate(l, t0 + 4 + a, vt[:, a, :])
                    for n in range(3):
                        gate_out(l, n8, t0 + 6, n)
                    act.wait_ge(S["rope_done"], CR + n8 + 1)
                    chunks(l, h, n8, t0 + 6, False)
                with act.Fori(0, HEADS) as h:
                    n8 = 8 * l + 4 + h
                    t0 = ML0 + 4 * h
                    for n in range(2):
                        gate_out(l, n8, t0, n)
                    for n in range(12):
                        if n == 6:
                            act.wait_ge(S["dm_arg"], CR + 4 * l + h + 1)
                            activate(dm, dm, ACT.Exp).then_inc(S["dm_exp"], 1)
                        act.wait_ge(S["qk_mm"], CR + 12 * (4 * l + h) + n + 1)
                        dst = (qt, kt)[n // 6][:, (n // 3) % 2, :]
                        activate(tok(dst, n % 3), psum[:, TK + n % 3, 0:GW], ACT.Copy,
                                       scale=(1.0, DH ** -0.5)[n // 6]).then_inc(S["qk_ev"], 1)
                    act.wait_ge(S["vs_mm"], CR + 4 * l + h + 1)
                    activate(qs[:, 2, :, :].rearrange("p a b -> p (a b)"), psum[:, PS, 0:16], ACT.Copy).then_inc(S["vs_out"], 1)
                    gate_out(l, n8, t0, 2)
                    for a in range(2):
                        settle(act)
                        activate(xc2[:, a, :], xc2[:, a, :], ACT.Copy, scale=pcol("ml_skip", 2 * h + a))
                    act.wait_ge(S["rope_done"], CR + n8 + 1)
                    chunks(l, h, n8, t0, True)
                act.wait_ge(S["br_done"], CR + 8 * l + 7)
                for k in range(KT):
                    if k == KT - 2:
                        act.wait_ge(S["br_done"], CR + 8 * l + 8)
                    activate(uH[:, k, :], xm[:, k, :], ACT.Copy).then_inc(S["uH_ready"], 1)
                act.wait_ge(S["plane_ready"], CR + 2 * KT * (l + 1))
                with act.Fori(0, KT // 2) as i:
                    for s in range(2):
                        j = 2 * i + s
                        n = KT * l + j
                        for g in range(NG):
                            act.wait_ge(S["mm"], CR + mms(l, OUT0 + j, g))
                            settle(act)
                            activate(xm[:, bass.ds(j, 1), g * GW:(g + 1) * GW], psum[:, g, 0:GW].unsqueeze(1), ACT.Copy).then_inc(S["evac"], 1)
                        act.wait_ge(S["osq_used"], CR + n - 1)
                        settle(act)
                        activate(sq[s].unsqueeze(1), xm[:, bass.ds(j, 1), :], ACT.Square).then_inc(S["osq"], 1)
                act.wait_ge(S["ors_var"], CR + l + 1)
                activate(rs, rs, ACT.Sqrt).then_inc(S["ors_sqrt"], 1)

        @block.vector
        def _(dve):
            open_balance(dve, "dve")

            def fenced(op):
                def run(*args, **kw):
                    made = op(*args, **kw)
                    dve.drain()
                    return made
                return run

            tt, ts, stt_, cp, rec, scan, memset, bn_stats, bn_aggr, nop = map(fenced, (
                nc.vector.tensor_tensor, nc.vector.tensor_scalar, nc.vector.scalar_tensor_tensor, nc.vector.tensor_copy,
                nc.vector.reciprocal, nc.vector.tensor_tensor_scan, nc.vector.memset, nc.vector.bn_stats,
                nc.vector.bn_aggr, nc.vector.engine_nop))

            tt_, ts_, stt1, bn_stats_, bn_aggr_ = (nc.vector.tensor_tensor, nc.vector.tensor_scalar,
                                                   nc.vector.scalar_tensor_tensor, nc.vector.bn_stats, nc.vector.bn_aggr)

            def log1p(z, z2, p):
                ts(p, z2, LOG1P_TERMS[0], None, ALU.mult)
                for c in LOG1P_TERMS[1:]:
                    stt_(p, p, c, z2, ALU.add, ALU.mult)
                stt_(p, p, 1.0, z, ALU.add, ALU.mult)

            def conv(x, y, name, j, state, new, pout):
                w = "rg_conv_w" if name == "rg" else "ml_conv_w"
                b = "rg_conv_b" if name == "rg" else "ml_conv_b"
                ts(y, x[:, 3:3 + T], pcol(w, 3 * KT + j), pcol(b, j), ALU.mult, ALU.add)
                for tap in (2, 1, 0):
                    stt_(y[:, 0:SEQ], x[:, tap:tap + SEQ], pcol(w, tap * KT + j), y[:, 0:SEQ], ALU.mult, ALU.add)
                    stt_(y[:, SEQ:T].unsqueeze(1), state[:, bass.ds(j, 1), tap, :], pcol(w, tap * KT + j),
                         y[:, SEQ:T].unsqueeze(1), ALU.mult, ALU.add)
                cp(new[:, bass.ds(j, 1), 0:2, :], state[:, bass.ds(j, 1), 1:3, :])
                cp(new[:, bass.ds(j, 1), 2, :], x[:, 3 + SEQ:3 + T].unsqueeze(1))
                return cp(pcn[:, pout, bass.ds(j, 1), :], x[:, SEQ:SEQ + 3].unsqueeze(1))

            memset(zf[:, :], 0.0)
            memset(mc[:, 0:1], 0.0).then_inc(S["zeroed"], 1)
            with dve.Fori(0, DEPTH) as l:
                dve.wait_ge(S["sdone"], CR + l)
                dve.wait_ge(S["par_in"], 128 * (l + 1))
                memset(fold, 0.0).then_inc(S["fold_zero"], 1)
                lam = pcol("rg_lambda", 0, KT)
                stt_(sm[:, 16:24], lam, -1.0, lam, ALU.mult, ALU.max).then_inc(S["lam_abs"], 1)
                dve.wait_ge(S["lam_exp"], CR + l + 1)
                ts(sm[:, 24:32], sm[:, 16:24], 2.0, None, ALU.add)
                rec(sm[:, 24:32], sm[:, 24:32])
                tt(sm[:, 24:32], sm[:, 24:32], sm[:, 16:24], ALU.mult)
                tt(sm[:, 32:40], sm[:, 24:32], sm[:, 24:32], ALU.mult)
                log1p(sm[:, 24:32], sm[:, 32:40], sm[:, 40:48])
                ts(sm[:, 48:56], lam, -1.0, 0.0, ALU.mult, ALU.max)
                stt_(sm[:, 48:56], sm[:, 40:48], 2.0, sm[:, 48:56], ALU.mult, ALU.add)
                ts(nsp[:, 0, :], sm[:, 48:56], -RG_C, None, ALU.mult)
                ts(nsp[:, 1, :], sm[:, 48:56], RG_C, None, ALU.mult)
                dve.wait_ge(S["sq_used"], CR + KT * (l + 1))
                ts(rs.rearrange("p (g t) -> p g t", g=NG), psum[:, 0:NG, 0:GW], 1.0 / D, EPS, ALU.mult, ALU.add).then_inc(S["rs_var"], 1)
                dve.wait_ge(S["rs_sqrt"], CR + l + 1)
                rec(rs, rs)
                dve.wait_ge(S["ada_out"], CR + l + 1)
                tt(ada[:, :, :], ada[:, :, :], pcol("b_ada", 0, NADA).unsqueeze(2).to_broadcast([P, NADA, 10]), ALU.add)
                stt_(s1[:, :, :], ada[:, KT:2 * KT, :], 1.0, pcol("norm_pre", 0, KT).unsqueeze(2).to_broadcast([P, KT, 10]),
                     ALU.add, ALU.mult)
                tt(gpo[:, :, :], ada[:, 2 * KT:, :], pcol("norm_post", 0, KT).unsqueeze(2).to_broadcast([P, KT, 10]),
                   ALU.mult).then_inc(S["ada_ready"], 1)

                def low(k):
                    dve.wait_ge(S["uH_ready"], CR + 2 * KT * l + k + 1)
                    tt(uL[:, k, :], tmp_n[k % 2], uH[:, k, :].bitcast(F32), ALU.subtract).then_inc(S["plane_ready"], 1)

                for k in range(KT):
                    t_ = tmp_n[k % 2]
                    tt(t_, xm[:, k, :], rs, ALU.mult)
                    tt(t_[:, SEQ:T], t_[:, SEQ:T], s1[:, k, 1:9], ALU.mult)
                    tt(t_[:, SEQ:T], t_[:, SEQ:T], ada[:, k, 1:9], ALU.add).then_inc(S["tmp_ready"], 1)
                    if k >= 1:
                        low(k - 1)
                low(KT - 1)
                dve.wait_ge(S["ab_out"], CR + 4 * (l + 1))
                for s in range(2):
                    o = memset(xj[s][:, 0:3], 0.0)
                o.then_inc(S["xj_pad"], 1)
                settle(dve)
                with dve.Fori(0, KT // 2) as i:
                    for s in range(2):
                        j = 2 * i + s
                        n = KT * l + j
                        dve.wait_ge(S["gp_done"], CR + n - 1)
                        dve.wait_ge(S[f"xsp{s}"], CD + 32 * (4 * l + i))
                        cp(fj[s][:, :, :].unsqueeze(2), fold[:, :, bass.ds(j, 1), :])
                        dve.wait_ge(S["evac"], CR + evs(l, XML0 + j, 2))
                        conv(xj[s], yj[s], "ml", j, mcs, mcsn, 1).then_inc(S["conv_done"], 1)
                        dve.wait_ge(S["sig_done"], CR + n + 1)
                        tt(yj[s], yj[s], sg[s], ALU.mult).then_inc(S["xc_ready"], 1)
                dve.wait_ge(S["rows_in"], CR + l + 1)
                R = row
                R0 = row[0]
                dve.wait_ge(S["spill"], 16 * (l + 1))
                memset(stk, 0.0)
                cp(R[1], work[32:36, ROW0:ROW0 + T])
                stt_(R[2], R[1], -1.0, R[1], ALU.mult, ALU.max).then_inc(S["row_abs"], 1)
                ts(R[6], R[1], 0.0, None, ALU.min)
                for s in range(2):
                    dve.wait_ge(S[f"xsp{s}"], CD + 128 * (l + 1))
                memset(rgx[:, 0:3], 0.0)
                cs = [slice(c * CH, (c + 1) * CH) for c in range(NC)]

                def rg_tile(l, j):
                    n = KT * l + j
                    dve.wait_ge(S["evac"], CR + evs(l, RG0 + 3 * j, 2))
                    dve.wait_ge(S["rg_mm"], CR + 3 * n)
                    conv(rgx, rg["xc"], "rg", j, rcs, rcsn, 0).then_inc(S["rg_xc"], 1)
                    dve.wait_ge(S["rg_sig"], CR + n + 1)
                    tt(rg["z"], rg["z"], rg["sz"], ALU.mult)
                    tt(rg["z"], rg["z"], rg["sg"], ALU.mult)
                    dve.wait_ge(S["rg_sq2"], CR + n + 1)
                    stt_(rg["r"], rg["r"], 1.0, rg["t"], ALU.add, ALU.mult).then_inc(S["rg_fac"], 1)
                    tt(rg["i"], rg["i"], rg["xc"], ALU.mult)
                    dve.wait_ge(S["rg_sqrt"], CR + n + 1)
                    tt(rg["i"], rg["i"], rg["t"], ALU.mult)
                    scan(rg["h"][:, 0:SEQ], rg["a"][:, 0:SEQ], rg["i"][:, 0:SEQ], 0.0, ALU.mult, ALU.add)
                    tt(rg["h"][:, SEQ:T].unsqueeze(1), rg["a"][:, SEQ:T].unsqueeze(1), rh0[:, bass.ds(j, 1), :], ALU.mult)
                    tt(rg["h"][:, SEQ:T], rg["h"][:, SEQ:T], rg["i"][:, SEQ:T], ALU.add)
                    cp(rhn[:, bass.ds(j, 1), :], rg["h"][:, SEQ - 1:T].unsqueeze(1))
                    tt(xm[:, bass.ds(j, 1), :], rg["h"].unsqueeze(1), rg["z"].unsqueeze(1), ALU.mult).then_inc(S["rg_y"], 1)

                def row_ratios():
                    dve.wait_ge(S["row_exp"], CR + l + 1)
                    ts(R[3], R[2], 2.0, None, ALU.add)
                    rec(R[3], R[3])
                    tt(R[3], R[2], R[3], ALU.mult)
                    tt(R[4], R[3], R[3], ALU.mult)

                def row_sums():
                    log1p(R[3], R[4], R[5])
                    stt_(R[6], R[5], -2.0, R[6], ALU.mult, ALU.add)
                    for c in range(NC):
                        scan(R[7][:, cs[c]], ones[0:4, :], R[6][:, cs[c]], 0.0, ALU.mult, ALU.add)

                def row_maxima():
                    tt(R[2][:, 0:SEQ], R0[:, 0:SEQ], R[7][:, 0:SEQ], ALU.subtract)
                    for c in range(NC):
                        scan(R[1][:, cs[c]], R[2][:, cs[c]], R[2][:, cs[c]], mc[:, c:c + 1], ALU.max, ALU.max)
                        e = (c + 1) * CH - 1
                        tt(mc[:, c + 1:c + 2], R[1][:, e:e + 1], R[7][:, e:e + 1], ALU.add)
                        ts(stk[32:36, cs[c]], R[1][:, cs[c]], -1.0, mc[:, c:c + 1], ALU.mult, ALU.add)
                        ts(stk[96:100, cs[c]], R[2][:, cs[c]], R[1][:, e:e + 1], None, ALU.subtract)
                    ts(nmrow[:, :], R[1][:, 0:SEQ], -1.0, None, ALU.mult)
                    cp(stk[0:4, :], R[2][:, 0:SEQ])
                    stt_(stk[64:68, :], R[7][:, 0:SEQ], -1.0, R[1][:, 0:SEQ], ALU.mult, ALU.subtract)
                    tt(exr[:, 0, :], mc[:, 0:NC], R[1][:, CH - 1:SEQ:CH], ALU.subtract)
                    tt(smx[:, 0, :], R[6][:, SEQ:T], mm0[:, :], ALU.add)
                    tt(smx[:, 1, :], smx[:, 0, :], R0[:, SEQ:T], ALU.max)
                    tt(exr[:, 1, :], smx[:, 0, :], smx[:, 1, :], ALU.subtract)
                    tt(exr[:, 2, :], R0[:, SEQ:T], smx[:, 1, :], ALU.subtract)
                    ts(exr[:, 3, :], smx[:, 1, :], -1.0, None, ALU.mult).then_inc(S["stk_ready"], 1)

                rg_tile(l, 0)
                row_ratios()
                rg_tile(l, 1)
                row_sums()
                rg_tile(l, 2)
                row_maxima()
                rg_tile(l, 3)
                settle(dve)
                with dve.Fori(2, KT // 2) as i:
                    for s in range(2):
                        rg_tile(l, 2 * i + s)

                def chunks(l, h, n8, t0, ml):
                    e = 257 if ml else 256
                    for slot in range(NC + 2):
                        if slot < NC:
                            sample_value(n8, slot)
                        if slot >= 2:
                            dve.wait_ge(S["sq_done"], CR + 8 * n8 + slot - 1)
                            rec(sm[:, 14:15], sm[:, 13:14])
                            ts_(hn[:, 0:256], hn[:, 0:256], sm[:, 6:7], sm[:, 14:15], ALU.subtract, ALU.mult).then_inc(S["hn_ready"], 1)
                        if slot < NC:
                            c = slot
                            dve.wait_ge(S["st_mm"], CR + 8 * n8 + c + 1)
                            if ml:
                                tt_(sd[c % 2], psum[:, ST, 0:CH], dm[:, c * CH:(c + 1) * CH], ALU.mult).then_inc(S["sd_done"], 1)
                            else:
                                tt_(sd[c % 2].unsqueeze(1), psum[:, ST, 0:CH].unsqueeze(1), dret[:, bass.ds(h, 1), :],
                                   ALU.mult).then_inc(S["sd_done"], 1)
                        if slot >= 2:
                            c = slot - 2
                            dve.wait_ge(S["ht_mm"], CR + 8 * n8 + c + 1)
                            for a in range(2):
                                src = psum[:, ST, (a + 1) * P:(a + 2) * P]
                                dst = vt[:, a, c * CH:(c + 1) * CH]
                                if ml:
                                    o = stt1(dst, src, pcol("ml_gn", 2 * h + a), xc2[:, a, c * CH:(c + 1) * CH], ALU.mult, ALU.add)
                                else:
                                    o = ts_(dst, src, pcol("ret_gn", 2 * h + a), None, ALU.mult)
                            o.then_inc(S["ht_done"], 1)
                        if 1 <= slot <= NC:
                            c = slot - 1
                            dve.wait_ge(S["ps_mm"], CR + 8 * n8 + c + 1)
                            dec = bc[:, bass.ds(h, 1), 0, c] if ml else rcol[:, bass.ds(8 + h, 1)]
                            if ml:
                                stt_(st[:, :, 256], st[:, :, 256], dec, psum[:, PN1, 300:302], ALU.mult, ALU.add)
                                if c == NC - 1:
                                    cp(pn[:, :], st[:, :, 256])
                            stt_(st[:, :, 0:256], st[:, :, 0:256], dec, psum[:, PS, 0:512].rearrange("p (a e) -> p a e", a=2),
                                 ALU.mult, ALU.add).then_inc(S["stt"], 1)
                            dve.wait_ge(S["in_done"], CR + 8 * n8 + c + 1)
                            dve.wait_ge(S["ht_mm"], CR + 8 * n8 + c)
                            tt(hn[:, 0:e], inter[:, 0:e], psum[:, PN1, 0:e], ALU.add).then_inc(S["h_ready"], 1)
                            (bn_stats_ if ml else bn_stats)(sm[:, 0:6], hn[:, 0:256])
                            if ml:
                                stt_(sm[:, 10:11], hn[:, 256:257], -1.0, hn[:, 256:257], ALU.mult, ALU.max)
                            (bn_aggr_ if ml else bn_aggr)(sm[:, 6:8], sm[:, 0:6])
                            if ml:
                                ts(sm[:, 10:11], sm[:, 10:11], ucol[:, c, 2, bass.ds(h, 1)], None, ALU.max)
                                ts(sm[:, 11:12], sm[:, 10:11], sm[:, 10:11], EPS, ALU.mult, ALU.mult)
                            ts_(sm[:, 12:13], sm[:, 7:8], sm[:, 11:12] if ml else EPS, None, ALU.add).then_inc(S["var_ready"], 1)
                        if slot <= NC:
                            gate_mul(l, n8, t0, slot + 3)
                        if slot < NC:
                            sample_update(n8, slot)
                        if slot == NC:
                            sample_heads(l, h, n8, ml)
                        if slot == NC + 1:
                            sample_norm(l, h, n8, ml)

                def gate_mul(l, n8, t0, n):
                    cs = slice((n % 3) * GW, (n % 3 + 1) * GW)
                    dve.wait_ge(S["evac"], CR + evs(l, t0 + n // 3, n % 3))
                    x = tg[n // 6][:, cs]
                    tt_(x, x, tg[2][:, cs], ALU.mult).then_inc(S["g_mul"], 1)

                def sample_value(n8, b):
                    dve.wait_ge(S["vb_mm"], CR + 8 * n8 + b)
                    tt_(dg[:, :].rearrange("p (a e) -> p a e", a=2), ident[:, :].unsqueeze(1).to_broadcast([P, 2, P]),
                       qs[:, 2, :, b:b + 1].to_broadcast([P, 2, P]), ALU.mult).then_inc(S["dg_done"], 1)

                def sample_update(n8, b):
                    dve.wait_ge(S["vb_mm"], CR + 8 * n8 + b + 1)
                    dve.wait_ge(S["cs_dec"], CR + 8 * n8 + b + 1)
                    for d in range(2):
                        v = cst[b % 2][:, d, :]
                        o = stt1(v, psum[:, 2, 0:DH], qs[:, 1, d, b:b + 1], v, ALU.mult, ALU.add)
                    o.then_inc(S["cs_new"], 1)

                def sample_heads(l, h, n8, ml):
                    hs = sm2[:, 1, :]
                    hs3 = hs.rearrange("p (a b) -> p a b", a=2)
                    dve.wait_ge(S["hs_mm"], CR + 8 * n8 + NB)
                    o = cp(hs, psum[:, 2, 256:272])
                    if ml:
                        o = cp(sm2[:, 4, 8:16], psum[:, 2, 300:308])
                    o.then_inc(S["red_in"], 1)
                    if ml:
                        stt_(sm2[:, 4, 0:8], sm2[:, 4, 8:16], -1.0, sm2[:, 4, 8:16], ALU.mult, ALU.max)
                        tt(sm2[:, 4, 0:8].unsqueeze(1), sm2[:, 4, 0:8].unsqueeze(1), bc[:, bass.ds(h, 1), 3, :], ALU.max)
                        tt(sm2[:, 4, 8:16], sm2[:, 4, 0:8], sm2[:, 4, 0:8], ALU.mult)
                    dve.wait_ge(S["red_mm"], CR + 2 * n8 + 1)
                    ts(sm2[:, 5, 0:8], psum[:, TK, 0:8], 1.0 / DH, None, ALU.mult)
                    tt(hs3, hs3, sm2[:, 5, 0:8].unsqueeze(1).to_broadcast([P, 2, NB]), ALU.subtract)
                    tt(sm2[:, 2, :], hs, hs, ALU.mult).then_inc(S["red_in"], 1)

                def sample_norm(l, h, n8, ml):
                    hs = sm2[:, 1, :]
                    hs3 = hs.rearrange("p (a b) -> p a b", a=2)
                    dve.wait_ge(S["red_mm"], CR + 2 * n8 + 2)
                    if ml:
                        ts(sm2[:, 3, 0:8], psum[:, TK, 16:24], 1.0 / DH, None, ALU.mult)
                        stt_(sm2[:, 3, 0:8], sm2[:, 4, 8:16], EPS, sm2[:, 3, 0:8], ALU.mult, ALU.add).then_inc(S["red_out"], 1)
                    else:
                        ts(sm2[:, 3, 0:8], psum[:, TK, 16:24], 1.0 / DH, EPS, ALU.mult, ALU.add).then_inc(S["red_out"], 1)
                    dve.wait_ge(S["red_sqrt"], CR + n8 + 1)
                    rec(sm2[:, 5, 8:16], sm2[:, 3, 8:16])
                    tt(hs3, hs3, sm2[:, 5, 8:16].unsqueeze(1).to_broadcast([P, 2, NB]), ALU.mult)
                    for a in range(2):
                        if ml:
                            o = stt_(vt[:, a, SEQ:T], hs[:, 8 * a:8 * a + 8], pcol("ml_gn", 2 * h + a), xc2[:, a, SEQ:T], ALU.mult, ALU.add)
                        else:
                            o = ts(vt[:, a, SEQ:T], hs[:, 8 * a:8 * a + 8], pcol("ret_gn", 2 * h + a), None, ALU.mult)
                    o.then_inc(S["xc_used"], 1)

                def merge(l, h, n8):
                    tt(vt, vt, tg01, ALU.mult)
                    x2 = xm[:, bass.ds(2 * h, 2), :]
                    tt(x2, x2, vt, ALU.add).then_inc(S["br_done"], 1)

                settle(dve)
                with dve.Fori(0, HEADS) as h:
                    n8 = 8 * l + h
                    t0 = RET0 + 10 * h
                    dve.wait_ge(S["rope_in"], 16 * (l + 1))
                    dve.wait_ge(S["st_out"], CD + 48 * n8)
                    for q, x in ((1, qt), (3, kt)):
                        dve.wait_ge(S["evac"], CR + evs(l, t0 + q, 2))
                        tt(rtmp[0], x[:, 0, :], rope[:, 0, :], ALU.mult)
                        tt(rtmp[1], x[:, 1, :], rope[:, 1, :], ALU.mult)
                        tt(x[:, 0, :], x[:, 0, :], rope[:, 1, :], ALU.mult)
                        tt(x[:, 1, :], x[:, 1, :], rope[:, 0, :], ALU.mult)
                        tt(x[:, 1, :], x[:, 0, :], x[:, 1, :], ALU.add)
                        tt(x[:, 0, :], rtmp[0], rtmp[1], ALU.subtract)
                    cp(qs[:, 0, :, :], qt[:, :, SEQ:T])
                    cp(qs[:, 1, :, :], kt[:, :, SEQ:T])
                    dve.wait_ge(S["evac"], CR + evs(l, t0 + 5, 2))
                    cp(qs[:, 2, :, :], vt[:, :, SEQ:T])
                    memset(st, 0.0).then_inc(S["stt"], 1)
                    nop().then_inc(S["rope_done"], 1)
                    for n in range(3):
                        gate_mul(l, n8, t0 + 6, n)
                    chunks(l, h, n8, t0 + 6, False)
                    merge(l, h, n8)
                cp(selh[:, :], ident[0:4, 0:1].to_broadcast([4, P])).then_inc(S["selh"], 1)
                settle(dve)
                with dve.Fori(0, HEADS) as h:
                    n8 = 8 * l + 4 + h
                    hh = 4 * l + h
                    t0 = ML0 + 4 * h
                    dve.wait_ge(S["dm_mm"], CR + hh + 1)
                    for c in range(NC):
                        o = ts(dm[:, c * CH:(c + 1) * CH], psum[:, PN2 + c // 4, (c % 4) * CH:(c % 4 + 1) * CH],
                               ucol[:, c, 0, bass.ds(h, 1)], 0.0, ALU.add, ALU.min)
                    o.then_inc(S["dm_arg"], 1)
                    dve.wait_ge(S["st_out"], CD + 48 * n8)
                    memset(st, 0.0).then_inc(S["stt"], 1)
                    dve.wait_ge(S["dm_exp"], CR + hh + 1)
                    d3 = dm.rearrange("p (c t) -> p c t", c=NC)
                    tt(d3, d3, mask[:, :].unsqueeze(1).to_broadcast([P, NC, CH]), ALU.mult)
                    dve.wait_ge(S["vs_out"], CR + hh + 1)
                    for s in range(2):
                        memset(vtok[s][:, 256:257], 1.0)
                    cp(qs[:, 0, :, :], qt[:, :, SEQ:T])
                    cp(qs[:, 1, :, :], kt[:, :, SEQ:T])
                    nn3 = sm2[:, 6, :].rearrange("p (a b) -> p a b", a=2)
                    d8 = bc[:, bass.ds(h, 1), 1, :].to_broadcast([P, 2, NB])
                    w8 = bc[:, bass.ds(h, 1), 2, :].to_broadcast([P, 2, NB])
                    tt(mnn[:, :, :], mn0[:, bass.ds(h, 1), :, :].rearrange("p o a b -> p (o a) b"), d8, ALU.mult)
                    tt(nn3, qs[:, 1, :, :], w8, ALU.mult)
                    tt(qs[:, 2, :, :], qs[:, 2, :, :], w8, ALU.mult)
                    tt(mnn[:, :, :], mnn[:, :, :], nn3, ALU.add)
                    tt(nn3, mnn[:, :, :], qs[:, 0, :, :], ALU.mult)
                    nop().then_inc(S["rope_done"], 1)
                    for n in range(3):
                        gate_mul(l, n8, t0, n)
                    chunks(l, h, n8, t0, True)
                    cp(selh[:, :], ident[0:4, bass.ds(h + 1, 1)].to_broadcast([4, P])).then_inc(S["selh"], 1)
                    merge(l, h, n8)
                for k in range(KT):
                    dve.wait_ge(S["uH_ready"], CR + 2 * KT * l + KT + k + 1)
                    tt(uL[:, k, :], xm[:, k, :], uH[:, k, :].bitcast(F32), ALU.subtract).then_inc(S["plane_ready"], 1)
                dve.wait_ge(S["osq_used"], CR + KT * (l + 1))
                ts(rs.rearrange("p (g t) -> p g t", g=NG), psum[:, ST:ST + NG, 0:GW], 1.0 / D, EPS, ALU.mult, ALU.add).then_inc(S["ors_var"], 1)
                dve.wait_ge(S["ors_sqrt"], CR + l + 1)
                rec(rs, rs)
                for k in range(KT):
                    x = xm[:, k, :]
                    dve.wait_ge(S[f"xt_in{k % 2}"], 64 * l + 16 * (k // 2) + 16)
                    tt(x, x, rs, ALU.mult)
                    stt_(x[:, 0:SEQ], x[:, 0:SEQ], gpo[:, k, 0:1], xt[k % 2][:, 0:SEQ], ALU.mult, ALU.add)
                    tt(x[:, SEQ:T], x[:, SEQ:T], gpo[:, k, 1:9], ALU.mult)
                    tt(x[:, SEQ:T], x[:, SEQ:T], xt[k % 2][:, SEQ:T], ALU.add).then_inc(S["xnew"], 1)
                nop().then_inc(S["ldone"], 1)


_OUTS = {
    "y": (KT, P, T), "rg_h": (DEPTH, P, KT, 9), "p_conv": (DEPTH, P, 2, KT, 3), "p_st": (DEPTH * 8, P, 2, DH),
    "p_n": (DEPTH, HEADS, P, 2), "p_m": (DEPTH, 4, 1),
    "s_rconv": (DEPTH, P, KT, 3, NB), "s_st": (DEPTH * 8, P, NB, 2, DH), "s_n": (DEPTH, HEADS, P, 2, NB),
    "s_m": (DEPTH, 4, NB), "s_mconv": (DEPTH, P, KT, 3, NB),
}
_SCRATCH = {"xkeep": (P, KT, T), "xml_d": (KT, P, T), "xc_d": (KT, P, T)}


def tables():
    f = np.float32
    t = {"ident": np.eye(P, dtype=f), "ones": np.ones((P, P), f), "mask": np.triu(np.ones((P, P), f))}
    lg = np.log1p(-np.exp2(-5.0 - np.arange(HEADS, dtype=f))).astype(f)
    i = np.arange(CH, dtype=f)
    rel = i[None, :] - i[:, None]
    t["dret"] = np.ascontiguousarray(np.where(rel[:, None, :] >= 0, np.exp(np.maximum(rel, 0)[:, None, :] * lg[None, :, None]), 0).astype(f))
    rc = np.zeros((P, 16), f)
    rc[:, 0:4] = np.exp((i + 1)[:, None] * lg)
    rc[:, 4:8] = np.exp((CH - 1 - i)[:, None] * lg)
    rc[:, 8:12] = np.exp(CH * lg)
    rc[:, 12:16] = np.exp(lg)
    t["rcol"] = rc
    half = DH // 2
    step = np.arange(half, dtype=f) / f(half - 1)
    inv = np.power(f(10000.0), -step, dtype=f)
    pos = np.concatenate([np.arange(SEQ, dtype=f), np.full(NB, PAST, f)])
    ang = (inv[:, None] * pos[None, :]).astype(f)
    t["rope"] = np.ascontiguousarray(np.stack([np.cos(ang), np.sin(ang)], 1).astype(f))
    return t


def layouts(a):
    c = np.ascontiguousarray
    chan = lambda x: c(np.moveaxis(x.reshape(x.shape[:-1] + (KT, P)), -1, 1))
    tiles = lambda w: w.reshape(DEPTH, KT, P, -1, P).transpose(0, 3, 2, 1, 4)
    win = tiles(a["w_in"])[:, weight_order()]
    wall = np.concatenate([win, tiles(a["w_out"])], 1).reshape(DEPTH * NT, P, KT * P)
    b_ada = a["b_ada"].reshape(DEPTH, NADA, P).transpose(0, 2, 1)
    par = np.concatenate([b_ada if n == "b_ada" else chan(a[n]).reshape(DEPTH, P, -1) for n in PAR], 2)
    o = dict(tables())
    o["xp"] = c(a["x_prompt"][0].T.reshape(KT, P, SEQ))
    o["xs"] = c(a["x_sample"][:, 0].T.reshape(KT, P, NB))
    cT = np.zeros((P, KT, 10), np.float32)
    cT[:, :, 0] = a["c_prompt"][0].reshape(KT, P).T
    cT[:, :, 1:9] = a["c_sample"].reshape(NB, KT, P).transpose(2, 1, 0)
    o["cT"] = cT
    o["wall"] = c(wall)
    o["wada"] = c(a["w_ada"].reshape(DEPTH, KT, P, 3, D).transpose(0, 1, 3, 2, 4).reshape(DEPTH * NADA, P, D))
    o["par"] = c(par)
    o["wif"] = c(a["ml_w_if"].reshape(DEPTH, 24, P, 8).transpose(0, 2, 1, 3))
    bif = np.zeros((DEPTH, HCOL, 1), np.float32)
    bif[:, 0:4, 0], bif[:, 32:36, 0] = a["ml_b_if"][:, 0:4], a["ml_b_if"][:, 4:8]
    o["bif"] = bif
    conv = lambda x: c(x.reshape(DEPTH, NB, 3, KT, P).transpose(0, 4, 3, 2, 1))
    o["rcs"], o["mcs"] = conv(a["state_rg_conv"]), conv(a["state_ml_conv"])
    o["rh0"] = c(a["state_rg_h"].reshape(DEPTH, NB, KT, P).transpose(0, 3, 2, 1))
    o["mn0"] = c(a["state_ml_n"].reshape(DEPTH, NB, HEADS, 2, P).transpose(0, 4, 2, 3, 1))
    o["mm0"] = c(a["state_ml_m"].transpose(0, 2, 1))
    mat = lambda x: c(x.reshape(DEPTH, NB, HEADS, 2, P, DH).transpose(0, 2, 4, 1, 3, 5))
    o["st_in"] = np.stack([mat(a["state_ret_S"]), mat(a["state_ml_C"])], 1).reshape(DEPTH * 8, P, NB, 2, DH)
    qkv = np.stack([a["ml_w_q"], a["ml_w_k"], a["ml_w_v"]], 2)
    o["wqkvT"] = c(qkv.reshape(DEPTH, HEADS, 3, DH, 2, P).transpose(0, 1, 5, 2, 4, 3).reshape(DEPTH, HEADS, P, 1536))
    nat = qkv.reshape(DEPTH, HEADS, 3, 2, P, DH).transpose(0, 1, 4, 2, 3, 5)
    o["wqk"] = c(nat[:, :, :, 0:2].reshape(DEPTH, HEADS, P, 1024))
    o["wv"] = c(nat[:, :, :, 2].reshape(DEPTH, HEADS, P, 512))
    o["rgw"] = c(np.stack([a["rg_w_a"], a["rg_w_x"]], 3).reshape(DEPTH, KT, P, 2 * P))
    return o


def kernel(**inputs):
    import concourse.bacc as bacc
    from concourse.bass_utils import run_bass_kernel_spmd as run

    arrays = layouts({k: np.asarray(v) for k, v in inputs.items()})
    nc = bacc.Bacc("TRN2", target_bir_lowering=False, num_devices=1)
    io = {n: nc.dram_tensor("in_" + n, x.shape, mybir.dt.from_np(x.dtype), kind="ExternalInput").ap() for n, x in arrays.items()}
    io |= {n: nc.dram_tensor("out_" + n, s, F32, kind="ExternalOutput").ap() for n, s in _OUTS.items()}
    io |= {n: nc.dram_tensor("tmp_" + n, s, F32, kind="Internal").ap() for n, s in _SCRATCH.items()}
    build(nc, io)
    r = run(nc, [{"in_" + n: x for n, x in arrays.items()}], core_ids=[0]).results[0]
    g = {n: r["out_" + n] for n in _OUTS}
    c = np.ascontiguousarray
    y = g["y"].reshape(D, T)
    rgh = g["rg_h"].transpose(0, 3, 2, 1).reshape(DEPTH, 9, D)
    pconv = g["p_conv"].transpose(0, 2, 4, 3, 1).reshape(DEPTH, 2, 1, 3, D)
    sconv = lambda x: c(x.transpose(0, 4, 3, 2, 1).reshape(DEPTH, NB, 3, D))
    pst = g["p_st"].reshape(DEPTH, 2, HEADS, P, 2, DH)
    sst = g["s_st"].reshape(DEPTH, 2, HEADS, P, NB, 2, DH)
    pmat = lambda x: c(x.transpose(0, 1, 3, 2, 4).reshape(DEPTH, 1, HEADS, DH, DH))
    smat = lambda x: c(x.transpose(0, 3, 1, 4, 2, 5).reshape(DEPTH, NB, HEADS, DH, DH))
    return (c(y[:, :SEQ].T)[None], c(y[:, SEQ:].T)[:, None],
            c(rgh[:, 0:1]), c(pconv[:, 0]), pmat(pst[:, 1]), c(g["p_n"].transpose(0, 1, 3, 2).reshape(DEPTH, 1, HEADS, DH)),
            c(g["p_m"].reshape(DEPTH, 1, HEADS)), c(pconv[:, 1]), pmat(pst[:, 0]),
            c(rgh[:, 1:9]), sconv(g["s_rconv"]), smat(sst[:, 1]), c(g["s_n"].transpose(0, 4, 1, 3, 2).reshape(DEPTH, NB, HEADS, DH)),
            c(g["s_m"].transpose(0, 2, 1)), sconv(g["s_mconv"]), smat(sst[:, 0]))
```
